# Optimizing a Trainium2 kernel written in Bass

```python
import math
import jax, jax.numpy as jnp
from jax import lax
import numpy as np

D_MODEL = 2048
BATCH = 1
SEQ = 256
DEPTH = 4

CHUNK = 64
Q_BLOCK = 128
N_MIXERS = 3
N_A = (DEPTH + 2) // 3
N_B = (DEPTH + 1) // 3
N_C = DEPTH // 3
PLE_DIM = 256
ROPE_THETA = 10000.0
EPS = 1e-6

DA_HEAD_DIM = 128
DA_V_DIM = 2 * DA_HEAD_DIM
DA_HEADS = D_MODEL // DA_V_DIM
DA_WIDTH = DA_HEADS * DA_V_DIM
MLA_NOPE = 128
MLA_ROPE = 64
MLA_V = 128
MLA_HEADS = D_MODEL // MLA_V
MLA_Q_RANK = 512
MLA_KV_RANK = 512
MLA_WIDTH = MLA_HEADS * MLA_V
LRU_WIDTH = D_MODEL
LRU_BLOCKS = 8
LRU_BLOCK = LRU_WIDTH // LRU_BLOCKS
CONV_WIDTH = 4
LRU_C = 8.0


F32 = jnp.float32

def rms_norm(x, g):
    xf = x.astype(F32)
    y = xf * lax.rsqrt(jnp.mean(xf * xf, axis=-1, keepdims=True) + EPS)
    return (y * g.astype(F32)).astype(x.dtype)

def rope(x, positions):
    d = x.shape[-1]
    half = d // 2
    inv = ROPE_THETA ** (-jnp.arange(half, dtype=F32) / half)
    ang = positions.astype(F32)[..., None] * inv
    ang = ang.reshape(ang.shape[:2] + (1,) * (x.ndim - 3) + (half,))
    cos, sin = jnp.cos(ang), jnp.sin(ang)
    xf = x.astype(F32)
    x1, x2 = xf[..., :half], xf[..., half:]
    return jnp.concatenate([x1 * cos - x2 * sin, x2 * cos + x1 * sin], axis=-1).astype(x.dtype)

def chunk_mask(q_start, q_len, k_len):
    qc = (q_start + jnp.arange(q_len)) // CHUNK
    kc = jnp.arange(k_len) // CHUNK
    return kc[None, :] <= qc[:, None]

def block_sweep(attend, seq):
    return jnp.concatenate([attend(s, s + Q_BLOCK) for s in range(0, seq, Q_BLOCK)], axis=1)

def diff_attention(xn, positions, w_in, q_gain, k_gain, lq1, lk1, lq2, lk2, sub_gain, w_out, layer_idx):
    B, S, _ = xn.shape
    H, d = DA_HEADS, DA_HEAD_DIM
    u = xn @ w_in
    q, k, v, gate = jnp.split(u, 4, axis=-1)
    q = rope(rms_norm(q.reshape(B, S, H, 2, d), q_gain), positions)
    k = rope(rms_norm(k.reshape(B, S, H, 2, d), k_gain), positions)
    v = v.reshape(B, S, H, DA_V_DIM)
    lam_init = 0.8 - 0.6 * math.exp(-0.3 * layer_idx)
    lam = (jnp.exp(jnp.sum(lq1.astype(F32) * lk1.astype(F32)))
           - jnp.exp(jnp.sum(lq2.astype(F32) * lk2.astype(F32))) + lam_init)
    scale = d ** -0.5

    def attend(s, e):
        sc = jnp.einsum('bqhcd,bkhcd->bhcqk', q[:, s:e].astype(F32), k[:, :e].astype(F32)) * scale
        sc = jnp.where(chunk_mask(s, e - s, e), sc, -jnp.inf)
        pr = jax.nn.softmax(sc, axis=-1)
        w = pr[:, :, 0] - lam * pr[:, :, 1]
        return jnp.einsum('bhqk,bkhe->bqhe', w, v[:, :e].astype(F32))

    o = block_sweep(attend, S)
    o = rms_norm(o, sub_gain) * (1.0 - lam_init)
    y = o.reshape(B, S, DA_WIDTH).astype(xn.dtype) * jax.nn.silu(gate)
    return y @ w_out

def mla(xn, positions, w_in, cq_gain, ckv_gain, w_uq, w_ukv, qn_gain, qr_gain, kn_gain, kr_gain, w_out):
    B, S, _ = xn.shape
    H = MLA_HEADS
    u = xn @ w_in
    c_q, c_kv, k_pe, gate = jnp.split(
        u, [MLA_Q_RANK, MLA_Q_RANK + MLA_KV_RANK, MLA_Q_RANK + MLA_KV_RANK + MLA_ROPE], axis=-1)
    q = (rms_norm(c_q, cq_gain) @ w_uq).reshape(B, S, H, MLA_NOPE + MLA_ROPE)
    kv = (rms_norm(c_kv, ckv_gain) @ w_ukv).reshape(B, S, H, MLA_NOPE + MLA_V)
    q_nope = rms_norm(q[..., :MLA_NOPE], qn_gain)
    q_pe = rope(rms_norm(q[..., MLA_NOPE:], qr_gain), positions)
    k_nope = rms_norm(kv[..., :MLA_NOPE], kn_gain)
    v = kv[..., MLA_NOPE:]
    k_pe = rope(rms_norm(k_pe, kr_gain), positions)
    scale = (MLA_NOPE + MLA_ROPE) ** -0.5

    def attend(s, e):
        sc = (jnp.einsum('bqhd,bkhd->bhqk', q_nope[:, s:e].astype(F32), k_nope[:, :e].astype(F32))
              + jnp.einsum('bqhr,bkr->bhqk', q_pe[:, s:e].astype(F32), k_pe[:, :e].astype(F32))) * scale
        sc = jnp.where(chunk_mask(s, e - s, e), sc, -jnp.inf)
        pr = jax.nn.softmax(sc, axis=-1)
        return jnp.einsum('bhqk,bkhe->bqhe', pr, v[:, :e].astype(F32))

    o = block_sweep(attend, S)
    y = o.reshape(B, S, MLA_WIDTH).astype(xn.dtype) * jax.nn.silu(gate)
    return y @ w_out

def rglru_block(xn, w_in, conv_w, conv_b, w_a, b_a, w_x, b_x, lam, w_out):
    B, S, _ = xn.shape
    u = xn @ w_in
    xb, gate = jnp.split(u, 2, axis=-1)
    xc = lax.conv_general_dilated(
        xb.astype(F32), conv_w.astype(F32)[:, None, :], window_strides=(1,),
        padding=[(CONV_WIDTH - 1, 0)], dimension_numbers=('NWC', 'WIO', 'NWC'),
        feature_group_count=LRU_WIDTH) + conv_b.astype(F32)
    xg = xc.reshape(B, S, LRU_BLOCKS, LRU_BLOCK)
    r = jax.nn.sigmoid(jnp.einsum('bsgi,gij->bsgj', xg, w_a.astype(F32)).reshape(B, S, LRU_WIDTH)
                       + b_a.astype(F32))
    i_gate = jax.nn.sigmoid(jnp.einsum('bsgi,gij->bsgj', xg, w_x.astype(F32)).reshape(B, S, LRU_WIDTH)
                            + b_x.astype(F32))
    log_a = -LRU_C * r * jax.nn.softplus(-lam.astype(F32))
    a = jnp.exp(log_a)
    bt = jnp.sqrt(-jnp.expm1(2.0 * log_a)) * (i_gate * xc)

    def combine(left, right):
        a1, b1 = left
        a2, b2 = right
        return a1 * a2, a2 * b1 + b2

    _, h = lax.associative_scan(combine, (a, bt), axis=1)
    y = h.astype(xn.dtype) * jax.nn.silu(gate)
    return y @ w_out

def first_inputs(seed: int = 0) -> dict:
    key = jax.random.key(seed)
    ks = iter(jax.random.split(key, 48))

    def nrm(shape, scale):
        return jax.random.normal(next(ks), shape, F32) * scale

    def gain(shape):
        return 1.0 + 0.05 * jax.random.normal(next(ks), shape, F32)

    D = D_MODEL
    x = nrm((BATCH, SEQ, D), 1.0)
    p = nrm((DEPTH, BATCH, SEQ, PLE_DIM), 1.0)
    offset = jax.random.randint(next(ks), (BATCH, 1), 0, 4096, dtype=jnp.int32)
    positions = (offset + jnp.arange(SEQ, dtype=jnp.int32)[None, :]).astype(jnp.int32)
    norm_gain = gain((DEPTH, D))
    a_w_in = nrm((N_A, D, 4 * DA_WIDTH), D ** -0.5)
    a_q_norm = gain((N_A, DA_HEAD_DIM))
    a_k_norm = gain((N_A, DA_HEAD_DIM))
    a_lambda_q1 = nrm((N_A, DA_HEAD_DIM), 0.1)
    a_lambda_k1 = nrm((N_A, DA_HEAD_DIM), 0.1)
    a_lambda_q2 = nrm((N_A, DA_HEAD_DIM), 0.1)
    a_lambda_k2 = nrm((N_A, DA_HEAD_DIM), 0.1)
    a_sub_norm = gain((N_A, DA_V_DIM))
    a_w_out = nrm((N_A, DA_WIDTH, D), DA_WIDTH ** -0.5)
    b_w_in = nrm((N_B, D, MLA_Q_RANK + MLA_KV_RANK + MLA_ROPE + MLA_WIDTH), D ** -0.5)
    b_cq_norm = gain((N_B, MLA_Q_RANK))
    b_ckv_norm = gain((N_B, MLA_KV_RANK))
    b_w_uq = nrm((N_B, MLA_Q_RANK, MLA_HEADS * (MLA_NOPE + MLA_ROPE)), MLA_Q_RANK ** -0.5)
    b_w_ukv = nrm((N_B, MLA_KV_RANK, MLA_HEADS * (MLA_NOPE + MLA_V)), MLA_KV_RANK ** -0.5)
    b_q_nope_norm = gain((N_B, MLA_NOPE))
    b_q_rope_norm = gain((N_B, MLA_ROPE))
    b_k_nope_norm = gain((N_B, MLA_NOPE))
    b_k_rope_norm = gain((N_B, MLA_ROPE))
    b_w_out = nrm((N_B, MLA_WIDTH, D), MLA_WIDTH ** -0.5)
    c_w_in = nrm((N_C, D, 2 * LRU_WIDTH), D ** -0.5)
    c_conv_w = nrm((N_C, CONV_WIDTH, LRU_WIDTH), CONV_WIDTH ** -0.5)
    c_conv_b = nrm((N_C, LRU_WIDTH), 0.02)
    c_w_a = nrm((N_C, LRU_BLOCKS, LRU_BLOCK, LRU_BLOCK), LRU_BLOCK ** -0.5)
    c_b_a = nrm((N_C, LRU_WIDTH), 0.02)
    c_w_x = nrm((N_C, LRU_BLOCKS, LRU_BLOCK, LRU_BLOCK), LRU_BLOCK ** -0.5)
    c_b_x = nrm((N_C, LRU_WIDTH), 0.02)
    a_target = jax.random.uniform(next(ks), (N_C, LRU_WIDTH), F32, minval=0.9, maxval=0.999)
    s = a_target ** (1.0 / LRU_C)
    c_lambda = jnp.log(s) - jnp.log1p(-s)
    c_w_out = nrm((N_C, LRU_WIDTH, D), LRU_WIDTH ** -0.5)
    ple_norm = gain((DEPTH, D))
    ple_w_gate = nrm((DEPTH, D, D), D ** -0.5)
    ple_w_proj = nrm((DEPTH, PLE_DIM, D), PLE_DIM ** -0.5)
    return {
        "x": x, "p": p, "positions": positions, "norm_gain": norm_gain,
        "a_w_in": a_w_in, "a_q_norm": a_q_norm, "a_k_norm": a_k_norm,
        "a_lambda_q1": a_lambda_q1, "a_lambda_k1": a_lambda_k1,
        "a_lambda_q2": a_lambda_q2, "a_lambda_k2": a_lambda_k2,
        "a_sub_norm": a_sub_norm, "a_w_out": a_w_out,
        "b_w_in": b_w_in, "b_cq_norm": b_cq_norm, "b_ckv_norm": b_ckv_norm,
        "b_w_uq": b_w_uq, "b_w_ukv": b_w_ukv, "b_q_nope_norm": b_q_nope_norm,
        "b_q_rope_norm": b_q_rope_norm, "b_k_nope_norm": b_k_nope_norm,
        "b_k_rope_norm": b_k_rope_norm, "b_w_out": b_w_out,
        "c_w_in": c_w_in, "c_conv_w": c_conv_w, "c_conv_b": c_conv_b,
        "c_w_a": c_w_a, "c_b_a": c_b_a, "c_w_x": c_w_x, "c_b_x": c_b_x,
        "c_lambda": c_lambda, "c_w_out": c_w_out,
        "ple_norm": ple_norm, "ple_w_gate": ple_w_gate, "ple_w_proj": ple_w_proj,
    }

def first_block(x, p, positions, norm_gain,
              a_w_in, a_q_norm, a_k_norm, a_lambda_q1, a_lambda_k1, a_lambda_q2, a_lambda_k2,
              a_sub_norm, a_w_out,
              b_w_in, b_cq_norm, b_ckv_norm, b_w_uq, b_w_ukv, b_q_nope_norm, b_q_rope_norm,
              b_k_nope_norm, b_k_rope_norm, b_w_out,
              c_w_in, c_conv_w, c_conv_b, c_w_a, c_b_a, c_w_x, c_b_x, c_lambda, c_w_out,
              ple_norm, ple_w_gate, ple_w_proj):
    h = x
    for i in range(DEPTH):
        xn = rms_norm(h, norm_gain[i])
        j = i // N_MIXERS
        kind = i % N_MIXERS
        if kind == 0:
            m = diff_attention(xn, positions, a_w_in[j], a_q_norm[j], a_k_norm[j],
                               a_lambda_q1[j], a_lambda_k1[j], a_lambda_q2[j], a_lambda_k2[j],
                               a_sub_norm[j], a_w_out[j], i)
        elif kind == 1:
            m = mla(xn, positions, b_w_in[j], b_cq_norm[j], b_ckv_norm[j], b_w_uq[j], b_w_ukv[j],
                    b_q_nope_norm[j], b_q_rope_norm[j], b_k_nope_norm[j], b_k_rope_norm[j],
                    b_w_out[j])
        else:
            m = rglru_block(xn, c_w_in[j], c_conv_w[j], c_conv_b[j], c_w_a[j], c_b_a[j],
                            c_w_x[j], c_b_x[j], c_lambda[j], c_w_out[j])
        h = h + m.astype(h.dtype)
        g = jax.nn.sigmoid((rms_norm(h, ple_norm[i]) @ ple_w_gate[i]).astype(F32))
        h = h + (g * (p[i] @ ple_w_proj[i]).astype(F32)).astype(h.dtype)
    return h


DEPTH_2 = 2

N_A_LAYERS = DEPTH_2 // 2
N_B_LAYERS = DEPTH_2 - N_A_LAYERS

SSD_EXPAND = 2
SSD_D_INNER = SSD_EXPAND * D_MODEL
SSD_HEAD_DIM = 64
SSD_N_HEADS = SSD_D_INNER // SSD_HEAD_DIM
SSD_N_GROUPS = 8
SSD_HEADS_PER_GROUP = SSD_N_HEADS // SSD_N_GROUPS
SSD_D_STATE = 128
SSD_CONV_W = 4
SSD_CHUNK = 256
SSD_BC_DIM = SSD_N_GROUPS * SSD_D_STATE
SSD_CONV_DIM = SSD_D_INNER + 2 * SSD_BC_DIM
SSD_IN_DIM = SSD_D_INNER + SSD_CONV_DIM + SSD_N_HEADS

DIL_PATTERNS = ((128, 1), (512, 4), (2048, 16))
DIL_N_GROUPS = len(DIL_PATTERNS)
DIL_HEADS = 8
DIL_HEAD_DIM = 128
DIL_Q_WIDTH = DIL_N_GROUPS * DIL_HEADS * DIL_HEAD_DIM
DIL_OUT_WIDTH = DIL_HEADS * DIL_HEAD_DIM
DIL_IN_DIM = DIL_Q_WIDTH + DIL_OUT_WIDTH
DIL_KV_DIM = 2 * DIL_Q_WIDTH
DIL_BLOCK = 128

DEEPNORM_ALPHA = (2 * DEPTH_2) ** 0.25
DEEPNORM_BETA = (8 * DEPTH_2) ** -0.25
LN_EPS = 1e-5
RMS_EPS = 1e-5


def _layer_norm(x, g, b):
    xf = x.astype(jnp.float32)
    mu = jnp.mean(xf, -1, keepdims=True)
    var = jnp.mean(jnp.square(xf - mu), -1, keepdims=True)
    return ((xf - mu) * lax.rsqrt(var + LN_EPS)).astype(x.dtype) * g + b

def _adaln(c, w, b):
    mod = jax.nn.silu(c) @ w + b
    shift, scale, gate = jnp.split(mod, 3, axis=-1)
    return shift[:, None, :], scale[:, None, :], gate[:, None, :]

def _causal_depthwise_conv(x, w, b):
    y = lax.conv_general_dilated(
        x, w[:, None, :], window_strides=(1,), padding=[(SSD_CONV_W - 1, 0)],
        dimension_numbers=("NWC", "WIO", "NWC"), feature_group_count=x.shape[-1])
    return y + b

def _ssd_chunked(xdt, dtA, Bm, Cm):
    f32 = jnp.float32
    bsz, L = xdt.shape[:2]
    G, K, P, N = SSD_N_GROUPS, SSD_HEADS_PER_GROUP, SSD_HEAD_DIM, SSD_D_STATE
    Lp = -(-L // SSD_CHUNK) * SSD_CHUNK
    nc = Lp // SSD_CHUNK

    def chunks(a):
        a = jnp.pad(a, [(0, 0), (0, Lp - L)] + [(0, 0)] * (a.ndim - 2))
        a = a.reshape((bsz, nc, SSD_CHUNK) + a.shape[2:])
        return jnp.moveaxis(a, 1, 0)

    xs = chunks(xdt.reshape(bsz, L, G, K, P).astype(f32))
    As = chunks(dtA.reshape(bsz, L, G, K).astype(f32))
    Bs = chunks(Bm.astype(f32))
    Cs = chunks(Cm.astype(f32))
    causal = jnp.tril(jnp.ones((SSD_CHUNK, SSD_CHUNK), bool))[None, :, :, None, None]

    def step(state, inp):
        xc, ac, bc, cc = inp
        acum = jnp.cumsum(ac, axis=1)
        seg = acum[:, :, None] - acum[:, None, :]
        decay = jnp.exp(jnp.where(causal, seg, -jnp.inf))
        cb = jnp.einsum("blgn,bsgn->blsg", cc, bc)
        y_diag = jnp.einsum("blsgk,bsgkp->blgkp", cb[..., None] * decay, xc)
        y_off = jnp.einsum("blgn,bgkpn->blgkp", cc, state) * jnp.exp(acum)[..., None]
        tail = jnp.exp(acum[:, -1:] - acum)
        new_state = (state * jnp.exp(acum[:, -1])[..., None, None]
                     + jnp.einsum("bsgn,bsgkp->bgkpn", bc, xc * tail[..., None]))
        return new_state, y_diag + y_off

    state0 = jnp.zeros((bsz, G, K, P, N), f32)
    _, ys = lax.scan(step, state0, (xs, As, Bs, Cs))
    ys = jnp.moveaxis(ys, 0, 1).reshape(bsz, Lp, SSD_N_HEADS * P)
    return ys[:, :L]

def _ssd_mixer(h, in_w, conv_w, conv_b, dt_bias, A_log, D_skip, norm_g, out_w):
    bsz, L, _ = h.shape
    proj = h @ in_w
    z, xBC, dt = jnp.split(proj, [SSD_D_INNER, SSD_D_INNER + SSD_CONV_DIM], axis=-1)
    xBC = jax.nn.silu(_causal_depthwise_conv(xBC, conv_w, conv_b))
    xs, Bm, Cm = jnp.split(xBC, [SSD_D_INNER, SSD_D_INNER + SSD_BC_DIM], axis=-1)
    xs = xs.reshape(bsz, L, SSD_N_HEADS, SSD_HEAD_DIM)
    Bm = Bm.reshape(bsz, L, SSD_N_GROUPS, SSD_D_STATE)
    Cm = Cm.reshape(bsz, L, SSD_N_GROUPS, SSD_D_STATE)
    dt = jax.nn.softplus((dt + dt_bias).astype(jnp.float32))
    A = -jnp.exp(A_log.astype(jnp.float32))
    y = _ssd_chunked(xs * dt[..., None], dt * A, Bm, Cm)
    y = y + (xs * D_skip[:, None]).reshape(bsz, L, SSD_D_INNER)
    y = y * jax.nn.silu(z.astype(jnp.float32))
    yg = y.reshape(bsz, L, SSD_N_GROUPS, -1)
    yg = yg * lax.rsqrt(jnp.mean(jnp.square(yg), -1, keepdims=True) + RMS_EPS)
    y = yg.reshape(bsz, L, SSD_D_INNER).astype(h.dtype) * norm_g
    return y @ out_w

def _alibi_slopes():
    n = DIL_N_GROUPS * DIL_HEADS
    s = 2.0 ** (-8.0 * np.arange(1, n + 1) / n)
    return jnp.asarray(s.reshape(DIL_N_GROUPS, DIL_HEADS), dtype=jnp.float32)

def _dilated_window_attention(q, k, v, window, dilation, slopes):
    f32 = jnp.float32
    bsz, L, H, E = q.shape
    span = window // dilation
    M = -(-L // (dilation * DIL_BLOCK)) * DIL_BLOCK
    nb = M // DIL_BLOCK
    pad = M * dilation - L

    def to_blocks(a):
        a = jnp.pad(a, [(0, 0), (0, pad), (0, 0), (0, 0)])
        a = a.reshape(bsz, M, dilation, H, E).transpose(0, 2, 1, 3, 4)
        return a.reshape(bsz, dilation, nb, DIL_BLOCK, H, E)

    def with_prev(a):
        prev = jnp.pad(a[:, :, :-1], [(0, 0), (0, 0), (1, 0), (0, 0), (0, 0), (0, 0)])
        return jnp.concatenate([prev, a], axis=3)

    qb = to_blocks(q)
    kb = with_prev(to_blocks(k))
    vb = with_prev(to_blocks(v))
    s = jnp.einsum("brnqhe,brnkhe->brnhqk", qb, kb,
                   preferred_element_type=f32) * (E ** -0.5)
    qi = jnp.arange(DIL_BLOCK)[:, None]
    kj = jnp.arange(2 * DIL_BLOCK)[None, :]
    delta = qi + DIL_BLOCK - kj
    valid = (delta >= 0) & (delta <= span)
    first = (jnp.arange(nb) == 0)[:, None, None]
    valid = valid[None] & ~(first & (kj < DIL_BLOCK)[None])
    alibi = -slopes[:, None, None] * (delta * dilation).astype(f32)[None]
    s = jnp.where(valid[None, None, :, None], s + alibi[None, None, None], -jnp.inf)
    m = jnp.max(s, -1, keepdims=True)
    p = jnp.exp(s - m)
    den = jnp.sum(p, -1)
    o = jnp.einsum("brnhqk,brnkhe->brnqhe", p, vb.astype(f32))
    o = o / jnp.moveaxis(den, 3, 4)[..., None]
    lse = jnp.moveaxis(m[..., 0] + jnp.log(den), 3, 4)

    def from_blocks(a):
        a = a.reshape((bsz, dilation, M) + a.shape[4:])
        a = jnp.moveaxis(a, 1, 2).reshape((bsz, M * dilation) + a.shape[3:])
        return a[:, :L]

    return from_blocks(o), from_blocks(lse)

def _shared_kv(x, kv_w):
    bsz, L, _ = x.shape
    k, v = jnp.split(x @ kv_w, 2, axis=-1)
    shp = (bsz, L, DIL_N_GROUPS, DIL_HEADS, DIL_HEAD_DIM)
    return k.reshape(shp), v.reshape(shp)

def _dilated_mixer(h, k_sh, v_sh, in_w, out_w):
    bsz, L, _ = h.shape
    q, z = jnp.split(h @ in_w, [DIL_Q_WIDTH], axis=-1)
    q = q.reshape(bsz, L, DIL_N_GROUPS, DIL_HEADS, DIL_HEAD_DIM)
    slopes = _alibi_slopes()
    outs, lses = [], []
    for g, (window, dilation) in enumerate(DIL_PATTERNS):
        o, lse = _dilated_window_attention(q[:, :, g], k_sh[:, :, g], v_sh[:, :, g],
                                           window, dilation, slopes[g])
        outs.append(o)
        lses.append(lse)
    o = jnp.stack(outs, 2)
    wts = jax.nn.softmax(jnp.stack(lses, 2), axis=2)
    o = jnp.einsum("blghe,blgh->blhe", o, wts).reshape(bsz, L, DIL_OUT_WIDTH)
    o = o.astype(h.dtype) * jax.nn.silu(z)
    return o @ out_w

def second_inputs(seed: int = 0) -> dict:
    key = jax.random.key(seed)
    ks = jax.random.split(key, 20)
    f32 = jnp.float32
    nA, nB, D = N_A_LAYERS, N_B_LAYERS, D_MODEL
    nrm = lambda k, shp, sc: jax.random.normal(k, shp, f32) * sc
    dt0 = jnp.exp(jax.random.uniform(ks[8], (nA, SSD_N_HEADS), f32,
                                     np.log(1e-3), np.log(1e-1)))
    return {
        "x": nrm(ks[0], (BATCH, SEQ, D), 1.0),
        "c": nrm(ks[1], (BATCH, D), 1.0),
        "ada_w": nrm(ks[2], (DEPTH_2, D, 3 * D), 0.1 * D ** -0.5),
        "ada_b": nrm(ks[3], (DEPTH_2, 3 * D), 0.01),
        "ln_g": 1.0 + nrm(ks[4], (DEPTH_2, D), 0.01),
        "ln_b": nrm(ks[5], (DEPTH_2, D), 0.01),
        "a_in_w": nrm(ks[6], (nA, D, SSD_IN_DIM), D ** -0.5),
        "a_conv_w": nrm(ks[7], (nA, SSD_CONV_W, SSD_CONV_DIM), SSD_CONV_W ** -0.5),
        "a_conv_b": nrm(ks[9], (nA, SSD_CONV_DIM), 0.01),
        "a_dt_bias": dt0 + jnp.log(-jnp.expm1(-dt0)),
        "a_A_log": jnp.log(jax.random.uniform(ks[10], (nA, SSD_N_HEADS), f32, 1.0, 16.0)),
        "a_D": 1.0 + nrm(ks[11], (nA, SSD_N_HEADS), 0.01),
        "a_norm_g": 1.0 + nrm(ks[12], (nA, SSD_D_INNER), 0.01),
        "a_out_w": nrm(ks[13], (nA, SSD_D_INNER, D), DEEPNORM_BETA * SSD_D_INNER ** -0.5),
        "kv_w": nrm(ks[14], (D, DIL_KV_DIM), D ** -0.5),
        "b_in_w": nrm(ks[15], (nB, D, DIL_IN_DIM), D ** -0.5),
        "b_out_w": nrm(ks[16], (nB, DIL_OUT_WIDTH, D), DEEPNORM_BETA * DIL_OUT_WIDTH ** -0.5),
    }

def second_block(x, c, ada_w, ada_b, ln_g, ln_b, a_in_w, a_conv_w, a_conv_b, a_dt_bias,
              a_A_log, a_D, a_norm_g, a_out_w, kv_w, b_in_w, b_out_w):
    k_sh, v_sh = None, None
    for layer in range(DEPTH_2):
        shift, scale, gate = _adaln(c, ada_w[layer], ada_b[layer])
        h = x * (1.0 + scale) + shift
        if layer < N_A_LAYERS:
            i = layer
            y = _ssd_mixer(h, a_in_w[i], a_conv_w[i], a_conv_b[i], a_dt_bias[i],
                           a_A_log[i], a_D[i], a_norm_g[i], a_out_w[i])
        else:
            i = layer - N_A_LAYERS
            y = _dilated_mixer(h, k_sh, v_sh, b_in_w[i], b_out_w[i])
        x = _layer_norm(DEEPNORM_ALPHA * x + (1.0 + gate) * y, ln_g[layer], ln_b[layer])
        if layer == N_A_LAYERS - 1:
            k_sh, v_sh = _shared_kv(x, kv_w)
    return x


def setup_inputs(seed=0):
    out = dict(first_inputs(seed))
    for name, value in second_inputs(seed + 1).items():
        if name != "x":
            out[name + "_2"] = value
    return out


def reference(
    x, p, positions, norm_gain, a_w_in, a_q_norm, a_k_norm, a_lambda_q1, a_lambda_k1,
    a_lambda_q2, a_lambda_k2, a_sub_norm, a_w_out, b_w_in, b_cq_norm, b_ckv_norm, b_w_uq,
    b_w_ukv, b_q_nope_norm, b_q_rope_norm, b_k_nope_norm, b_k_rope_norm, b_w_out, c_w_in,
    c_conv_w, c_conv_b, c_w_a, c_b_a, c_w_x, c_b_x, c_lambda, c_w_out, ple_norm, ple_w_gate,
    ple_w_proj, c_2, ada_w_2, ada_b_2, ln_g_2, ln_b_2, a_in_w_2, a_conv_w_2, a_conv_b_2,
    a_dt_bias_2, a_A_log_2, a_D_2, a_norm_g_2, a_out_w_2, kv_w_2, b_in_w_2, b_out_w_2,
):
    x = first_block(
        x, p, positions, norm_gain, a_w_in, a_q_norm, a_k_norm, a_lambda_q1, a_lambda_k1,
        a_lambda_q2, a_lambda_k2, a_sub_norm, a_w_out, b_w_in, b_cq_norm, b_ckv_norm, b_w_uq,
        b_w_ukv, b_q_nope_norm, b_q_rope_norm, b_k_nope_norm, b_k_rope_norm, b_w_out, c_w_in,
        c_conv_w, c_conv_b, c_w_a, c_b_a, c_w_x, c_b_x, c_lambda, c_w_out, ple_norm, ple_w_gate,
        ple_w_proj,
    )
    return second_block(
        x, c_2, ada_w_2, ada_b_2, ln_g_2, ln_b_2, a_in_w_2, a_conv_w_2, a_conv_b_2, a_dt_bias_2,
        a_A_log_2, a_D_2, a_norm_g_2, a_out_w_2, kv_w_2, b_in_w_2, b_out_w_2,
    )


_drawn_inputs = setup_inputs


def setup_inputs(seed=0):
    import zlib

    import numpy as np

    out = dict(_drawn_inputs(seed))
    spreads = {}
    factors = {'a_lambda_k1': 5.25,
     'a_lambda_q2': 3.025,
     'b_cq_norm': 8.0,
     'b_ckv_norm': 8.0,
     'b_q_nope_norm': 8.0,
     'b_q_rope_norm': 8.0,
     'b_k_nope_norm': 8.0,
     'b_k_rope_norm': 8.0,
     'c_b_a': 41.33,
     'c_b_x': 8.0,
     'ple_norm': 3.669,
     'ada_b_2': 8.0,
     'ln_g_2': 3.936,
     'ln_b_2': 4.018,
     'a_conv_b_2': 8.0,
     'a_D_2': 64.0,
     'a_norm_g_2': 26.151}
    for name, (base, spread) in spreads.items():
        noise = np.random.default_rng([zlib.crc32(name.encode()), seed]).standard_normal(out[name].shape)
        drawn = base * np.exp(spread * noise) if base else spread * noise
        out[name] = __import__('jax').numpy.asarray(drawn.astype(out[name].dtype))
    for name, factor in factors.items():
        out[name] = (out[name] * factor).astype(out[name].dtype)
    return out
```

```python
from contextlib import ExitStack, contextmanager
import math

import numpy as np
import concourse.bass as bass
from concourse import mybir

F32 = mybir.dt.float32
F32R = mybir.dt.float32r
I32 = mybir.dt.int32
ALU = mybir.AluOpType
ACT = mybir.ActivationFunctionType
AX = mybir.AxisListType
MUL, ADD, SUB, MAX, MIN = ALU.mult, ALU.add, ALU.subtract, ALU.max, ALU.min

P = 128
SEQ = 256
D = 2048
DT = D // P
DEPTH = 4
SLOT = 16
HALF = SLOT // 2 * P
RAW, SPLIT = 4, 2
A_HEADS = 8
B_PAIRS = 8
C_GROUPS = 8
S_GROUPS = 8
S_PAIRS = 4
DIL_HEADS = 8
NEG = -1.0e30
DEEPNORM_ALPHA = 4 ** 0.25
SIG_MIN = -43.0

VEC_PARTS = [("norm_gain", DEPTH * DT), ("ple_norm", DEPTH * DT),
             ("a_q_norm", 2), ("a_k_norm", 2), ("a_lq1", 2), ("a_lq2", 2), ("a_lk1", 2), ("a_lk2", 2),
             ("a_sub_norm", 4), ("b_cq_norm", 4), ("b_ckv_norm", 4), ("b_qn", 1), ("b_qr", 1),
             ("b_kn", 1), ("b_kr", 1), ("c_conv_w", 4 * DT), ("c_conv_b", DT), ("c_b_a", DT),
             ("c_b_x", DT), ("c_lambda", DT), ("c_vec", DT), ("ada_b", 96), ("ln_g", 2 * DT),
             ("ln_b", 2 * DT), ("s_conv_w", 4 * 48), ("s_conv_b", 48), ("s_dt_bias", 1),
             ("s_A_log", 1), ("s_D", 32), ("s_norm_g", 32)]
VEC = {}
_at = 0
for _name, _n in VEC_PARTS:
    VEC[_name] = _at
    _at += _n
NVEC = _at

CONST_PARTS = [("avg_model", P), ("avg_512", P), ("avg_256", P), ("avg_128", P), ("avg_64", P),
               ("ones", P), ("ident", P), ("swap_128", P), ("swap_64", P), ("mask", 3 * P), ("causal", P),
               ("inv_128", 1), ("inv_64", 1), ("eps_6", 1), ("eps_5", 1), ("slopes", 24)]
CON = {}
_at = 0
for _name, _n in CONST_PARTS:
    CON[_name] = _at
    _at += _n
NCON = _at

A_SLOTS = 8 * A_HEADS
PLE_SLOTS = 1 + DT + 8 + 1 + 8


class Steps:

    def __init__(self, counts, who):
        self.k, self.i, self.per, self.bank = {}, None, {}, 0
        self.counts, self.who = counts, who

    def at(self, name, more=0):
        k = self.k.get(name, 0) + more
        n = self.per.get(name, 0)
        if self.i is None or n == 0:
            return max(k, 0)
        return self.i * n + k

    def next(self, name, n=1):
        self.k[name] = self.k.get(name, 0) + n
        return self.at(name)

    def fours(self, name, more):
        k = (self.k.get(name, 0) + more) // 4
        n = self.per.get(name, 0)
        return k + 1 if self.i is None or n == 0 else self.i * (n // 4) + (k + 1)

    @contextmanager
    def loop(self, eng, name, first, last):
        per = self.counts.get((self.who, name), {})
        start = dict(self.k)
        with eng.Fori(first, last) as i:
            self.i, self.per = i, per
            for n, v in per.items():
                self.k[n] = self.k.get(n, 0) - first * v
            inside = dict(self.k)
            yield i
            seen = {n: v - inside.get(n, 0) for n, v in self.k.items() if v != inside.get(n, 0)}
        self.i, self.per = None, {}
        assert seen == per, (self.who, name, seen)
        self.k = {n: start.get(n, 0) + (last - first) * seen.get(n, 0) for n in set(start) | set(seen)}


def program(nc, t, counts):
    ctx = ExitStack()
    with ctx:
        _program(nc, ctx, t, counts)


def _program(nc, ctx, t, counts):
    def sb(name, shape, dt=F32):
        return ctx.enter_context(nc.sbuf_tensor(name, shape, dt))

    def sem(name):
        return ctx.enter_context(nc.semaphore(name))

    h = sb("h", [P, DT, SEQ])
    raw = [sb(f"w_raw{n}", [P, SLOT * P]) for n in range(RAW)]
    w_hi = [sb(f"w_hi{n}", [P, SLOT * P], F32R) for n in range(SPLIT)]
    w_lo = [sb(f"w_lo{n}", [P, SLOT * P], F32R) for n in range(SPLIT)]
    p_hi, p_lo = sb("p_hi", [P, DT, SEQ], F32R), sb("p_lo", [P, DT, SEQ], F32R)
    q_hi, q_lo = sb("q_hi", [P, DT, SEQ], F32R), sb("q_lo", [P, DT, SEQ], F32R)
    c_hi, c_lo = sb("c_hi", [P, 8, SEQ], F32R), sb("c_lo", [P, 8, SEQ], F32R)
    vec = sb("vec", [P, NVEC])
    con = sb("con", [P, NCON])
    cos_a, sin_a = sb("cos_a", [P, SEQ]), sb("sin_a", [P, SEQ])
    cos_b, sin_b = sb("cos_b", [P, SEQ]), sb("sin_b", [P, SEQ])
    rstd = sb("rstd", [P, SEQ])
    acc = sb("acc", [P, SEQ])
    sq = sb("sq", [P, 2, SEQ])
    rsn = sb("rsn", [P, 3, SEQ])
    tiny = sb("tiny", [P, 64])
    lam = sb("lam", [P, 2])
    sp8 = tiny[:, 32:32 + DT]
    ada_hl = sb("ada_hl", [P, DT, 2], F32R)
    ada_hz = sb("ada_hz", [P, DT, 2], F32R)
    mod = sb("mod", [P, 96])
    scratch = sb("scratch", [P, (nc.sbuf_bytes_remaining - 64) // 4 // 8 * 8])

    def view(at, *shape):
        n = int(np.prod(shape))
        assert at + n <= scratch.shape[1], (at + n, scratch.shape)
        v = scratch[:, at:at + n]
        if len(shape) == 2:
            v = v.rearrange("p (a b) -> p a b", a=shape[0])
        if len(shape) == 3:
            v = v.rearrange("p (a b c) -> p a b c", a=shape[0], b=shape[1])
        return v

    G = [ctx.enter_context(nc.psum_tensor(f"g{n}", [P, 512], F32)) for n in range(2)]
    bN = ctx.enter_context(nc.psum_tensor("norm_bank", [P, 512], F32))
    bR = ctx.enter_context(nc.psum_tensor("rope_bank", [P, 512], F32))
    bT = ctx.enter_context(nc.psum_tensor("turn_bank", [P, 512], F32))
    bS = [ctx.enter_context(nc.psum_tensor(f"score_bank{n}", [P, 512], F32)) for n in range(2)]
    bO = ctx.enter_context(nc.psum_tensor("out_bank", [P, 512], F32))

    small_in = sem("small_in")
    h_in = sem("h_in")
    p_in = sem("p_in")
    landed = [sem(f"landed{n}") for n in range(RAW)]
    hi_ready, lo_ready = sem("hi_ready"), sem("lo_ready")
    half_used = sem("half_used")
    tile_done, tile_taken = sem("tile_done"), sem("tile_taken")
    x_hi, x_lo = sem("x_hi"), sem("x_lo")
    res_ready = sem("res_ready")
    squared, summed = sem("squared"), sem("summed")
    norm_summed, factor_ready = sem("norm_summed"), sem("factor_ready")
    rot_done, rot_read = sem("rot_done"), sem("rot_read")
    scaled, cos_done, roped = sem("scaled"), sem("cos_done"), sem("roped")
    turn_done, turn_read = sem("turn_done"), sem("turn_read")
    scored, score_read, maxed, exped = sem("scored"), sem("score_read"), sem("maxed"), sem("exped")
    weighted, mixed, mixed_read, y_ready = sem("weighted"), sem("mixed"), sem("mixed_read"), sem("y_ready")
    clamped, sig_ready = sem("clamped"), sem("sig_ready")
    trig_in, trig_out = sem("trig_in"), sem("trig_out")
    lam_in, lam_sum, lam_exp, lam_ready = sem("lam_in"), sem("lam_sum"), sem("lam_exp"), sem("lam_ready")
    p_ready, p_hi_ready = sem("p_ready"), sem("p_hi_ready")
    sq_head = sem("sq_head")
    dve_step, act_step = sem("dve_step"), sem("act_step")
    act_passed, pool_passed = sem("act_passed"), sem("pool_passed")
    soft_in, soft_out = sem("soft_in"), sem("soft_out")
    gates_in, gates_out, chain_in, chain_out = sem("gates_in"), sem("gates_out"), sem("chain_in"), sem("chain_out")
    gated, conv_done = sem("gated"), sem("conv_done")
    ada_in, ada_z, ada_out, mod_ready = sem("ada_in"), sem("ada_z"), sem("ada_out"), sem("mod_ready")
    swap_in, dt_ready, conved = sem("swap_in"), sem("dt_ready"), sem("conved")
    masked, rows_done, rows_read, decayed = sem("masked"), sem("rows_done"), sem("rows_read"), sem("decayed")
    m_ready, yd_done, s_y_ready, s_sq = sem("m_ready"), sem("yd_done"), sem("s_y_ready"), sem("s_sq")
    s_sum, cb_done, cb_read, gluon = sem("s_sum"), sem("cb_done"), sem("cb_read"), sem("gluon")
    xdt_done, y_scaled = sem("xdt_done"), sem("y_scaled")
    pool_step, scaled_h = sem("pool_step"), sem("scaled_h")
    ln_done, ln_go, ln_sq, mod_x, mod_y = sem("ln_done"), sem("ln_go"), sem("ln_sq"), sem("mod_x"), sem("mod_y")
    d_in, scratch_free = sem("d_in"), sem("scratch_free")
    out_ready, stored = sem("out_ready"), sem("stored")

    def K(name, n=None, rows=P):
        a = CON[name]
        w = dict(CONST_PARTS)[name] if n is None else n
        return con[0:rows, a:a + w]

    def V(name, j=0):
        a = VEC[name]
        return vec[:, a + j:a + j + 1]

    at = 0
    qs = view(at, 3, SEQ); at += 3 * SEQ
    sqh = view(at, 2, SEQ); at += 2 * SEQ
    qn = view(at, 2, SEQ); at += 2 * SEQ
    qr = view(at, 4, SEQ); at += 4 * SEQ
    t2 = view(at, 2, SEQ); at += 2 * SEQ
    vs = view(at, 2, SEQ); at += 2 * SEQ
    vtok = view(at, 2, 256); at += 512
    gz = view(at, 2, SEQ); at += 2 * SEQ
    zc = view(at, 2, SEQ); at += 2 * SEQ
    sm = view(at, 2, 384); at += 768
    pt = sm[:, 1]
    yo = view(at, 512); at += 512
    proj = view(0, 8, SEQ)
    zg = view(8 * SEQ, 2, SEQ)
    sg = view(10 * SEQ, 2, SEQ)
    p_raw = view(13 * SEQ, 2, SEQ)

    bq = view(0, 3, SEQ)
    bk = view(3 * SEQ, 2, SEQ)
    bv = view(5 * SEQ, 2, SEQ)
    bsk = view(7 * SEQ, 2, SEQ)
    b_pe = view(9 * SEQ, SEQ)
    b_t2 = view(10 * SEQ, SEQ)
    b_kpe = view(11 * SEQ, SEQ)
    bsq = view(12 * SEQ, 3, SEQ)
    b_yo = view(12 * SEQ, 512)
    b_sm = view(15 * SEQ, 2, 384)
    b_vtok = view(15 * SEQ + 768, 2, 2, P)
    b_gz = view(15 * SEQ + 1280, 2, SEQ)
    b_zc = view(15 * SEQ + 1792, 2, SEQ)
    b_rq, b_rkv = view(24 * SEQ, SEQ), view(25 * SEQ, SEQ)
    b_cs = view(0, 2, SEQ)
    b_csq = view(15 * SEQ, 8, SEQ)

    xc = view(0, DT, SEQ)
    xbp = view(DT * SEQ, 2, 264)
    rg = view(DT * SEQ, 4, SEQ)
    ig = view(20 * SEQ, 4, SEQ)
    c_gz, c_zc = view(24 * SEQ, SEQ), view(25 * SEQ, SEQ)
    soft = view(25 * SEQ, 3, DT)

    s_dx = view(0, 4, SEQ)
    s_z = view(4 * SEQ, 4, SEQ)
    s_y = view(8 * SEQ, 4, SEQ)
    s_xdt = view(12 * SEQ, 2, 4, P)
    s_cb = view(16 * SEQ, 384)
    s_tok = view(16 * SEQ + 384, 4, P)
    s_xbp = view(18 * SEQ + 384, 2, 264)
    s_e = view(20 * SEQ + 400, 2, 384)
    s_zc = view(23 * SEQ + 400, SEQ)
    s_ac, s_dt, s_acm = cos_a, sin_a, [cos_b, sin_b]
    s_bc = [sq[:, 0], sq[:, 1]]
    s_xv = [rstd[:], vec[:, 0:SEQ]]
    ln_c = view(0, DT, SEQ)
    d_q, d_k, d_v = view(0, 3, SEQ), view(3 * SEQ, 3, SEQ), view(6 * SEQ, 3, SEQ)
    d_vtok = view(9 * SEQ, 3, 2, P)
    d_s = view(12 * SEQ, 3, 384)
    d_mat = view(12 * SEQ + 1152, 3, 384)
    d_gz, d_zc = cos_a, sin_a

    block = ctx.enter_context(nc.Block())

    @block.sync
    def _(sp):
        c = Steps(counts, "sp")
        sp.dma_start(vec[:], t["vecs"]).then_inc(small_in, 16)
        sp.dma_start(con[:], t["consts"]).then_inc(small_in, 16)
        sp.dma_start(scratch[:, 0:SEQ].bitcast(I32), t["positions"].to_broadcast([P, SEQ])).then_inc(small_in, 16)
        sp.dma_start(h[:], t["x"]).then_inc(h_in, 16)
        n_slots = t["slots"].shape[0]
        for s in range(RAW):
            sp.dma_start(raw[s][:], t["slots"][s]).then_inc(landed[s], 16)
        c.k["slot"] = RAW
        with c.loop(sp, "slots", 1, n_slots // RAW) as i:
            for s in range(RAW):
                sp.wait_ge(lo_ready, c.at("slot", -RAW + 1) * 2)
                sp.dma_start(raw[s][:], t["slots"][i * RAW + s]).then_inc(landed[s], 16)
                c.next("slot")
        sp.wait_ge(out_ready, 1)
        sp.dma_start(t["out"], h[:]).then_inc(stored, 16)
        sp.wait_ge(stored, 16)

    @block.tensor
    def _(pe):
        c = Steps(counts, "pe")

        def slot():
            c.next("slot")
            pe.wait_ge(lo_ready, c.at("slot") * 2 + -1)
            return (c.k["slot"] - 1) % SPLIT

        def second_half():
            pe.wait_ge(lo_ready, c.at("slot") * 2)

        def tile(w, blocks, hi, lo, ks, fresh=False):
            pe.wait_ge(tile_taken, c.at("tile", 0 if fresh else -1))
            g = G[c.bank][:, 0:SEQ]
            c.bank ^= 1
            for n, (b, k) in enumerate(zip(blocks, ks)):
                if b == SLOT // 2:
                    second_half()
                wh, wl = w_hi[w][:, b * P:(b + 1) * P], w_lo[w][:, b * P:(b + 1) * P]
                pe.matmul(g, wh, hi[:, k], start=n == 0, stop=False)
                pe.matmul(g, wh, lo[:, k], start=False, stop=False)
                last = pe.matmul(g, wl, hi[:, k], start=False, stop=n == len(ks) - 1)
                if b == SLOT // 2 - 1 and len(ks) == SLOT:
                    last.then_inc(half_used, 1)
            last.then_inc(tile_done, 1)
            c.next("tile")

        def norm(mats, srcs, need, value):
            pe.wait_ge(factor_ready, c.at("norm"))
            pe.wait_ge(need, value)
            for n, s in enumerate(srcs):
                last = pe.matmul(bN[:, 0:SEQ], mats, s, start=n == 0, stop=n == len(srcs) - 1)
            last.then_inc(norm_summed, 1)
            c.next("norm")

        def model_norm():
            norm(K("avg_model"), [acc[:]], summed, c.next("sum", DT))

        def rotate(buf, swap, n=1):
            pe.wait_ge(rot_read, c.at("rot"))
            pe.wait_ge(scaled, c.next("scaled", n))
            pe.matmul(bR[:, 0:SEQ], swap, buf, start=True, stop=True).then_inc(rot_done, 1)
            c.next("rot")

        def turn(srcs, need, value):
            pe.wait_ge(turn_read, c.at("turn"))
            pe.wait_ge(need, value)
            for n, s in enumerate(srcs):
                last = pe.transpose(bT[:, n * P:(n + 1) * P], s, K("ident"))
            last.then_inc(turn_done, 1)
            c.next("turn")

        def square_tiles(hi, lo):
            w = slot()
            tile(w, range(SLOT), hi, lo, range(SLOT))

        def mod_slot(m, fresh=False):
            w = slot()
            pe.wait_ge(tile_taken, c.at("tile", 0 if fresh else -1))
            g = G[c.bank][0:2, 0:SEQ]
            c.bank ^= 1
            for b in range(8):
                if b == 4:
                    second_half()
                k = 8 * (m % 2) + b
                cols = slice(b * SEQ, (b + 1) * SEQ)
                pe.matmul(g, ada_hl[:, k], w_hi[w][:, cols], start=b == 0, stop=False)
                last = pe.matmul(g, ada_hz[:, k], w_lo[w][:, cols], start=False, stop=b == 7)
                if b == 3:
                    last.then_inc(half_used, 1)
            last.then_inc(tile_done, 1)
            c.next("tile")

        def mod_columns():
            pe.wait_ge(tile_taken, c.at("tile"))
            g = G[c.bank]
            c.bank ^= 1
            for e in range(2):
                last = pe.matmul(g[:, e:e + 1], acc[0:2, e * P:(e + 1) * P], K("ones", 1, rows=2), start=True, stop=True)
            last.then_inc(tile_done, 1)
            c.next("tile")

        def proj_slot(fresh=False):
            w = slot()
            pe.wait_ge(p_ready, c.at("p"))
            for n in range(8):
                tile(w, [2 * n, 2 * n + 1], c_hi, c_lo, [0, 1], fresh=fresh and n == 0)

        def gates_and_next(hi, lo):
            for half in range(2):
                if half:
                    proj_slot()
                with c.loop(pe, "gates", 0, 2):
                    for _ in range(4):
                        square_tiles(hi, lo)

        def out_and_gates(y, x):
            pe.wait_ge(x_lo, c.k["x"])
            with c.loop(pe, "outs", 0, 4):
                for _ in range(4):
                    square_tiles(*y)
            model_norm()
            pe.wait_ge(x_lo, c.next("x", DT))
            gates_and_next(*x)
            c.next("x", DT)

        def a_turn_weights():
            turn([sm[:, 0, 0:P], sm[:, 0, P:2 * P], sm[:, 0, 2 * P:3 * P]], weighted, c.next("weighted"))

        def a_mix():
            pe.wait_ge(turn_read, c.at("turn"))
            pe.wait_ge(y_ready, c.at("mixed"))
            for e in range(2):
                o = bO[:, e * SEQ:(e + 1) * SEQ]
                pe.matmul(o, vtok[:, 0, e * P:(e + 1) * P], pt[:, 0:SEQ], start=True, stop=False)
                last = pe.matmul(o[:, P:SEQ], vtok[:, 1, e * P:(e + 1) * P], pt[:, SEQ:SEQ + P],
                                 start=False, stop=True)
            last.then_inc(mixed, 1)
            c.next("mixed")

        def a_norm_out():
            norm(K("avg_256"), [yo[:, 0:SEQ], yo[:, SEQ:512]], mixed_read, c.next("mixed_read"))

        def a_head(hi, lo, prev, first):
            for j in range(8):
                if first and j == 0:
                    pe.wait_ge(x_lo, c.k["x"])
                square_tiles(hi, lo)
                if first and j == 0:
                    model_norm()
                if j in (1, 2, 3, 4):
                    norm(K("avg_128"), [sqh[:, (j - 1) % 2]], sq_head, c.next("sq_head"))
                if j == 1 and prev:
                    a_turn_weights()
                if j == 2 and prev:
                    a_mix()
                if j == 3 and prev:
                    a_norm_out()
                if j in (3, 4, 5, 6):
                    rotate(qn[:, (j - 3) % 2], K("swap_128"))
                if j in (5, 6):
                    turn([vs[:, j - 5, 0:P], vs[:, j - 5, P:SEQ]], tile_taken, c.at("tile", -1))
                if j == 7:
                    pe.wait_ge(roped, c.next("roped", 4))
                    pe.wait_ge(score_read, c.at("score_read"))
                    for s in range(2):
                        q, k = qr[:, s], qr[:, 2 + s]
                        pe.matmul(bS[s][:, 0:P], q[:, 0:P], k[:, 0:P], start=True, stop=True)
                        pe.matmul(bS[s][:, P:3 * P], q[:, P:SEQ], k, start=True, stop=True).then_inc(scored, 1)
                    c.next("score_read", 2)
                if j % 2 == 0:
                    mod_slot(j // 2)
                if j in (3, 7):
                    mod_columns()

        def layer_a(x, y):
            hi, lo = x
            a_head(hi, lo, False, True)
            with c.loop(pe, "a_heads", 1, A_HEADS):
                a_head(hi, lo, True, False)
            c.next("p")
            proj_slot()
            a_turn_weights()
            a_mix()
            a_norm_out()
            c.next("x", A_HEADS)
            out_and_gates(y, x)

        def b_pair(hi, lo, prev):
            c.bank = 0
            mod_slot(0, fresh=True)
            w = slot()
            for n in range(3):
                tile(w, range(4 * n, 4 * n + 4), c_hi, c_lo, range(4))
            if prev:
                for s in range(2):
                    turn([b_sm[:, s, n * P:(n + 1) * P] for n in range(3)], weighted,
                         c.next("weighted") if s == 0 else c.at("weighted"))
            mod_slot(1)
            w = slot()
            for n in range(4):
                tile(w, range(4 * n, 4 * n + 4), c_hi, c_lo, range(4, 8))
            for n in range(3):
                norm(K("avg_64" if n == 2 else "avg_128"), [bsq[:, n]], sq_head, c.next("sq_head"))
            if prev:
                pe.wait_ge(turn_read, c.at("turn"))
                pe.wait_ge(y_ready, c.at("mixed"))
                for s in range(2):
                    o = bO[:, s * SEQ:(s + 1) * SEQ]
                    pe.matmul(o, b_vtok[:, s, 0], b_sm[:, s, 0:SEQ], start=True, stop=False)
                    last = pe.matmul(o[:, P:SEQ], b_vtok[:, s, 1], b_sm[:, s, SEQ:SEQ + P], start=False, stop=True)
                last.then_inc(mixed, 1)
                c.next("mixed")
            mod_columns()
            mod_slot(2)
            square_tiles(hi, lo)
            rotate(bq[:, 2], K("swap_64"), 3)
            for n in range(2):
                norm(K("avg_128"), [bsk[:, n]], sq_head, c.next("sq_head"))
            for s in range(2):
                turn([bv[:, s, 0:P], bv[:, s, P:SEQ]], tile_taken, c.at("tile", -1))
            mod_slot(3)
            square_tiles(hi, lo)
            pe.wait_ge(roped, c.next("roped"))
            pe.wait_ge(scaled, c.next("scaled", 2))
            pe.wait_ge(score_read, c.at("score_read"))
            for s in range(2):
                r = slice(64 * s, 64 * s + 64)
                for u, v, w_ in ((0, P, P), (P, 3 * P, SEQ)):
                    q = slice(u, u + P)
                    pe.matmul(bS[s][:, u:v], bq[:, s, q], bk[:, s, 0:w_], start=True, stop=False)
                    last = pe.matmul(bS[s][:, u:v], b_pe[r, q], b_kpe[r, 0:w_], start=False, stop=True)
                last.then_inc(scored, 1)
            c.next("score_read", 2)
            mod_columns()

        def b_tail():
            for s in range(2):
                turn([b_sm[:, s, n * P:(n + 1) * P] for n in range(3)], weighted,
                     c.next("weighted") if s == 0 else c.at("weighted"))
            pe.wait_ge(turn_read, c.at("turn"))
            pe.wait_ge(y_ready, c.at("mixed"))
            for s in range(2):
                o = bO[:, s * SEQ:(s + 1) * SEQ]
                pe.matmul(o, b_vtok[:, s, 0], b_sm[:, s, 0:SEQ], start=True, stop=False)
                last = pe.matmul(o[:, P:SEQ], b_vtok[:, s, 1], b_sm[:, s, SEQ:SEQ + P], start=False, stop=True)
            last.then_inc(mixed, 1)
            c.next("mixed")

        def layer_b(x, y):
            hi, lo = x
            for n in range(9):
                if n == 0:
                    pe.wait_ge(x_lo, c.k["x"])
                square_tiles(hi, lo)
                if n == 0:
                    model_norm()
                if n in (4, 8):
                    c.next("sq_head", 4)
                    norm(K("avg_512"), [b_csq[:, n - 4 + m] for m in range(4)], sq_head, c.k["sq_head"])
            norm(K("avg_64"), [bsq[:, 0]], sq_head, c.next("sq_head"))
            rotate(b_cs[:, 0], K("swap_64"))
            c.next("roped")
            pe.wait_ge(x_lo, c.next("x", 8))
            b_pair(hi, lo, False)
            with c.loop(pe, "b_pairs", 1, B_PAIRS):
                b_pair(hi, lo, True)
            c.bank = 0
            c.next("p")
            proj_slot(fresh=True)
            b_tail()
            c.next("x", B_PAIRS)
            out_and_gates(y, x)

        def layer_c(x, y):
            pe.wait_ge(x_lo, c.k["x"])
            model_norm()
            with c.loop(pe, "c_in", 0, 4):
                for _ in range(4):
                    square_tiles(*x)

            def group_gates(g):
                w = slot()
                pe.wait_ge(x_lo, c.next("x"))
                for n in range(8):
                    k = 4 * (g % 2) + 2 * (n // 4)
                    tile(w, [2 * n, 2 * n + 1], c_hi, c_lo, [k, k + 1])

            for g in range(5):
                if g < 4:
                    group_gates(g)
                if g:
                    for _ in range(4):
                        square_tiles(*x)
            c.next("p")
            proj_slot()
            c.next("x", DT)
            out_and_gates(y, x)

        def s_rows(m):
            pe.wait_ge(masked, c.next("rows"))
            pe.wait_ge(rows_read, c.at("rows", -1))
            pe.matmul(bR[:, 0:SEQ], K("ones", rows=64), s_acm[0][0:64], start=True, stop=True)
            pe.matmul(bS[1][:, 0:SEQ], K("ones", rows=64), s_acm[1][0:64], start=True, stop=True).then_inc(rows_done, 1)

        def s_out(m):
            pe.wait_ge(m_ready, c.next("yd"))
            pe.wait_ge(turn_read, c.at("turn"))
            pe.wait_ge(s_y_ready, c.at("yd", -1))
            for hh in range(2):
                r = slice(64 * hh, 64 * hh + 64)
                o = bO[r, 0:SEQ]
                pe.matmul(o, s_xdt[:, 0, m, r], s_e[:, hh, 0:SEQ], start=True, stop=False)
                last = pe.matmul(o[:, P:SEQ], s_xdt[:, 1, m, r], s_e[:, hh, SEQ:384], start=False, stop=True)
            last.then_inc(yd_done, 1)

        def s_norm():
            norm(K("avg_512"), [acc[:]], s_sum, c.next("s_sum"))

        def s_group(prev):
            for n in range(10):
                j = n - 2
                square_tiles(p_hi, p_lo)
                if prev and 1 <= j <= 4:
                    s_out(j - 1)
                if prev and 0 <= j <= 3:
                    s_rows(j)
                if 1 <= j <= 4:
                    x = s_xv[(j - 1) % 2]
                    turn([x[:, 0:P], x[:, P:SEQ]], gluon, c.next("gluon", 3 if j == 1 else 1))
                if j == 5:
                    pe.wait_ge(cb_read, c.at("cb"))
                    b, q = s_bc
                    pe.matmul(bS[0][:, 0:SEQ], b[:, 0:P], q, start=True, stop=True)
                    pe.matmul(bS[0][:, SEQ:384], b[:, P:SEQ], q[:, P:SEQ], start=True, stop=True).then_inc(cb_done, 1)
                    c.next("cb")
                    if prev:
                        s_norm()
            c.next("gluon", 4)

        def s_project():
            pe.wait_ge(x_lo, c.next("x", 2))
            for _ in range(8):
                w = slot()
                for e in range(2):
                    tile(w, range(8 * e, 8 * e + 8), q_hi, q_lo, range(8))

        def layer_norm():
            pe.wait_ge(tile_taken, c.at("tile"))
            for n in range(DT):
                last = pe.matmul(bR[:, 0:SEQ], K("avg_model"), h[:, n], start=n == 0, stop=n == DT - 1)
            last.then_inc(ln_done, 1)
            pe.wait_ge(factor_ready, c.at("norm"))
            for n in range(DT):
                pe.wait_ge(ln_sq, c.next("ln"))
                last = pe.matmul(bN[:, 0:SEQ], K("avg_model"), ln_c[:, n], start=n == 0, stop=n == DT - 1)
            last.then_inc(norm_summed, 1)
            c.next("norm")

        def layer_s():
            pe.wait_ge(x_lo, c.k["x"])
            square_tiles(p_hi, p_lo)
            turn([s_dt[:, 0:P], s_dt[:, P:SEQ], s_ac[:, 0:P], s_ac[:, P:SEQ]], dt_ready, 1)
            s_group(False)
            s_group(True)
            with c.loop(pe, "s_pairs", 1, S_PAIRS):
                s_group(True)
                s_project()
                s_group(True)
            s_rows(0)
            for m in range(4):
                if m < 3:
                    s_rows(m + 1)
                s_out(m)
            s_norm()
            s_project()
            layer_norm()

        def d_scores(g):
            pe.wait_ge(tile_taken, c.at("tile", -1))
            pe.wait_ge(score_read, c.at("score_read"))
            b = (bS[0], bS[1], bR)[g]
            q, k = d_q[:, g], d_k[:, g]
            pe.matmul(b[:, 0:P], q[:, 0:P], k[:, 0:P], start=True, stop=True)
            pe.matmul(b[:, P:3 * P], q[:, P:SEQ], k, start=True, stop=True).then_inc(scored, 1)
            if g == 2:
                c.next("score_read", 3)

        def d_turn_weights(g):
            turn([d_s[:, g, n * P:(n + 1) * P] for n in range(3)], weighted,
                 c.next("weighted") if g == 0 else c.at("weighted"))

        def d_turn_values(g):
            turn([d_v[:, g, 0:P], d_v[:, g, P:SEQ]], tile_taken, c.at("tile", -1))

        def d_mix():
            pe.wait_ge(turn_read, c.at("turn"))
            pe.wait_ge(y_ready, c.at("mixed", S_GROUPS))
            for g in range(3):
                pe.matmul(bO[:, 0:SEQ], d_vtok[:, g, 0], d_s[:, g, 0:SEQ], start=g == 0, stop=False)
                last = pe.matmul(bO[:, P:SEQ], d_vtok[:, g, 1], d_s[:, g, SEQ:384], start=False, stop=g == 2)
            last.then_inc(mixed, 1)
            c.next("mixed")

        def d_head(prev):
            for n in range(10):
                square_tiles(*((p_hi, p_lo) if 3 <= n <= 8 else (q_hi, q_lo)))
                if prev and n == 0:
                    d_turn_weights(2)
                if prev and n in (1, 2):
                    d_turn_values(n)
                if prev and n == 3:
                    d_mix()
                if n in (4, 5, 6):
                    d_scores(n - 4)
                if n == 7:
                    d_turn_values(0)
                if n in (8, 9):
                    d_turn_weights(n - 8)

        def layer_d():
            pe.wait_ge(x_lo, c.next("x", 2 * DT))
            d_head(False)
            d_head(True)
            with c.loop(pe, "d_pairs", 1, DIL_HEADS // 2):
                d_head(True)
                d_head(True)
            d_turn_weights(2)
            d_turn_values(1)
            d_turn_values(2)
            d_mix()
            pe.wait_ge(x_lo, c.next("x", DIL_HEADS))
            with c.loop(pe, "d_out", 0, 2):
                for _ in range(4):
                    w = slot()
                    for e in range(2):
                        tile(w, range(8 * e, 8 * e + 8), c_hi, c_lo, range(8))
            layer_norm()

        pe.wait_ge(lam_in, 1)
        pe.matmul(bS[0][:, 0:4], K("ones"), tiny[:, 0:4], start=True, stop=True).then_inc(lam_sum, 1)
        c.next("x", DT)
        PQ = [(p_hi, p_lo), (q_hi, q_lo)]
        for layer in range(DEPTH):
            x, y = PQ[layer % 2], PQ[(layer + 1) % 2]
            if layer in (0, 3):
                layer_a(x, y)
            elif layer == 1:
                layer_b(x, y)
            else:
                layer_c(x, y)
        layer_s()
        layer_d()

    @block.scalar
    def _(act):
        c = Steps(counts, "act")

        def link(ins):
            ins.then_inc(act_step, 1)
            act.wait_ge(act_step, c.next("act"))

        def hold(sem_, value):
            act.wait_ge(sem_, value)
            act.sem_inc(act_passed, 1)

        def hi_ahead(half, ahead=2):
            k = c.k["slot"] + ahead - 1
            cols = slice(half * HALF, (half + 1) * HALF)
            if half == 0:
                act.wait_ge(landed[k % RAW], c.fours("slot", ahead - 1) * 16)
            act.activation(w_hi[k % SPLIT][:, cols], raw[k % RAW][:, cols], ACT.Copy).then_inc(hi_ready, 1)

        def tick(tiles=1):
            c.next("slot")
            if tiles == 1:
                act.wait_ge(half_used, c.next("half"))
            else:
                act.wait_ge(tile_done, c.at("tile", (tiles + 1) // 2))
            hi_ahead(0)
            act.wait_ge(tile_done, c.next("tile", tiles))
            hi_ahead(1)
            act.wait_ge(tile_taken, c.at("tile"))

        def tail(n, hi, gain, sem_, value, par):
            hold(sem_, value)
            act.activation(hi[:, n], h[:, n], ACT.Copy, scale=gain).then_inc(x_hi, 1)
            hold(summed, c.at("sum", -1))
            act.activation(sq[:, par], h[:, n], ACT.Square).then_inc(squared, 1)
            c.next("sum")

        def factor(dst, eps="eps_6"):
            act.wait_ge(factor_ready, c.at("norm"))
            act.wait_ge(norm_summed, c.next("norm"))
            link(act.activation(bN[:, SEQ:], bN[:, 0:SEQ], ACT.Ln, bias=K(eps)))
            act.activation(dst, bN[:, SEQ:], ACT.Exp, scale=-0.5).then_inc(factor_ready, 1)

        def sigmoid(buf, sem_, value):
            act.wait_ge(sem_, value)
            link(act.activation(buf, buf, ACT.Exp, scale=-1.0))
            link(act.activation(buf, buf, ACT.Ln, bias=1.0))
            act.activation(buf, buf, ACT.Exp, scale=-1.0).then_inc(sig_ready, 1)
            c.next("sig")

        def p_slot(layer):
            tick(8)

        def gates(hi, gain_at, last):
            for half in range(2):
                if half:
                    tick(8)
                for i4 in range(1):
                    with c.loop(act, "gates_last" if last else "gates", 0, 2) as i:
                        for j in range(4):
                            n = i * 4 + (8 * half + j)
                            tick()
                            sigmoid(zg[:, j % 2], clamped, c.next("clamped"))
                            if not last:
                                tail(n, hi, vec[:, bass.ds(i * 4 + (gain_at + 8 * half + j), 1)], res_ready,
                                     c.next("res"), j % 2)
                            else:
                                act.wait_ge(res_ready, c.next("res"))

        def out_and_gates(layer, x, y):
            a = VEC["ple_norm"] + layer * DT
            with c.loop(act, "outs", 0, 4) as i:
                for j in range(4):
                    tick()
                    tail(i * 4 + j, x[0], vec[:, bass.ds(i * 4 + (a + j), 1)], tile_taken, c.at("tile"), j % 2)
            factor(rstd[:])
            gates(y[0], VEC["norm_gain"] + (layer + 1) * DT, layer == DEPTH - 1)

        def turned(dst, src):
            act.wait_ge(turn_done, c.next("turn"))
            act.activation(dst, src, ACT.Copy).then_inc(turn_read, 1)

        def a_square_out():
            act.wait_ge(mixed, c.next("mixed"))
            act.activation(yo, bO[:], ACT.Square).then_inc(mixed_read, 1)

        def a_y_hi(y, i):
            hold(y_ready, c.next("y"))
            act.activation(y[0][:, bass.ds(i * 2, 2), :], yo.rearrange("p (a b) -> p a b", a=2), ACT.Copy).then_inc(x_hi, 1)

        def a_softmax():
            act.wait_ge(maxed, c.next("maxed"))
            for s in range(2):
                act.activation(sm[:, s, 0:P], sm[:, s, 0:P], ACT.Exp, bias=tiny[:, 4 + 2 * s:5 + 2 * s],
                               accum_out=tiny[:, 8 + 2 * s:9 + 2 * s])
                last = act.activation(sm[:, s, P:384], sm[:, s, P:384], ACT.Exp, bias=tiny[:, 5 + 2 * s:6 + 2 * s],
                                      accum_out=tiny[:, 9 + 2 * s:10 + 2 * s])
            last.then_inc(exped, 1)

        def a_head(y, i, prev, first):
            for j in range(8):
                tick()
                if j < 4:
                    act.activation(sqh[:, j % 2], qs[:, j % 3], ACT.Square).then_inc(sq_head, 1)
                if first and j == 0:
                    pass
                if j in (1, 2, 3, 4):
                    factor(rsn[:, (j - 1) % 2])
                if j == 1 and prev:
                    turned(pt, bT[:, 0:384])
                if j == 2 and prev:
                    a_square_out()
                if j == 3 and prev:
                    factor(rsn[:, 2])
                if j == 4 and prev:
                    a_y_hi(y, i - 1)
                if j in (5, 6):
                    turned(vtok[:, :, (j - 5) * P:(j - 4) * P], bT[:, 0:SEQ].rearrange("p (a b) -> p a b", a=2))
                if j in (6, 7):
                    sigmoid(zc[:, j - 6], clamped, c.next("clamped"))
                if j == 7:
                    a_softmax()
                if j % 2 == 0:
                    tick()
                if j in (3, 7):
                    c.next("tile")

        def layer_a(layer, x, y):
            factor(rstd[:])
            a_head(y, 0, False, True)
            with c.loop(act, "a_heads", 1, A_HEADS) as i:
                a_head(y, i, True, False)
            split_p(layer)
            tick(8)
            turned(pt, bT[:, 0:384])
            a_square_out()
            factor(rsn[:, 2])
            a_y_hi(y, A_HEADS - 1)
            out_and_gates(layer, x, y)

        def squares(dst, src):
            act.activation(dst, src, ACT.Square).then_inc(sq_head, 1)

        def b_y_hi(y, i):
            hold(y_ready, c.next("y"))
            act.activation(y[0][:, bass.ds(i * 2, 2), :], b_yo.rearrange("p (a b) -> p a b", a=2), ACT.Copy).then_inc(x_hi, 1)

        def b_pair(y, i, prev):
            tick()
            tick(3)
            for n in range(3):
                squares(bsq[:, n], bq[:, n])
            if prev:
                for s in range(2):
                    turned(b_sm[:, s], bT[:, 0:384])
            tick()
            tick(4)
            for n in range(2):
                squares(bsk[:, n], bk[:, n])
            for n in range(3):
                factor(rsn[:, n])
            c.next("tile")
            tick()
            tick()
            for n in range(2):
                factor(rsn[:, n])
            for s in range(2):
                turned(b_vtok[:, s], bT[:, 0:SEQ].rearrange("p (a b) -> p a b", a=2))
            sigmoid(b_zc[:, 0], clamped, c.next("clamped"))
            if prev:
                b_y_hi(y, i - 1)
            tick()
            tick()
            sigmoid(b_zc[:, 1], clamped, c.next("clamped"))
            act.wait_ge(maxed, c.next("maxed"))
            for s in range(2):
                act.activation(b_sm[:, s, 0:P], b_sm[:, s, 0:P], ACT.Exp, bias=tiny[:, 4 + 2 * s:5 + 2 * s],
                               accum_out=tiny[:, 8 + 2 * s:9 + 2 * s])
                last = act.activation(b_sm[:, s, P:384], b_sm[:, s, P:384], ACT.Exp, bias=tiny[:, 5 + 2 * s:6 + 2 * s],
                                      accum_out=tiny[:, 9 + 2 * s:10 + 2 * s])
            last.then_inc(exped, 1)
            c.next("tile")

        def layer_b(layer, x, y):
            for n in range(9):
                tick_first = n == 0
                if tick_first:
                    factor(rstd[:])
                tick()
                if n < 8:
                    name = "b_cq_norm" if n < 4 else "b_ckv_norm"
                    act.activation(c_hi[:, n], b_cs[:, n % 2], ACT.Copy, scale=V(name, n % 4)).then_inc(x_hi, 1)
                    squares(b_csq[:, n], b_cs[:, n % 2])
                else:
                    squares(bsq[:, 0], b_cs[:, 0])
                if n == 4:
                    factor(b_rq)
            factor(b_rkv)
            factor(rsn[:, 0])
            b_pair(y, 0, False)
            with c.loop(act, "b_pairs", 1, B_PAIRS) as i:
                b_pair(y, i, True)
            split_p(layer)
            tick(8)
            for s in range(2):
                turned(b_sm[:, s], bT[:, 0:384])
            b_y_hi(y, B_PAIRS - 1)
            c.next("mixed", B_PAIRS)
            out_and_gates(layer, x, y)

        def softplus(e, u, w, l):
            act.wait_ge(soft_in, c.next("soft"))
            act.activation(e, u, ACT.Exp, scale=-1.0).then_inc(soft_out, 1)
            act.wait_ge(soft_in, c.next("soft"))
            link(act.activation(l, u, ACT.Ln))
            act.activation(w, l, ACT.Exp, scale=-1.0).then_inc(soft_out, 1)

        def c_split(g):
            act.wait_ge(conv_done, DT)
            act.activation(c_hi[:, 4 * (g % 2):4 * (g % 2) + 4], xc[:, 4 * g:4 * g + 4], ACT.Copy).then_inc(x_hi, 1)

        def c_chain(half):
            u = rg[:, 2 * half:2 * half + 2].rearrange("p a b -> p (a b)")
            act.wait_ge(chain_in, c.next("chain"))
            act.preload_act_table(ACT.Tanh)
            link(act.activation(bS[0][:], u, ACT.Tanh))
            act.activation(u, u, ACT.Exp, scale=-1.0).then_inc(chain_out, 1)
            act.preload_act_table_set("natural_log_exp_and_others")
            act.wait_ge(chain_in, c.next("chain"))
            act.activation(bS[1][:], bS[0][:], ACT.Ln, scale=2.0).then_inc(act_step, 1)
            c.next("act")
            link(act.activation(bR[:], bS[0][:], ACT.Ln, bias=1.0))
            act.activation(bS[1][:], bS[1][:], ACT.Exp, scale=0.5).then_inc(chain_out, 1)
            act.activation(bR[:], bR[:], ACT.Exp, scale=-0.5).then_inc(chain_out, 1)

        def layer_c(layer, x, y):
            softplus(soft[:, 0], soft[:, 1], soft[:, 2], sp8)
            factor(rstd[:])
            with c.loop(act, "c_in", 0, 4):
                for _ in range(4):
                    tick()
            c_split(0)
            for g in range(5):
                if g < 4:
                    tick(8)
                    for buf in (rg, ig):
                        b = buf.rearrange("p a b -> p (a b)")
                        link(act.activation(b, b, ACT.Exp, scale=-1.0))
                        link(act.activation(b, b, ACT.Ln, bias=1.0))
                        act.activation(b, b, ACT.Exp, scale=-1.0).then_inc(gates_out, 1)
                if g < 3:
                    c_split(g + 1)
                for j in range(4 if g else 0):
                    tick()
                    sigmoid(c_zc, clamped, c.next("clamped"))
                    act.wait_ge(gated, c.next("gated"))
                    act.activation(y[0][:, 4 * (g - 1) + j], c_gz, ACT.Copy).then_inc(x_hi, 1)
                    if g < 4 and j in (1, 3):
                        c_chain(j // 2)
                if g == 0:
                    c_chain(0)
                    c_chain(1)
            split_p(layer)
            tick(8)
            out_and_gates(layer, x, y)

        def split_p(layer):
            act.wait_ge(p_in, 16 * (c.next("p")))
            act.activation(c_hi[:, 0:2], p_raw, ACT.Copy).then_inc(p_hi_ready, 1)

        def modulated(hi, at, name):
            with c.loop(act, name, 0, 4) as i:
                for j in range(4):
                    n = i * 4 + j
                    act.activation(hi[:, n], h[:, n], ACT.Identity, bias=mod[:, bass.ds(i * 4 + (at + j), 1)],
                                   scale=mod[:, bass.ds(i * 4 + (at + DT + j), 1)]).then_inc(x_hi, 1)

        def s_decay():
            act.wait_ge(rows_read, c.next("rows"))
            act.activation(s_e, s_e, ACT.Exp).then_inc(decayed, 1)

        def s_y_hi(par):
            act.wait_ge(y_ready, c.next("y"))
            act.activation(q_hi[:, 4 * par:4 * par + 4], s_y, ACT.Copy).then_inc(x_hi, 1)

        def s_group(par, prev):
            for n in range(10):
                tick()
                if prev and 2 <= n <= 5:
                    s_decay()
                sigmoid(s_zc, clamped, c.next("clamped"))
                if prev and n == 7:
                    factor(rsn[:, 2], "eps_5")
                if prev and n == 8:
                    s_y_hi(1 - par)

        def s_project():
            for _ in range(8):
                tick(2)

        def layer_norm(w):
            for n in range(DT):
                act.wait_ge(ln_go, c.next("ln_go"))
                act.activation(ln_c[:, n], h[:, n], ACT.Square).then_inc(ln_sq, 1)
            factor(rstd[:], "eps_5")

        def layer_s():
            act.wait_ge(mod_ready, 1)
            modulated(p_hi, 0, "mod")
            tick()
            act.activation(tiny[:, 0:1], V("s_A_log"), ACT.Exp).then_inc(soft_out, 1)
            s_softplus()
            s_group(0, False)
            s_group(1, True)
            with c.loop(act, "s_pairs", 1, S_PAIRS):
                s_group(0, True)
                s_project()
                s_group(1, True)
            for m in range(4):
                s_decay()
            factor(rsn[:, 2], "eps_5")
            s_y_hi(1)
            s_project()
            layer_norm(0)

        def s_softplus():
            softplus(s_y[:, 0], s_y[:, 1], s_y[:, 2], s_y[:, 3])

        def d_softmax():
            act.wait_ge(maxed, c.next("maxed"))
            act.activation(d_s[:, :, 0:P], d_s[:, :, 0:P], ACT.Exp, bias=tiny[:, 4:5], scale=P ** -0.5,
                           accum_out=tiny[:, 8:9])
            act.activation(d_s[:, :, P:384], d_s[:, :, P:384], ACT.Exp, bias=tiny[:, 5:6], scale=P ** -0.5,
                           accum_out=tiny[:, 9:10]).then_inc(exped, 1)

        def d_weights(g):
            turned(d_s[:, g], bT[:, 0:384])

        def d_values(g):
            turned(d_vtok[:, g], bT[:, 0:SEQ].rearrange("p (a b) -> p a b", a=2))

        def d_y_hi(n):
            hold(y_ready, c.next("y"))
            act.activation(c_hi[:, n], rsn[:, 0], ACT.Copy).then_inc(x_hi, 1)

        def d_head(i, par, prev):
            for n in range(10):
                tick()
                if prev and n == 0:
                    d_weights(2)
                if prev and n in (1, 2):
                    d_values(n)
                if prev and n == 3:
                    d_y_hi(i * 2 + (par - 1))
                if n == 6:
                    d_softmax()
                if n == 7:
                    d_values(0)
                if n in (8, 9):
                    d_weights(n - 8)
                if n == 9:
                    sigmoid(d_zc[:], clamped, c.next("clamped"))

        def layer_d():
            c.next("turn", 1 + 4 * S_GROUPS)
            act.wait_ge(ln_go, c.next("ln_go", DT))
            with c.loop(act, "kv", 0, 4) as i:
                for j in range(4):
                    n = i * 4 + j
                    act.activation(p_hi[:, n], h[:, n], ACT.Copy).then_inc(x_hi, 1)
            modulated(q_hi, 48, "mod")
            d_head(0, 0, False)
            d_head(0, 1, True)
            with c.loop(act, "d_pairs", 1, DIL_HEADS // 2) as i:
                d_head(i, 0, True)
                d_head(i, 1, True)
            d_weights(2)
            d_values(1)
            d_values(2)
            d_y_hi(DIL_HEADS - 1)
            with c.loop(act, "d_out", 0, 2):
                for _ in range(4):
                    tick(2)
            layer_norm(1)

        act.preload_act_table(ACT.Sin)
        act.wait_ge(trig_in, 1)
        for n, (sin, half) in enumerate(((sin_a, cos_a), (sin_b, cos_b))):
            act.activation(half[:], sin[:], ACT.Sin, scale=0.5).then_inc(act_step, 1)
            act.wait_ge(act_step, c.next("act"))
            act.activation(sin[:], sin[:], ACT.Sin).then_inc(trig_out, 1)
        act.preload_act_table_set("natural_log_exp_and_others")
        b = tiny[:, 48:64]
        act.wait_ge(ada_in, 1)
        link(act.activation(b, b, ACT.Exp, scale=-1.0))
        link(act.activation(b, b, ACT.Ln, bias=1.0))
        act.activation(b, b, ACT.Exp, scale=-1.0).then_inc(ada_z, 1)
        act.wait_ge(ada_in, 2)
        link(act.activation(ada_hl[:, :, 0], b, ACT.Copy))
        act.activation(ada_hz[:, :, 0], b, ACT.Copy).then_inc(ada_out, 1)
        act.wait_ge(lam_sum, 1)
        act.activation(tiny[:, 4:8], bS[0][:, 0:4], ACT.Exp).then_inc(lam_exp, 1)
        c.k["slot"] = 0
        for ahead in (1, 2):
            hi_ahead(0, ahead)
            hi_ahead(1, ahead)
        act.wait_ge(h_in, 16)

        def start(i):
            for j in range(4):
                tail(i * 4 + j, p_hi, vec[:, bass.ds(i * 4 + (VEC["norm_gain"] + j), 1)], h_in, 16, j % 2)
        start(0)
        with c.loop(act, "start", 1, 4) as i:
            start(i)
        PQ = [(p_hi, p_lo), (q_hi, q_lo)]
        for layer in range(DEPTH):
            x, y = PQ[layer % 2], PQ[(layer + 1) % 2]
            if layer in (0, 3):
                layer_a(layer, x, y)
            elif layer == 1:
                layer_b(layer, x, y)
            else:
                layer_c(layer, x, y)
        layer_s()
        layer_d()

    @block.vector
    def _(dve):
        c = Steps(counts, "dve")

        def link(ins):
            ins.then_inc(dve_step, 1)
            dve.wait_ge(dve_step, c.next("dve"))

        def lo_half(half, ahead=2):
            k = c.k["slot"] + ahead - 1
            cols = slice(half * HALF, (half + 1) * HALF)
            dve.wait_ge(hi_ready, c.at("slot", ahead) * 2 + (half - 1) if half == 0 else c.at("slot", ahead) * 2)
            dve.tensor_tensor(w_lo[k % SPLIT][:, cols], raw[k % RAW][:, cols], w_hi[k % SPLIT][:, cols], SUB).then_inc(lo_ready, 1)

        def begin():
            c.next("slot")
            lo_half(0)

        def take():
            dve.wait_ge(tile_done, c.next("tile"))
            g = G[c.bank][:, 0:SEQ]
            c.bank ^= 1
            return g

        def mod_tick(m):
            begin()
            g = take()[0:2]
            if m % 2 == 0:
                dve.tensor_copy(acc[0:2], g).then_inc(tile_taken, 1)
            else:
                dve.wait_ge(tile_taken, c.at("tile", -1))
                dve.tensor_tensor(acc[0:2], acc[0:2], g, ADD).then_inc(tile_taken, 1)
            lo_half(1)

        def mod_columns(i, at):
            two = lambda base: bass.ds(i * 4 + (base + at), 2)
            dve.tensor_tensor(mod[:, two(0)], take()[:, 0:2], vec[:, two(VEC["ada_b"])], ADD).then_inc(tile_taken, 1)

        def tail(n, x, gain):
            dve.wait_ge(x_hi, c.next("x"))
            dve.scalar_tensor_tensor(x[1][:, n], h[:, n], gain, x[0][:, n], MUL, SUB).then_inc(x_lo, 1)

        def factor():
            dve.wait_ge(factor_ready, c.next("norm"))

        def p_slot():
            c.next("slot")
            for n in range(8):
                g = take()
                dve.tensor_copy(proj[:, n], g).then_inc(tile_taken, 1)
            lo_half(0)
            lo_half(1)

        def gates(x, gain_at, last):
            for half in range(2):
                if half:
                    p_slot()
                with c.loop(dve, "gates_last" if last else "gates", 0, 2) as i:
                    for j in range(4):
                        n = i * 4 + (8 * half + j)
                        begin()
                        g = take()
                        dve.tensor_tensor(zg[:, j % 2], g, rstd[:], MUL).then_inc(tile_taken, 1)
                        lo_half(1)
                        dve.wait_ge(sig_ready, c.next("sig"))
                        link(dve.tensor_tensor(sg[:, j % 2], zg[:, j % 2], proj[:, i * 4 + j], MUL))
                        dve.tensor_tensor(h[:, n], h[:, n], sg[:, j % 2], ADD).then_inc(res_ready, 1)
                        dve.wait_ge(res_ready, c.next("res"))
                        if not last:
                            tail(n, x, vec[:, bass.ds(i * 4 + (gain_at + 8 * half + j), 1)])

        def out_and_gates(layer, x, y):
            a = VEC["ple_norm"] + layer * DT
            with c.loop(dve, "outs", 0, 4) as i:
                for j in range(4):
                    n = i * 4 + j
                    begin()
                    g = take()
                    dve.tensor_tensor(h[:, n], g, h[:, n], ADD).then_inc(tile_taken, 1)
                    lo_half(1)
                    dve.wait_ge(tile_taken, c.at("tile"))
                    tail(n, x, vec[:, bass.ds(i * 4 + (a + j), 1)])
            factor()
            gates(y, VEC["norm_gain"] + (layer + 1) * DT, layer == DEPTH - 1)

        def a_weigh(j):
            dve.wait_ge(exped, c.next("exped"))
            link(dve.reciprocal(tiny[:, 12:16], tiny[:, 8:12]))
            link(dve.tensor_scalar(tiny[:, 14:16], tiny[:, 14:16], lam[:, j:j + 1], None, MUL))
            spans = ((0, P), (P, 384))
            for b, (u, v) in enumerate(spans):
                last = dve.tensor_scalar(sm[:, 0, u:v], sm[:, 0, u:v], tiny[:, 12 + b:13 + b], None, MUL)
            link(last)
            for b, (u, v) in enumerate(spans):
                last = dve.scalar_tensor_tensor(sm[:, 0, u:v], sm[:, 1, u:v], tiny[:, 14 + b:15 + b],
                                                sm[:, 0, u:v], MUL, ADD)
            last.then_inc(weighted, 1)

        def a_silu(e):
            dve.wait_ge(sig_ready, c.next("sig"))
            link(dve.tensor_tensor(gz[:, e], gz[:, e], zc[:, e], MUL))

        def a_finish(j):
            factor()
            for e in range(2):
                last = dve.tensor_tensor(gz[:, e], gz[:, e], rsn[:, 2], MUL)
            link(last)
            for e in range(2):
                last = dve.scalar_tensor_tensor(yo[:, e * SEQ:(e + 1) * SEQ], bO[:, e * SEQ:(e + 1) * SEQ],
                                                tiny[:, 16 + 2 * j + e:17 + 2 * j + e], gz[:, e], MUL, MUL)
            last.then_inc(y_ready, 1)
            dve.wait_ge(y_ready, c.next("y"))

        def a_y_lo(y, i):
            dve.wait_ge(x_hi, c.next("x"))
            y2 = bass.ds(i * 2, 2)
            dve.tensor_tensor(y[1][:, y2, :], yo.rearrange("p (a b) -> p a b", a=2), y[0][:, y2, :], SUB).then_inc(x_lo, 1)

        def a_head(y, i, prev, first, jl):
            for j in range(8):
                begin()
                g = take()
                if first and j == 0:
                    factor()
                dve.wait_ge(scaled, c.at("scaled"))
                dve.wait_ge(roped, c.at("rot"))
                if j < 4:
                    dst = qs[:, j % 3]
                elif j < 6:
                    dst = vs[:, j - 4]
                else:
                    dst = gz[:, j - 6]
                dve.tensor_tensor(dst, g, rstd[:], MUL).then_inc(tile_taken, 1)
                lo_half(1)
                if j in (2, 3, 4, 5):
                    n = j - 2
                    factor()
                    gain = V("a_q_norm" if n < 2 else "a_k_norm", jl)
                    dve.scalar_tensor_tensor(qn[:, n % 2], qs[:, n % 3], gain, rsn[:, n % 2], MUL, MUL).then_inc(scaled, 1)
                    c.next("scaled")
                if j in (3, 4, 5, 6):
                    n = j - 3
                    dve.wait_ge(rot_done, c.next("rot"))
                    dve.tensor_tensor(qr[:, n], bR[:, 0:SEQ], sin_a[:], MUL).then_inc(rot_read, 1)
                    dve.wait_ge(rot_read, c.at("rot"))
                    dve.wait_ge(cos_done, c.at("rot"))
                    dve.tensor_tensor(qr[:, n], qr[:, n], t2[:, n % 2], ADD).then_inc(roped, 1)
                if j == 0 and prev:
                    a_silu(1)
                    a_weigh(jl)
                if j == 4 and prev:
                    a_finish(jl)
                if j == 5 and prev:
                    a_y_lo(y, i - 1)
                if j == 7:
                    a_silu(0)
                    for s in range(2):
                        dve.wait_ge(scored, c.next("scored"))
                        dve.scalar_tensor_tensor(sm[:, s], bS[s][:, 0:384], P ** -0.5, K("mask"), MUL, ADD).then_inc(score_read, 1)
                    dve.wait_ge(score_read, c.at("scored"))
                    for s in range(2):
                        dve.tensor_reduce(tiny[:, 4 + 2 * s:5 + 2 * s], sm[:, s, 0:P], AX.X, MAX, negate=True)
                        last = dve.tensor_reduce(tiny[:, 5 + 2 * s:6 + 2 * s], sm[:, s, P:384], AX.X, MAX, negate=True)
                    last.then_inc(maxed, 1)
                if j % 2 == 0:
                    mod_tick(j // 2)
                if j in (3, 7):
                    mod_columns(i, 64 * jl + j // 2 - 1)

        def layer_a(layer, x, y):
            jl = 0 if layer == 0 else 1
            a_head(y, 0, False, True, jl)
            with c.loop(dve, "a_heads", 1, A_HEADS) as i:
                a_head(y, i, True, False, jl)
            split_p(layer)
            a_silu(1)
            a_weigh(jl)
            p_slot()
            a_finish(jl)
            a_y_lo(y, A_HEADS - 1)
            c.next("mixed", A_HEADS)
            out_and_gates(layer, x, y)

        def b_scale(buf, gain, fac, out=None):
            factor()
            dve.scalar_tensor_tensor(buf, buf, gain, fac, MUL, MUL).then_inc(scaled, 1)
            c.next("scaled")

        def rope(dst, sin, other):
            dve.wait_ge(rot_done, c.next("rot"))
            dve.tensor_tensor(dst, bR[:, 0:SEQ], sin, MUL).then_inc(rot_read, 1)
            dve.wait_ge(rot_read, c.at("rot"))
            dve.wait_ge(cos_done, c.at("rot"))
            dve.tensor_tensor(dst, dst, other, ADD).then_inc(roped, 1)

        def b_finish():
            dve.wait_ge(sig_ready, c.next("sig", 2))
            for s in range(2):
                last = dve.tensor_tensor(b_gz[:, s], b_gz[:, s], b_zc[:, s], MUL)
            link(last)
            dve.wait_ge(mixed, c.next("mixed"))
            dve.tensor_tensor(b_yo, bO[:], b_gz.rearrange("p a b -> p (a b)"), MUL).then_inc(y_ready, 1)
            dve.wait_ge(y_ready, c.next("y"))

        def b_y_lo(y, i):
            dve.wait_ge(x_hi, c.next("x"))
            y2 = bass.ds(i * 2, 2)
            dve.tensor_tensor(y[1][:, y2, :], b_yo.rearrange("p (a b) -> p a b", a=2), y[0][:, y2, :], SUB).then_inc(x_lo, 1)

        def b_pair(y, i, prev):
            c.bank = 0
            mod_tick(0)
            c.next("slot")
            for n in range(3):
                g = take()
                dve.wait_ge(weighted, c.at("exped"))
                dve.tensor_tensor(bq[:, n], g, b_rq, MUL).then_inc(tile_taken, 1)
            lo_half(0)
            lo_half(1)
            mod_tick(1)
            c.next("slot")
            for n in range(4):
                g = take()
                dst = bv[:, n // 2] if n % 2 else bk[:, n // 2]
                dve.tensor_tensor(dst, g, b_rkv, MUL).then_inc(tile_taken, 1)
            lo_half(0)
            lo_half(1)
            dve.wait_ge(tile_taken, c.at("tile"))
            for n in range(3):
                b_scale(bq[:, n], V("b_qr" if n == 2 else "b_qn"), rsn[:, n])
            if prev:
                b_finish()
            mod_columns(i, 32)
            mod_tick(2)
            begin()
            g = take()
            dve.tensor_tensor(b_gz[:, 0], g, rstd[:], MUL).then_inc(tile_taken, 1)
            lo_half(1)
            rope(b_pe, sin_b[:], b_t2)
            for n in range(2):
                b_scale(bk[:, n], V("b_kn"), rsn[:, n])
            if prev:
                b_y_lo(y, i - 1)
            mod_tick(3)
            begin()
            g = take()
            dve.tensor_tensor(b_gz[:, 1], g, rstd[:], MUL).then_inc(tile_taken, 1)
            lo_half(1)
            for s in range(2):
                dve.wait_ge(scored, c.next("scored"))
                dve.scalar_tensor_tensor(b_sm[:, s], bS[s][:, 0:384], 192 ** -0.5, K("mask"), MUL, ADD).then_inc(score_read, 1)
            dve.wait_ge(score_read, c.at("scored"))
            for s in range(2):
                dve.tensor_reduce(tiny[:, 4 + 2 * s:5 + 2 * s], b_sm[:, s, 0:P], AX.X, MAX, negate=True)
                last = dve.tensor_reduce(tiny[:, 5 + 2 * s:6 + 2 * s], b_sm[:, s, P:384], AX.X, MAX, negate=True)
            last.then_inc(maxed, 1)
            dve.wait_ge(exped, c.next("exped"))
            link(dve.reciprocal(tiny[:, 12:16], tiny[:, 8:12]))
            for s in range(2):
                for b, (u, v) in enumerate(((0, P), (P, 384))):
                    last = dve.tensor_scalar(b_sm[:, s, u:v], b_sm[:, s, u:v],
                                             tiny[:, 12 + 2 * s + b:13 + 2 * s + b], None, MUL)
            last.then_inc(weighted, 1)
            mod_columns(i, 34)

        def layer_b(layer, x, y):
            for n in range(9):
                begin()
                g = take()
                if n == 0:
                    factor()
                dve.tensor_tensor(b_cs[:, n % 2], g, rstd[:], MUL).then_inc(tile_taken, 1)
                lo_half(1)
                if n < 8:
                    name = "b_cq_norm" if n < 4 else "b_ckv_norm"
                    dve.wait_ge(x_hi, c.next("x"))
                    dve.scalar_tensor_tensor(c_lo[:, n], b_cs[:, n % 2], V(name, n % 4), c_hi[:, n], MUL, SUB).then_inc(x_lo, 1)
                    dve.wait_ge(x_lo, c.at("x"))
            c.next("norm", 2)
            b_scale(b_cs[:, 0], V("b_kr"), rsn[:, 0])
            rope(b_kpe, sin_b[:], b_t2)
            dve.wait_ge(roped, c.at("rot"))
            b_pair(y, 0, False)
            with c.loop(dve, "b_pairs", 1, B_PAIRS) as i:
                b_pair(y, i, True)
            c.bank = 0
            split_p(layer)
            p_slot()
            b_finish()
            b_y_lo(y, B_PAIRS - 1)
            out_and_gates(layer, x, y)

        def softplus(z, e, u, w, l, out):
            dve.scalar_tensor_tensor(u, z, -1.0, z, MUL, MAX).then_inc(soft_in, 1)
            dve.wait_ge(soft_out, c.next("soft"))
            dve.tensor_scalar(u, e, 1.0, None, ADD).then_inc(soft_in, 1)
            dve.wait_ge(soft_out, c.next("soft"))
            link(dve.tensor_scalar(u, u, 1.0, None, SUB))
            link(dve.tensor_tensor(e, e, u, SUB))
            link(dve.tensor_tensor(e, e, w, MUL))
            link(dve.tensor_tensor(l, l, e, ADD))
            link(dve.scalar_tensor_tensor(out, z, 0.0, l, MAX, ADD))

        def c_split(g):
            dve.wait_ge(x_hi, c.next("x"))
            k = slice(4 * (g % 2), 4 * (g % 2) + 4)
            dve.tensor_tensor(c_lo[:, k], xc[:, 4 * g:4 * g + 4], c_hi[:, k], SUB).then_inc(x_lo, 1)

        def c_chain(g, half):
            two = slice(2 * half, 2 * half + 2)
            u, b = rg[:, two].rearrange("p a b -> p (a b)"), ig[:, two].rearrange("p a b -> p (a b)")
            for n in range(2):
                last = dve.tensor_scalar(rg[:, 2 * half + n], rg[:, 2 * half + n],
                                         sp8[:, 4 * g + 2 * half + n:4 * g + 2 * half + n + 1], None, MUL)
            last.then_inc(chain_in, 1)
            link(dve.tensor_tensor(ig[:, two], ig[:, two], xc[:, 4 * g + 2 * half:4 * g + 2 * half + 2], MUL))
            dve.wait_ge(chain_out, c.next("chain"))
            dve.tensor_scalar(bS[0][:], bS[0][:], 1e-19, None, MAX).then_inc(chain_in, 1)
            dve.wait_ge(chain_out, c.next("chain", 2))
            link(dve.tensor_tensor(b, b, bS[1][:], MUL))
            link(dve.tensor_tensor(b, b, bR[:], MUL))
            for n in range(2):
                m = 2 * half + n
                last = dve.tensor_tensor_scan(xc[:, 4 * g + m], rg[:, m], ig[:, m], 0.0, MUL, ADD)
            link(last)

        def layer_c(layer, x, y):
            lam_ = vec[:, VEC["c_lambda"]:VEC["c_lambda"] + DT]
            z = c_gz[:, 0:DT]
            link(dve.tensor_scalar(z, lam_, -1.0, None, MUL))
            softplus(z, soft[:, 0], soft[:, 1], soft[:, 2], sp8, sp8)
            link(dve.tensor_scalar(sp8, sp8, 8.0, None, MUL))
            link(dve.memset(xbp[:, :, 0:3], 0.0))
            factor()
            with c.loop(dve, "c_in", 0, 4) as i:
                for j in range(4):
                    n = i * 4 + j
                    begin()
                    g = take()
                    xb = xbp[:, j % 2]
                    dve.tensor_tensor(xb[:, 3:259], g, rstd[:], MUL).then_inc(tile_taken, 1)
                    lo_half(1)
                    dve.wait_ge(tile_taken, c.at("tile"))
                    w = lambda k: vec[:, bass.ds(i * 4 + (VEC["c_conv_w"] + DT * k + j), 1)]
                    link(dve.tensor_scalar(xc[:, n], xb[:, 0:SEQ], w(0),
                                           vec[:, bass.ds(i * 4 + (VEC["c_conv_b"] + j), 1)], MUL, ADD))
                    for k in (1, 2):
                        link(dve.scalar_tensor_tensor(xc[:, n], xb[:, k:k + SEQ], w(k), xc[:, n], MUL, ADD))
                    dve.scalar_tensor_tensor(xc[:, n], xb[:, 3:3 + SEQ], w(3), xc[:, n], MUL, ADD).then_inc(conv_done, 1)
            dve.wait_ge(conv_done, DT)
            c_split(0)
            for g in range(5):
                if g < 4:
                    c.next("slot")
                    for n in range(8):
                        t_ = take()
                        m = 2 * (n // 4) + n % 2
                        bias = V("c_b_x" if n % 4 > 1 else "c_b_a", 4 * g + m)
                        dst = (ig if n % 4 > 1 else rg)[:, m]
                        dve.tensor_scalar(dst, t_, bias, SIG_MIN, ADD, MAX).then_inc(tile_taken, 1)
                    lo_half(0)
                    lo_half(1)
                if g < 3:
                    c_split(g + 1)
                if g < 4:
                    dve.wait_ge(gates_out, 2 * g + 2)
                for j in range(4 if g else 0):
                    begin()
                    t_ = take()
                    dve.wait_ge(x_lo, c.at("x"))
                    dve.tensor_tensor(c_gz, t_, rstd[:], MUL).then_inc(tile_taken, 1)
                    lo_half(1)
                    dve.wait_ge(sig_ready, c.next("sig"))
                    link(dve.tensor_tensor(c_gz, c_gz, c_zc, MUL))
                    n = 4 * (g - 1) + j
                    dve.tensor_tensor(c_gz, c_gz, xc[:, n], MUL).then_inc(gated, 1)
                    dve.wait_ge(x_hi, c.next("x"))
                    dve.tensor_tensor(y[1][:, n], c_gz, y[0][:, n], SUB).then_inc(x_lo, 1)
                    if g < 4 and j in (1, 3):
                        c_chain(g, j // 2)
                if g == 0:
                    c_chain(0, 0)
                    c_chain(0, 1)
            split_p(layer)
            dve.wait_ge(x_lo, c.at("x"))
            p_slot()
            out_and_gates(layer, x, y)

        def split_p(layer):
            dve.wait_ge(p_hi_ready, c.next("p"))
            dve.tensor_tensor(c_lo[:, 0:2], p_raw, c_hi[:, 0:2], SUB).then_inc(p_ready, 1)

        def modulated(x, at, name):
            with c.loop(dve, name, 0, 4) as i:
                for j in range(4):
                    n = i * 4 + j
                    x1 = ln_c[:, j]
                    link(dve.tensor_scalar(x1, h[:, n], mod[:, bass.ds(i * 4 + (at + DT + j), 1)],
                                           mod[:, bass.ds(i * 4 + (at + j), 1)], MUL, ADD))
                    dve.wait_ge(x_hi, c.next("x"))
                    dve.tensor_tensor(x[1][:, n], x1, x[0][:, n], SUB).then_inc(x_lo, 1)
                    dve.wait_ge(x_lo, c.at("x"))
            dve.sem_inc(mod_x, 1)

        def s_conv(i, par, n):
            xb = s_xbp[:, n % 2]
            if n < 2:
                dst = s_bc[n]
                dve.wait_ge(cb_done, c.at("cb"))
                a, b = 2, 32 + 8 * n + par
            else:
                dst = s_xv[n % 2]
                a, b = 8, 4 * par + n - 2
            dve.wait_ge(tile_taken, c.at("tile"))
            w = lambda k: vec[:, bass.ds(i * a + (VEC["s_conv_w"] + 48 * k + b), 1)]
            link(dve.tensor_scalar(dst, xb[:, 0:SEQ], w(0), vec[:, bass.ds(i * a + (VEC["s_conv_b"] + b), 1)], MUL, ADD))
            for k in (1, 2):
                link(dve.scalar_tensor_tensor(dst, xb[:, k:k + SEQ], w(k), dst, MUL, ADD))
            dve.scalar_tensor_tensor(dst, xb[:, 3:3 + SEQ], w(3), dst, MUL, ADD).then_inc(conved, 1)
            c.next("conved")

        def s_y_out(m):
            dve.wait_ge(yd_done, c.next("yd"))
            link(dve.tensor_tensor(s_y[:, m], bO[:, 0:SEQ], s_dx[:, m], ADD))
            dve.tensor_tensor(s_y[:, m], s_y[:, m], s_z[:, m], MUL).then_inc(s_y_ready, 1)

        def s_inputs(i, par, m):
            dve.wait_ge(gluon, c.next("gluon", 3 if m == 0 else 1))
            dve.wait_ge(s_y_ready, c.at("yd"))
            link(dve.tensor_scalar(s_dx[:, m], s_xv[m % 2], vec[:, bass.ds(i * 8 + (VEC["s_D"] + 4 * par + m), 1)], None, MUL))
            dve.wait_ge(turn_done, c.next("turn"))
            for b in range(2):
                for hh in range(2):
                    head = bass.ds(i * 16 + (8 * par + 2 * m + hh), 1)
                    last = dve.tensor_scalar(s_xdt[:, b, m, 64 * hh:64 * hh + 64], bT[:, b * P + 64 * hh:b * P + 64 * hh + 64],
                                             s_tok[:, b, head], None, MUL)
            last.then_inc(turn_read, 1)

        def s_segments(i, par, m):
            dve.wait_ge(rows_done, c.next("rows"))
            for hh in range(2):
                bank = (bR, bS[1])[hh]
                for b in range(2):
                    head = bass.ds(i * 16 + (8 * par + 2 * m + hh), 1)
                    last = dve.tensor_scalar(s_e[:, hh, SEQ * b:SEQ + P * b], bank[:, P * b:SEQ], s_tok[:, 2 + b, head],
                                             0.0, SUB, MIN)
            last.then_inc(rows_read, 1)

        def s_scale_y(i, par):
            factor()
            for m in range(4):
                last = dve.scalar_tensor_tensor(s_y[:, m], s_y[:, m], vec[:, bass.ds(i * 8 + (VEC["s_norm_g"] + 4 * par + m), 1)],
                                                rsn[:, 2], MUL, MUL)
            last.then_inc(y_ready, 1)
            dve.wait_ge(y_ready, c.next("y"))

        def s_y_lo(par):
            dve.wait_ge(x_hi, c.next("x"))
            four = slice(4 * par, 4 * par + 4)
            dve.tensor_tensor(q_lo[:, four], s_y, q_hi[:, four], SUB).then_inc(x_lo, 1)

        def s_group(i, par, prev):
            for n in range(10):
                j = n - 2
                begin()
                g = take()
                dve.wait_ge(conved, c.at("conved"))
                dve.tensor_copy(s_xbp[:, n % 2, 3:3 + SEQ] if n < 6 else s_z[:, n - 6], g).then_inc(tile_taken, 1)
                lo_half(1)
                if 1 <= j <= 4:
                    if prev:
                        s_y_out(j - 1)
                    s_inputs(i, par, j - 1)
                if prev and 0 <= j <= 3:
                    s_segments(i, par - 1, j)
                if n < 6:
                    s_conv(i, par, n)
                if n == 7:
                    dve.wait_ge(cb_done, c.next("cb"))
                    dve.tensor_tensor(s_cb[:, 0:P], bS[0][:, 0:P], K("causal"), MUL)
                    dve.tensor_copy(s_cb[:, P:SEQ], bS[0][:, P:SEQ])
                    dve.tensor_tensor(s_cb[:, SEQ:384], bS[0][:, SEQ:384], K("causal"), MUL).then_inc(cb_read, 1)
                if prev and n == 8:
                    s_scale_y(i, par - 1)
                if prev and n == 9:
                    s_y_lo(1 - par)
            c.next("gluon", 4)
            dve.wait_ge(gluon, c.at("gluon"))

        def project_tile(n, gate):
            g = take()
            dve.scalar_tensor_tensor(h[:, n], g, gate, h[:, n], MUL, ADD).then_inc(tile_taken, 1)

        def s_project():
            dve.wait_ge(scaled_h, 1)
            for s in range(8):
                c.next("slot")
                for e in range(2):
                    n = 2 * s + e
                    project_tile(n, mod[:, 32 + n:33 + n])
                    lo_half(e)

        def layer_norm(w):
            dve.wait_ge(ln_done, c.next("mean"))
            for n in range(DT):
                dve.tensor_tensor(h[:, n], h[:, n], bR[:, 0:SEQ], SUB).then_inc(ln_go, 1)
            factor()
            with c.loop(dve, "ln", 0, 4) as i:
                for j in range(4):
                    n = i * 4 + j
                    link(dve.scalar_tensor_tensor(h[:, n], h[:, n], vec[:, bass.ds(i * 4 + (VEC["ln_g"] + w * DT + j), 1)],
                                                  rstd[:], MUL, MUL))
                    link(dve.tensor_scalar(h[:, n], h[:, n], vec[:, bass.ds(i * 4 + (VEC["ln_b"] + w * DT + j), 1)],
                                           None, ADD))
                    dve.sem_inc(ln_go, 1)

        def layer_s():
            c.k["turn"] = 2 * 3 * A_HEADS + 4 * B_PAIRS
            link(dve.tensor_scalar(mod[:, DT:3 * DT], mod[:, DT:3 * DT], 1.0, None, ADD))
            dve.tensor_scalar(mod[:, 4 * DT:6 * DT], mod[:, 4 * DT:6 * DT], 1.0, None, ADD).then_inc(mod_ready, 1)
            dve.wait_ge(mod_ready, 1)
            modulated((p_hi, p_lo), 0, "mod")
            link(dve.memset(s_xbp[:, :, 0:3], 0.0))
            begin()
            g = take()
            dve.tensor_scalar(s_dt[:], g, V("s_dt_bias"), None, ADD).then_inc(tile_taken, 1)
            lo_half(1)
            dve.wait_ge(tile_taken, c.at("tile"))
            c.next("soft")
            softplus(s_dt[:], s_y[:, 0], s_y[:, 1], s_y[:, 2], s_y[:, 3], s_dt[:])
            link(dve.tensor_scalar(s_y[:, 0], s_dt[:], tiny[:, 0:1], -1.0, MUL, MUL))
            link(dve.memset(s_y[:, 1], 1.0))
            dve.tensor_tensor_scan(s_ac[:], s_y[:, 1], s_y[:, 0], 0.0, MUL, ADD).then_inc(dt_ready, 1)
            dve.wait_ge(turn_done, c.next("turn"))
            dve.tensor_copy(s_tok.rearrange("p a b -> p (a b)"), bT[:]).then_inc(turn_read, 1)
            dve.wait_ge(turn_read, c.at("turn"))
            s_group(0, 0, False)
            s_group(0, 1, True)
            with c.loop(dve, "s_pairs", 1, S_PAIRS) as i:
                s_group(i, 0, True)
                s_project()
                s_group(i, 1, True)
            last = S_PAIRS
            s_segments(last, -1, 0)
            for m in range(4):
                s_y_out(m)
                if m < 3:
                    s_segments(last, -1, m + 1)
            s_scale_y(last, -1)
            s_y_lo(1)
            s_project()
            dve.wait_ge(tile_taken, c.at("tile"))
            layer_norm(0)

        def d_finish_scores(g, i, par):
            b = (bS[0], bS[1], bR)[g]
            dve.wait_ge(scored, c.next("scored"))
            dve.scalar_tensor_tensor(d_s[:, g], d_mat[:, g], con[:, bass.ds(i * 2 + (CON["slopes"] + 8 * g + par), 1)],
                                     b[:, 0:384], MUL, ADD).then_inc(score_read, 1)
            if g == 2:
                dve.wait_ge(score_read, c.at("scored"))
                dve.tensor_reduce(tiny[:, 4:5], d_s[:, :, 0:P], AX.XY, MAX, negate=True)
                link(dve.tensor_reduce(tiny[:, 5:6], d_s[:, :, P:384], AX.XY, MAX, negate=True))
                dve.tensor_scalar(tiny[:, 4:6], tiny[:, 4:6], P ** -0.5, None, MUL).then_inc(maxed, 1)

        def d_weigh():
            dve.wait_ge(exped, c.next("exped"))
            link(dve.reciprocal(tiny[:, 12:14], tiny[:, 8:10]))
            dve.tensor_scalar(d_s[:, :, 0:P], d_s[:, :, 0:P], tiny[:, 12:13], None, MUL)
            dve.tensor_scalar(d_s[:, :, P:384], d_s[:, :, P:384], tiny[:, 13:14], None, MUL).then_inc(weighted, 1)

        def d_finish():
            dve.wait_ge(gluon, c.next("gluon"))
            dve.wait_ge(mixed, c.next("mixed"))
            dve.tensor_tensor(rsn[:, 0], bO[:, 0:SEQ], d_gz[:], MUL).then_inc(y_ready, 1)
            dve.wait_ge(y_ready, c.next("y"))

        def d_y_lo(n):
            dve.wait_ge(x_hi, c.next("x"))
            dve.tensor_tensor(c_lo[:, n], rsn[:, 0], c_hi[:, n], SUB).then_inc(x_lo, 1)
            dve.wait_ge(x_lo, c.at("x"))

        def d_head(i, par, prev):
            dsts = [d_q[:, 0], d_q[:, 1], d_q[:, 2], d_k[:, 0], d_k[:, 1], d_k[:, 2],
                    d_v[:, 0], d_v[:, 1], d_v[:, 2], d_gz[:]]
            for n in range(10):
                begin()
                g = take()
                dve.tensor_copy(dsts[n], g).then_inc(tile_taken, 1)
                lo_half(1)
                if prev and n == 3:
                    d_finish()
                if prev and n == 4:
                    d_y_lo(i * 2 + (par - 1))
                if n in (4, 5, 6):
                    d_finish_scores(n - 4, i, par)
                if n == 7:
                    d_weigh()

        def layer_d():
            dve.wait_ge(d_in, 16)
            with c.loop(dve, "kv", 0, 4) as i:
                for j in range(4):
                    n = i * 4 + j
                    dve.wait_ge(x_hi, c.next("x"))
                    dve.tensor_tensor(p_lo[:, n], h[:, n], p_hi[:, n], SUB).then_inc(x_lo, 1)
            modulated((q_hi, q_lo), 48, "mod")
            d_head(0, 0, False)
            d_head(0, 1, True)
            with c.loop(dve, "d_pairs", 1, DIL_HEADS // 2) as i:
                d_head(i, 0, True)
                d_head(i, 1, True)
            d_finish()
            d_y_lo(DIL_HEADS - 1)
            dve.wait_ge(scaled_h, 2)
            with c.loop(dve, "d_out", 0, 2) as i:
                for s in range(4):
                    c.next("slot")
                    for e in range(2):
                        project_tile(i * 8 + (2 * s + e), mod[:, bass.ds(i * 8 + (80 + 2 * s + e), 1)])
                        lo_half(e)
            dve.wait_ge(tile_taken, c.at("tile"))
            layer_norm(1)

        dve.wait_ge(small_in, 48)
        ang, n_ = view(SEQ, SEQ), view(2 * SEQ, SEQ)
        link(dve.tensor_copy(ang, scratch[:, 0:SEQ].bitcast(I32)))
        c1 = 6.28125
        c2 = round((2 * math.pi - c1) * 2 ** 20) / 2 ** 20
        c3 = 2 * math.pi - c1 - c2
        big = 1.5 * 2 ** 23
        for dst, inv in ((sin_a, "inv_128"), (sin_b, "inv_64")):
            link(dve.tensor_scalar(dst[:], ang, K(inv), None, MUL))
            link(dve.tensor_scalar(n_, dst[:], 1 / (2 * math.pi), None, MUL))
            link(dve.tensor_scalar(n_, n_, big, None, ADD))
            link(dve.tensor_scalar(n_, n_, big, None, SUB))
            for cc in (c1, c2, c3):
                link(dve.scalar_tensor_tensor(dst[:], n_, -cc, dst[:], MUL, ADD))
            link(dve.tensor_scalar(dst[:], dst[:], -3.1415925, 3.1415925, MAX, MIN))
        for n, (a, b) in enumerate((("a_lq1", "a_lk1"), ("a_lq2", "a_lk2"))):
            last = dve.tensor_tensor(tiny[:, 2 * n:2 * n + 2], vec[:, VEC[a]:VEC[a] + 2], vec[:, VEC[b]:VEC[b] + 2], MUL)
        link(last)
        dve.sem_inc(trig_in, 1)
        dve.sem_inc(lam_in, 1)
        dve.wait_ge(trig_out, 2)
        for cos in (cos_a, cos_b):
            link(dve.tensor_tensor(cos[:], cos[:], cos[:], MUL))
            link(dve.tensor_scalar(cos[:], cos[:], -2.0, 1.0, MUL, ADD))
        b, cv = tiny[:, 48:64], vec[:, VEC["c_vec"]:VEC["c_vec"] + DT]
        dve.tensor_scalar(b, cv, SIG_MIN, None, MAX).then_inc(ada_in, 1)
        link(dve.memset(ada_hz[:, :, 1].bitcast(F32), 0.0))
        dve.wait_ge(ada_z, 1)
        dve.tensor_tensor(b, b, cv, MUL).then_inc(ada_in, 1)
        dve.wait_ge(ada_out, 1)
        link(dve.tensor_tensor(ada_hl[:, :, 1], b, ada_hl[:, :, 0], SUB))
        dve.wait_ge(lam_exp, 1)
        for n, layer in enumerate((0, 3)):
            init = 0.8 - 0.6 * math.exp(-0.3 * layer)
            link(dve.tensor_tensor(lam[:, n:n + 1], tiny[:, 6 + n:7 + n], tiny[:, 4 + n:5 + n], SUB))
            link(dve.tensor_scalar(lam[:, n:n + 1], lam[:, n:n + 1], init, None, SUB))
            link(dve.tensor_scalar(tiny[:, 16 + 2 * n:18 + 2 * n],
                                   vec[:, VEC["a_sub_norm"] + 2 * n:VEC["a_sub_norm"] + 2 * n + 2],
                                   1.0 - init, None, MUL))
        c.k["slot"] = 0
        for ahead in (1, 2):
            lo_half(0, ahead)
            lo_half(1, ahead)
        with c.loop(dve, "start", 0, 4) as i:
            for j in range(4):
                tail(i * 4 + j, (p_hi, p_lo), vec[:, bass.ds(i * 4 + (VEC["norm_gain"] + j), 1)])
        PQ = [(p_hi, p_lo), (q_hi, q_lo)]
        for layer in range(DEPTH):
            x, y = PQ[layer % 2], PQ[(layer + 1) % 2]
            if layer in (0, 3):
                layer_a(layer, x, y)
            elif layer == 1:
                layer_b(layer, x, y)
            else:
                layer_c(layer, x, y)
        layer_s()
        layer_d()
        dve.wait_ge(dve_step, c.at("dve"))
        dve.sem_inc(out_ready, 1)

    @block.gpsimd
    def _(pool):
        c = Steps(counts, "pool")

        def add_squares(j, n_first):
            pool.wait_ge(squared, c.next("sq"))
            if n_first:
                pool.wait_ge(norm_summed, c.at("model_norm"))
                pool.tensor_copy(acc[:], sq[:, j % 2]).then_inc(summed, 1)
            else:
                pool.wait_ge(summed, c.at("sq", -1))
                pool.tensor_tensor(acc[:], acc[:], sq[:, j % 2], ADD).then_inc(summed, 1)

        def sixteen_squares(norms_before):
            c.k["model_norm"] = norms_before
            add_squares(0, True)
            for j in range(1, 4):
                add_squares(j, False)
            with c.loop(pool, "squares", 1, 4):
                for j in range(4):
                    add_squares(j, False)

        def clamp(dst, src):
            pool.wait_ge(tile_taken, c.at("tile"))
            pool.sem_inc(pool_passed, 1)
            pool.tensor_scalar(dst, src, SIG_MIN, None, MAX).then_inc(clamped, 1)
            c.next("sig")

        def gates(last):
            for half in range(2):
                if half:
                    c.next("tile", 8)
                if last:
                    with c.loop(pool, "gates_last", 0, 2):
                        for j in range(4):
                            c.next("tile")
                            clamp(zg[:, j % 2], zg[:, j % 2])
                    continue
                for q in range(2):
                    for j in range(4):
                        c.next("tile")
                        clamp(zg[:, j % 2], zg[:, j % 2])
                        add_squares(j, half == 0 and q == 0 and j == 0)

        def out_and_gates(layer):
            sixteen_squares(c.k["norm"])
            c.next("tile", DT)
            c.next("norm")
            c.k["model_norm"] = c.k["norm"]
            gates(layer == DEPTH - 1)

        def a_head(prev):
            for j in range(8):
                c.next("tile")
                if j in (2, 3, 4, 5):
                    n = j - 2
                    pool.wait_ge(scaled, c.next("scaled"))
                    pool.tensor_tensor(t2[:, n % 2], qn[:, n % 2], cos_a[:], MUL).then_inc(cos_done, 1)
                if j in (6, 7):
                    clamp(zc[:, j - 6], gz[:, j - 6])
                if j % 2 == 0 or j in (3, 7):
                    c.next("tile")
            c.next("turn", 3 if prev else 2)

        def layer_a(layer):
            c.next("norm")
            a_head(False)
            with c.loop(pool, "a_heads", 1, A_HEADS):
                a_head(True)
            c.next("norm", 5 * A_HEADS)
            pool.wait_ge(turn_read, c.at("turn"))
            c.next("turn")
            pool.dma_start(p_raw, t["p"][layer]).then_inc(p_in, 16)
            c.next("tile", 8)
            out_and_gates(layer)

        def cosine(src):
            pool.tensor_tensor(b_t2, src, cos_b[:], MUL).then_inc(cos_done, 1)

        def b_pair(prev):
            pool.wait_ge(scaled, c.next("scaled", 3))
            cosine(bq[:, 2])
            c.next("scaled", 2)
            for s in range(2):
                c.next("tile", 12 if s == 0 else 2)
                clamp(b_zc[:, s], b_gz[:, s])
            c.next("tile")
            c.next("turn", 4 if prev else 2)

        def layer_b(layer):
            c.next("norm")
            c.next("tile", 9)
            pool.wait_ge(scaled, c.next("scaled"))
            cosine(b_cs[:, 0])
            b_pair(False)
            with c.loop(pool, "b_pairs", 1, B_PAIRS):
                b_pair(True)
            c.next("norm", 3 + 5 * B_PAIRS)
            pool.wait_ge(turn_read, c.at("turn"))
            c.next("turn", 2)
            pool.dma_start(p_raw, t["p"][layer]).then_inc(p_in, 16)
            c.next("tile", 8)
            out_and_gates(layer)

        def layer_c(layer):
            c.next("norm")
            c.next("tile", DT)
            for g in range(5):
                if g < 4:
                    c.next("tile", 8)
                for j in range(4 if g else 0):
                    c.next("tile")
                    clamp(c_zc, c_gz)
            pool.wait_ge(sig_ready, c.at("sig"))
            pool.dma_start(p_raw, t["p"][layer]).then_inc(p_in, 16)
            c.next("tile", 8)
            out_and_gates(layer)

        def s_silu(buf, sem_, value):
            pool.wait_ge(gluon, c.at("gluon"))
            pool.wait_ge(sem_, value)
            pool.sem_inc(pool_passed, 1)
            pool.tensor_scalar(s_zc, buf, SIG_MIN, None, MAX).then_inc(clamped, 1)
            c.next("gluon")
            pool.wait_ge(sig_ready, c.next("sig"))
            pool.tensor_tensor(buf, buf, s_zc, MUL).then_inc(gluon, 1)

        def s_mask_rows(i, par, m):
            pool.wait_ge(rows_done, c.at("rows"))
            pool.sem_inc(pool_passed, 1)
            for hh in range(2):
                one = con[0:64, bass.ds(i * 16 + (CON["ident"] + 8 * par + 2 * m + hh), 1)]
                last = pool.tensor_tensor(s_acm[hh][0:64], s_ac[0:64], one.to_broadcast([64, SEQ]), MUL)
            last.then_inc(masked, 1)
            c.next("rows")

        def s_weights():
            pool.wait_ge(decayed, c.next("decayed"))
            pool.wait_ge(cb_read, c.at("cb"))
            pool.tensor_tensor(s_e[:, 0], s_e[:, 0], s_cb, MUL)
            pool.tensor_tensor(s_e[:, 1], s_e[:, 1], s_cb, MUL).then_inc(m_ready, 1)

        def s_squares():
            pool.wait_ge(s_y_ready, c.next("s_y", 4))
            pool.wait_ge(norm_summed, c.at("norm"))
            for m in range(4):
                pool.tensor_tensor(acc[:] if m == 0 else rsn[:, 0], s_y[:, m], s_y[:, m], MUL).then_inc(pool_step, 1)
                pool.wait_ge(pool_step, c.next("step"))
                if m:
                    pool.tensor_tensor(acc[:], acc[:], rsn[:, 0], ADD).then_inc(s_sum if m == 3 else pool_step, 1)
                    if m < 3:
                        pool.wait_ge(pool_step, c.next("step"))
            c.next("norm")

        def s_group(i, par, prev):
            if prev:
                s_mask_rows(i, par - 1, 0)
            for n in range(10):
                j = n - 2
                c.next("tile")
                if prev and 0 <= j <= 3:
                    if j < 3:
                        s_mask_rows(i, par - 1, j + 1)
                    s_weights()
                if n < 6:
                    s_silu(s_bc[n] if n < 2 else s_xv[n % 2], conved, c.next("conved"))
                else:
                    s_silu(s_z[:, n - 6], tile_taken, c.at("tile"))
                if prev and n == 6:
                    s_squares()
            c.next("cb")

        def layer_s():
            pool.wait_ge(mod_x, 1)
            pool.tensor_scalar(h[:], h[:], DEEPNORM_ALPHA, None, MUL).then_inc(scaled_h, 1)
            c.next("tile")
            pool.wait_ge(dt_ready, 1)
            s_group(0, 0, False)
            s_group(0, 1, True)
            with c.loop(pool, "s_pairs", 1, S_PAIRS) as i:
                s_group(i, 0, True)
                c.next("tile", DT)
                s_group(i, 1, True)
            for m in range(4):
                if m == 0:
                    s_mask_rows(S_PAIRS, -1, 0)
                if m < 3:
                    s_mask_rows(S_PAIRS, -1, m + 1)
                s_weights()
            s_squares()
            c.next("tile", DT)
            c.next("norm")

        def layer_d():
            pool.wait_ge(norm_summed, c.at("norm"))
            pool.dma_start(d_mat.rearrange("p a b -> p (a b)"), t["distance"]).then_inc(d_in, 16)
            pool.wait_ge(mod_x, 2)
            pool.tensor_scalar(h[:], h[:], DEEPNORM_ALPHA, None, MUL).then_inc(scaled_h, 1)

            def head():
                c.next("tile", 10)
                s_gate()

            def s_gate():
                pool.wait_ge(tile_taken, c.at("tile"))
                pool.wait_ge(gluon, c.at("gluon"))
                pool.sem_inc(pool_passed, 1)
                pool.tensor_scalar(d_zc[:], d_gz[:], SIG_MIN, None, MAX).then_inc(clamped, 1)
                c.next("gluon")
                pool.wait_ge(sig_ready, c.next("sig"))
                pool.tensor_tensor(d_gz[:], d_gz[:], d_zc[:], MUL).then_inc(gluon, 1)
            head()
            with c.loop(pool, "d_heads", 1, DIL_HEADS):
                head()

        sixteen_squares(0)
        for layer in range(DEPTH):
            if layer in (0, 3):
                layer_a(layer)
            elif layer == 1:
                layer_b(layer)
            else:
                layer_c(layer)
        layer_s()
        layer_d()


def _blocks(w):
    k, n = w.shape
    return w.reshape(k // P, P, n // P, P).transpose(2, 0, 1, 3)


def _slots(blocks):
    n = blocks.shape[0]
    return blocks.reshape(n // SLOT, SLOT, P, P).transpose(0, 2, 1, 3).reshape(n // SLOT, P, SLOT * P)


def _square_slots(w):
    b = _blocks(w)
    return _slots(b.reshape(-1, P, P))


def _ple_slots(w_out, w_gate, w_proj):
    proj = _slots(_blocks(w_proj).reshape(-1, P, P))
    gate = _square_slots(w_gate)
    return [proj[0:1], _square_slots(w_out), gate[0:8], proj[1:2], gate[8:16]]


def _layout(i):
    slots = []
    ada = i["ada_w_2"].reshape(2, 2, 8, P, 24, SEQ).transpose(0, 4, 1, 3, 2, 5).reshape(96, P, SLOT * P)
    for layer in range(DEPTH):
        j = layer // 3
        if layer in (0, 3):
            b = _blocks(i["a_w_in"][j]).reshape(4, A_HEADS, 2, DT, P, P).transpose(1, 0, 2, 3, 4, 5)
            main = _slots(b.reshape(-1, P, P))
            mods = ada[64 * j:64 * j + 32]
            slots.append(np.stack([main[0::2], mods, main[1::2]], 1).reshape(-1, P, SLOT * P))
            slots += _ple_slots(i["a_w_out"][j], i["ple_w_gate"][layer], i["ple_w_proj"][layer])
        if layer == 1:
            w = i["b_w_in"][0]
            slots.append(_square_slots(w[:, 0:1024]))
            slots.append(_square_slots(np.concatenate([w[:, 1024:1088], w[:, 1024:1088]], 1)))
            gate = _square_slots(w[:, 1088:])
            uq = i["b_w_uq"][0].reshape(512, 2 * B_PAIRS, 192)
            uq = [_blocks(np.concatenate([uq[:, 2 * n, :P], uq[:, 2 * n + 1, :P], uq[:, 2 * n, P:], uq[:, 2 * n + 1, P:]], 1))
                  for n in range(B_PAIRS)]
            ukv = _blocks(i["b_w_ukv"][0]).reshape(B_PAIRS, SLOT, P, P)
            for n in range(B_PAIRS):
                pad = np.zeros((4, P, P), np.float32)
                four = [_slots(np.concatenate([uq[n].reshape(12, P, P), pad])), _slots(ukv[n]),
                        gate[2 * n:2 * n + 1], gate[2 * n + 1:2 * n + 2]]
                for m in range(4):
                    slots += [ada[32 + 4 * n + m:33 + 4 * n + m], four[m]]
            slots += _ple_slots(i["b_w_out"][0], i["ple_w_gate"][layer], i["ple_w_proj"][layer])
        if layer == 2:
            w = i["c_w_in"][0]
            slots.append(_square_slots(w[:, :D]))
            gate = _square_slots(w[:, D:])
            groups = [_blocks(i[n][0, g]).reshape(4, P, P) for g in range(C_GROUPS) for n in ("c_w_a", "c_w_x")]
            groups = _slots(np.concatenate(groups))
            for g in range(5):
                slots += [groups[g:g + 1]] * (g < 4) + [gate[4 * g - 4:4 * g]] * (g > 0)
            slots += _ple_slots(i["c_w_out"][0], i["ple_w_gate"][layer], i["ple_w_proj"][layer])
    w = _square_slots(i["a_in_w_2"][0][:, :10240])
    z, xs, b, cc = w[0:32], w[32:64], w[64:72], w[72:80]
    dt = i["a_in_w_2"][0][:, 10240:]
    slots.append(_square_slots(np.concatenate([dt, dt], 1)))
    out = _blocks(i["a_out_w_2"][0]).reshape(8, 2, S_PAIRS, 8, P, P).transpose(2, 0, 1, 3, 4, 5)
    out = _slots(out.reshape(-1, P, P)).reshape(S_PAIRS, 8, P, SLOT * P)
    for g in range(8):
        slots += [b[g:g + 1], cc[g:g + 1], xs[4 * g:4 * g + 4], z[4 * g:4 * g + 4]]
        if g and g % 2 == 0:
            slots.append(out[g // 2 - 1])
    slots.append(out[S_PAIRS - 1])
    w, kv = _square_slots(i["b_in_w_2"][0]), _square_slots(i["kv_w_2"])
    for n in range(DIL_HEADS):
        slots += [w[n:24:8], kv[n:24:8], kv[24 + n:48:8], w[24 + n:25 + n]]
    slots.append(_slots(_blocks(i["b_out_w_2"][0]).reshape(-1, P, P)))
    n = sum(len(s) for s in slots)
    slots.append(np.zeros((-(n + 2) % RAW + 2, P, SLOT * P), np.float32))
    return np.concatenate(slots)


def _cols(v, n):
    return np.ascontiguousarray(v.reshape(n, P).T)


def _vectors(i):
    two = lambda v: np.concatenate([v, v])
    f = {
        "norm_gain": _cols(i["norm_gain"], DEPTH * DT), "ple_norm": _cols(i["ple_norm"], DEPTH * DT),
        "a_q_norm": _cols(i["a_q_norm"], 2), "a_k_norm": _cols(i["a_k_norm"], 2),
        "a_lq1": _cols(i["a_lambda_q1"], 2), "a_lq2": _cols(i["a_lambda_q2"], 2),
        "a_lk1": _cols(i["a_lambda_k1"], 2), "a_lk2": _cols(i["a_lambda_k2"], 2),
        "a_sub_norm": _cols(i["a_sub_norm"], 4), "b_cq_norm": _cols(i["b_cq_norm"], 4),
        "b_ckv_norm": _cols(i["b_ckv_norm"], 4), "b_qn": _cols(i["b_q_nope_norm"], 1),
        "b_qr": _cols(two(i["b_q_rope_norm"][0]), 1), "b_kn": _cols(i["b_k_nope_norm"], 1),
        "b_kr": _cols(two(i["b_k_rope_norm"][0]), 1), "c_conv_w": _cols(i["c_conv_w"], 4 * DT),
        "c_conv_b": _cols(i["c_conv_b"], DT), "c_b_a": _cols(i["c_b_a"], DT), "c_b_x": _cols(i["c_b_x"], DT),
        "c_lambda": _cols(i["c_lambda"], DT), "c_vec": _cols(i["c_2"], DT), "ada_b": _cols(i["ada_b_2"], 96),
        "ln_g": _cols(i["ln_g_2"], 2 * DT), "ln_b": _cols(i["ln_b_2"], 2 * DT),
        "s_conv_w": _cols(i["a_conv_w_2"], 4 * 48), "s_conv_b": _cols(i["a_conv_b_2"], 48),
        "s_dt_bias": _cols(two(i["a_dt_bias_2"][0]), 1), "s_A_log": _cols(two(i["a_A_log_2"][0]), 1),
        "s_D": _cols(np.repeat(i["a_D_2"][0], 64), 32), "s_norm_g": _cols(i["a_norm_g_2"], 32),
    }
    return np.ascontiguousarray(np.concatenate([f[n] for n, _ in VEC_PARTS], 1))


def _constants():
    f = {"avg_model": np.full((P, P), 1 / D), "avg_512": np.full((P, P), 1 / 512),
         "avg_256": np.full((P, P), 1 / 256), "avg_128": np.full((P, P), 1 / 128),
         "avg_64": np.kron(np.eye(2), np.full((64, 64), 1 / 64)), "ones": np.ones((P, P)), "ident": np.eye(P)}

    def swap(half):
        m = np.zeros((P, P))
        for o in range(P):
            base, r = o // (2 * half) * 2 * half, o % (2 * half)
            m[base + (r + half) % (2 * half), o] = -1.0 if r < half else 1.0
        return m
    f["swap_128"], f["swap_64"] = swap(64), swap(32)
    q, k = np.arange(P)[:, None] // 64, np.arange(P)[None] // 64
    diag = np.where(k <= q, 0.0, NEG)
    f["mask"] = np.concatenate([diag, np.zeros((P, P)), diag], 1)
    inv = lambda half: (10000.0 ** (-(np.arange(P) % half) / half))[:, None]
    f["inv_128"], f["inv_64"] = inv(64), inv(32)
    f["eps_6"], f["eps_5"] = np.full((P, 1), 1e-6), np.full((P, 1), 1e-5)
    f["slopes"] = np.tile((2.0 ** (-8.0 * np.arange(1, 25) / 24))[None], (P, 1))
    f["causal"] = np.triu(np.ones((P, P)))
    return np.ascontiguousarray(np.concatenate([f[n] for n, _ in CONST_PARTS], 1).astype(np.float32))


def _distance():
    d = np.arange(SEQ)[:, None] - np.arange(SEQ)[None]
    out = []
    for window, dilation in ((128, 1), (512, 4), (2048, 16)):
        ok = (d >= 0) & (d <= window) & (d % dilation == 0)
        m = np.where(ok, -d * P ** 0.5, NEG)
        out.append(np.concatenate([m[:P, :P], m[P:]], 1))
    return np.ascontiguousarray(np.concatenate(out, 1).astype(np.float32))


def _features_first(a):
    s, d = a.shape
    return np.ascontiguousarray(a.T.reshape(d // P, P, s).transpose(1, 0, 2))


COUNTS = {
    ('sp', 'slots'): {'slot': 4},
    ('pe', 'a_heads'): {'slot': 12, 'tile': 14, 'norm': 5, 'sq_head': 4, 'scaled': 4, 'rot': 4, 'turn': 3, 'roped': 4, 'score_read': 2, 'weighted': 1, 'mixed': 1, 'mixed_read': 1},
    ('pe', 'outs'): {'slot': 4, 'tile': 4},
    ('pe', 'gates'): {'tile': 4, 'slot': 4},
    ('pe', 'b_pairs'): {'mixed': 1, 'turn': 4, 'rot': 1, 'roped': 1, 'norm': 5, 'tile': 15, 'weighted': 1, 'score_read': 2, 'scaled': 5, 'slot': 8, 'sq_head': 5},
    ('pe', 'c_in'): {'tile': 4, 'slot': 4},
    ('pe', 's_pairs'): {'turn': 8, 'norm': 2, 'tile': 36, 'x': 2, 'slot': 28, 'gluon': 20, 'cb': 2, 'rows': 8, 'yd': 8, 's_sum': 2},
    ('pe', 'd_pairs'): {'mixed': 2, 'score_read': 6, 'slot': 20, 'turn': 12, 'weighted': 2, 'tile': 20},
    ('pe', 'd_out'): {'slot': 4, 'tile': 8},
    ('act', 'start'): {'sum': 4},
    ('act', 'a_heads'): {'slot': 12, 'act': 9, 'norm': 5, 'half': 12, 'tile': 14, 'turn': 3, 'clamped': 2, 'sig': 2, 'maxed': 1, 'mixed': 1, 'y': 1},
    ('act', 'outs'): {'sum': 4, 'half': 4, 'slot': 4, 'tile': 4},
    ('act', 'gates'): {'act': 8, 'clamped': 4, 'half': 4, 'sig': 4, 'slot': 4, 'tile': 4, 'sum': 4, 'res': 4},
    ('act', 'b_pairs'): {'act': 9, 'y': 1, 'half': 6, 'sig': 2, 'slot': 8, 'turn': 4, 'clamped': 2, 'maxed': 1, 'norm': 5, 'tile': 15},
    ('act', 'c_in'): {'half': 4, 'slot': 4, 'tile': 4},
    ('act', 'gates_last'): {'act': 8, 'res': 4, 'half': 4, 'sig': 4, 'slot': 4, 'clamped': 4, 'tile': 4},
    ('act', 's_pairs'): {'act': 42, 'y': 2, 'half': 20, 'sig': 20, 'slot': 28, 'clamped': 20, 'norm': 2, 'tile': 36, 'rows': 8},
    ('act', 'd_pairs'): {'act': 4, 'y': 2, 'half': 20, 'sig': 2, 'slot': 20, 'turn': 12, 'clamped': 2, 'tile': 20, 'maxed': 2},
    ('act', 'd_out'): {'slot': 4, 'tile': 8},
    ('dve', 'start'): {'x': 4},
    ('dve', 'a_heads'): {'dve': 6, 'slot': 12, 'x': 1, 'tile': 14, 'norm': 5, 'scaled': 4, 'rot': 4, 'sig': 2, 'scored': 2, 'exped': 1, 'y': 1},
    ('dve', 'outs'): {'x': 4, 'slot': 4, 'tile': 4},
    ('dve', 'gates'): {'tile': 4, 'dve': 4, 'x': 4, 'sig': 4, 'slot': 4, 'res': 4},
    ('dve', 'b_pairs'): {'scored': 2, 'mixed': 1, 'rot': 1, 'y': 1, 'x': 1, 'sig': 2, 'slot': 8, 'exped': 1, 'norm': 5, 'dve': 2, 'scaled': 5, 'tile': 15},
    ('dve', 'c_in'): {'slot': 4, 'dve': 12, 'tile': 4},
    ('dve', 'gates_last'): {'res': 4, 'sig': 4, 'slot': 4, 'dve': 4, 'tile': 4},
    ('dve', 'mod'): {'x': 4, 'dve': 4},
    ('dve', 's_pairs'): {'y': 2, 'x': 2, 'slot': 28, 'turn': 8, 'norm': 2, 'dve': 52, 'tile': 36, 'conved': 12, 'gluon': 20, 'cb': 2, 'rows': 8, 'yd': 8},
    ('dve', 'ln'): {'dve': 8},
    ('dve', 'kv'): {'x': 4},
    ('dve', 'd_pairs'): {'scored': 6, 'mixed': 2, 'y': 2, 'x': 2, 'slot': 20, 'exped': 2, 'gluon': 2, 'dve': 4, 'tile': 20},
    ('dve', 'd_out'): {'slot': 4, 'tile': 8},
    ('pool', 'squares'): {'sq': 4},
    ('pool', 'a_heads'): {'tile': 14, 'scaled': 4, 'sig': 2, 'turn': 3},
    ('pool', 'b_pairs'): {'turn': 4, 'scaled': 5, 'sig': 2, 'tile': 15},
    ('pool', 'gates_last'): {'sig': 4, 'tile': 4},
    ('pool', 's_pairs'): {'norm': 2, 'sig': 20, 'tile': 36, 'conved': 12, 'gluon': 20, 'cb': 2, 'rows': 8, 'decayed': 8, 's_y': 8, 'step': 12},
    ('pool', 'd_heads'): {'sig': 1, 'gluon': 1, 'tile': 10},
}


def kernel(**inputs):
    import concourse.bacc as _bacc
    from concourse.bass_utils import run_bass_kernel_spmd as _run
    i = {k: np.asarray(v) for k, v in inputs.items()}
    arrays = {
        "slots": _layout(i), "vecs": _vectors(i), "consts": _constants(),
        "positions": np.ascontiguousarray(i["positions"].reshape(1, SEQ).astype(np.int32)),
        "x": _features_first(i["x"][0]),
        "p": np.stack([_features_first(i["p"][n, 0]) for n in range(DEPTH)]),
        "distance": _distance(),
    }
    nc = _bacc.Bacc("TRN2", target_bir_lowering=False, num_devices=1)
    t = {n: nc.dram_tensor(f"in_{n}", a.shape, mybir.dt.from_np(a.dtype), kind="ExternalInput").ap()
         for n, a in arrays.items()}
    t["out"] = nc.dram_tensor("out_h", (P, DT, SEQ), F32, kind="ExternalOutput").ap()
    program(nc, t, COUNTS)
    r = _run(nc, [{f"in_{n}": a for n, a in arrays.items()}], core_ids=[0])
    o = r.results[0]["out_h"]
    return np.ascontiguousarray(o.transpose(2, 1, 0).reshape(1, SEQ, D))
```

```python
from contextlib import ExitStack, contextmanager
import math

import numpy as np
import concourse.bass as bass
from concourse import mybir

F32 = mybir.dt.float32
F32R = mybir.dt.float32r
I32 = mybir.dt.int32
ALU = mybir.AluOpType
ACT = mybir.ActivationFunctionType
AX = mybir.AxisListType
MUL, ADD, SUB, MAX, MIN = ALU.mult, ALU.add, ALU.subtract, ALU.max, ALU.min

P = 128
SEQ = 256
D = 2048
DT = D // P
DEPTH = 4
SLOT = 16
HALF = SLOT // 2 * P
RAW, SPLIT = 4, 2
A_HEADS = 8
B_PAIRS = 8
C_GROUPS = 8
S_GROUPS = 8
S_PAIRS = 4
DIL_HEADS = 8
NEG = -1.0e30
DEEPNORM_ALPHA = 4 ** 0.25
SIG_MIN = -43.0

VEC_PARTS = [("norm_gain", DEPTH * DT), ("ple_norm", DEPTH * DT),
             ("a_q_norm", 2), ("a_k_norm", 2), ("a_lq1", 2), ("a_lq2", 2), ("a_lk1", 2), ("a_lk2", 2),
             ("a_sub_norm", 4), ("b_cq_norm", 4), ("b_ckv_norm", 4), ("b_qn", 1), ("b_qr", 1),
             ("b_kn", 1), ("b_kr", 1), ("c_conv_w", 4 * DT), ("c_conv_b", DT), ("c_b_a", DT),
             ("c_b_x", DT), ("c_lambda", DT), ("c_vec", DT), ("ada_b", 96), ("ln_g", 2 * DT),
             ("ln_b", 2 * DT), ("s_conv_w", 4 * 48), ("s_conv_b", 48), ("s_dt_bias", 1),
             ("s_A_log", 1), ("s_D", 32), ("s_norm_g", 32)]
VEC = {}
_at = 0
for _name, _n in VEC_PARTS:
    VEC[_name] = _at
    _at += _n
NVEC = _at

CONST_PARTS = [("avg_model", P), ("avg_512", P), ("avg_256", P), ("avg_128", P), ("avg_64", P),
               ("ones", P), ("ident", P), ("swap_128", P), ("swap_64", P), ("mask", 3 * P), ("causal", P), ("pick", 64),
               ("inv_128", 1), ("inv_64", 1), ("eps_6", 1), ("eps_5", 1), ("slopes", 24)]
CON = {}
_at = 0
for _name, _n in CONST_PARTS:
    CON[_name] = _at
    _at += _n
NCON = _at



class Steps:

    def __init__(self, counts, who):
        self.k, self.i, self.per, self.bank = {}, None, {}, 0
        self.counts, self.who = counts, who

    def at(self, name, more=0):
        k = self.k.get(name, 0) + more
        n = self.per.get(name, 0)
        if self.i is None or n == 0:
            return max(k, 0)
        return self.i * n + k

    def next(self, name, n=1):
        self.k[name] = self.k.get(name, 0) + n
        return self.at(name)

    def fours(self, name, more):
        k = (self.k.get(name, 0) + more) // 4
        n = self.per.get(name, 0)
        return k + 1 if self.i is None or n == 0 else self.i * (n // 4) + (k + 1)

    @contextmanager
    def loop(self, eng, name, first, last):
        per = self.counts.get((self.who, name), {})
        start = dict(self.k)
        with eng.Fori(first, last) as i:
            self.i, self.per = i, per
            for n, v in per.items():
                self.k[n] = self.k.get(n, 0) - first * v
            inside = dict(self.k)
            yield i
            seen = {n: v - inside.get(n, 0) for n, v in self.k.items() if v != inside.get(n, 0)}
        self.i, self.per = None, {}
        assert seen == per, (self.who, name, seen)
        self.k = {n: start.get(n, 0) + (last - first) * seen.get(n, 0) for n in set(start) | set(seen)}


def program(nc, t, counts):
    ctx = ExitStack()
    with ctx:
        _program(nc, ctx, t, counts)


def _program(nc, ctx, t, counts):
    def sb(name, shape, dt=F32):
        return ctx.enter_context(nc.sbuf_tensor(name, shape, dt))

    def sem(name):
        return ctx.enter_context(nc.semaphore(name))

    h = sb("h", [P, DT, SEQ])
    raw = [sb(f"w_raw{n}", [P, SLOT * P]) for n in range(RAW)]
    w_hi = [sb(f"w_hi{n}", [P, SLOT * P], F32R) for n in range(SPLIT)]
    w_lo = [sb(f"w_lo{n}", [P, SLOT * P], F32R) for n in range(SPLIT)]
    p_hi, p_lo = sb("p_hi", [P, DT, SEQ], F32R), sb("p_lo", [P, DT, SEQ], F32R)
    q_hi, q_lo = sb("q_hi", [P, DT, SEQ], F32R), sb("q_lo", [P, DT, SEQ], F32R)
    c_hi, c_lo = sb("c_hi", [P, 8, SEQ], F32R), sb("c_lo", [P, 8, SEQ], F32R)
    vec = sb("vec", [P, NVEC])
    con = sb("con", [P, NCON])
    cos_a, sin_a = sb("cos_a", [P, SEQ]), sb("sin_a", [P, SEQ])
    cos_b, sin_b = sb("cos_b", [P, SEQ]), sb("sin_b", [P, SEQ])
    rstd = sb("rstd", [P, SEQ])
    acc = sb("acc", [P, SEQ])
    sq = sb("sq", [P, 2, SEQ])
    rsn = sb("rsn", [P, 3, SEQ])
    tiny = sb("tiny", [P, 64])
    lam = sb("lam", [P, 2])
    sp8 = tiny[:, 32:32 + DT]
    ada_hl = sb("ada_hl", [P, DT, 2], F32R)
    ada_hz = sb("ada_hz", [P, DT, 2], F32R)
    mod = sb("mod", [P, 96])
    scratch = sb("scratch", [P, (nc.sbuf_bytes_remaining - 64) // 4 // 8 * 8])

    def view(at, *shape):
        n = int(np.prod(shape))
        assert at + n <= scratch.shape[1], (at + n, scratch.shape)
        v = scratch[:, at:at + n]
        if len(shape) == 2:
            v = v.rearrange("p (a b) -> p a b", a=shape[0])
        if len(shape) == 3:
            v = v.rearrange("p (a b c) -> p a b c", a=shape[0], b=shape[1])
        return v

    G = [ctx.enter_context(nc.psum_tensor(f"g{n}", [P, 512], F32)) for n in range(2)]
    bN = ctx.enter_context(nc.psum_tensor("norm_bank", [P, 512], F32))
    bR = ctx.enter_context(nc.psum_tensor("rope_bank", [P, 512], F32))
    bT = ctx.enter_context(nc.psum_tensor("turn_bank", [P, 512], F32))
    bS = [ctx.enter_context(nc.psum_tensor(f"score_bank{n}", [P, 512], F32)) for n in range(2)]
    bO = ctx.enter_context(nc.psum_tensor("out_bank", [P, 512], F32))

    small_in = sem("small_in")
    h_in = sem("h_in")
    p_in = sem("p_in")
    landed = [sem(f"landed{n}") for n in range(RAW)]
    hi_ready, lo_ready = sem("hi_ready"), sem("lo_ready")
    half_used = sem("half_used")
    tile_done, tile_taken = sem("tile_done"), sem("tile_taken")
    x_hi, x_lo = sem("x_hi"), sem("x_lo")
    res_ready = sem("res_ready")
    squared, summed = sem("squared"), sem("summed")
    norm_summed, factor_ready = sem("norm_summed"), sem("factor_ready")
    rot_done, rot_read = sem("rot_done"), sem("rot_read")
    scaled, cos_done, roped = sem("scaled"), sem("cos_done"), sem("roped")
    turn_done, turn_read = sem("turn_done"), sem("turn_read")
    scored, score_read, maxed, exped = sem("scored"), sem("score_read"), sem("maxed"), sem("exped")
    weighted, mixed, mixed_read, y_ready = sem("weighted"), sem("mixed"), sem("mixed_read"), sem("y_ready")
    clamped, sig_ready = sem("clamped"), sem("sig_ready")
    trig_in, trig_out = sem("trig_in"), sem("trig_out")
    lam_in, lam_sum, lam_exp = sem("lam_in"), sem("lam_sum"), sem("lam_exp")
    p_ready, p_hi_ready = sem("p_ready"), sem("p_hi_ready")
    sq_head = sem("sq_head")
    dve_step, act_step = sem("dve_step"), sem("act_step")
    act_passed, pool_passed = sem("act_passed"), sem("pool_passed")
    soft_in, soft_out = sem("soft_in"), sem("soft_out")
    gates_out, chain_in, chain_out = sem("gates_out"), sem("chain_in"), sem("chain_out")
    gated, conv_done = sem("gated"), sem("conv_done")
    ada_in, ada_z, ada_out, mod_ready = sem("ada_in"), sem("ada_z"), sem("ada_out"), sem("mod_ready")
    dt_ready = sem("dt_ready")
    masked, rows_done, rows_read, decayed = sem("masked"), sem("rows_done"), sem("rows_read"), sem("decayed")
    m_ready, yd_done, s_y_ready, s_sq = sem("m_ready"), sem("yd_done"), sem("s_y_ready"), sem("s_sq")
    s_sum, cb_done, cb_read, gluon = sem("s_sum"), sem("cb_done"), sem("cb_read"), sem("gluon")
    scaled_h = sem("scaled_h")
    ln_done, ln_go, ln_sq, mod_x = sem("ln_done"), sem("ln_go"), sem("ln_sq"), sem("mod_x")
    d_in = sem("d_in")
    out_ready, stored = sem("out_ready"), sem("stored")

    def K(name, n=None, rows=P):
        a = CON[name]
        w = dict(CONST_PARTS)[name] if n is None else n
        return con[0:rows, a:a + w]

    def V(name, j=0):
        a = VEC[name]
        return vec[:, a + j:a + j + 1]

    at = 0
    qs = view(at, 3, SEQ); at += 3 * SEQ
    sqh = view(at, 2, SEQ); at += 2 * SEQ
    qn = view(at, 2, SEQ); at += 2 * SEQ
    qr = view(at, 4, SEQ); at += 4 * SEQ
    t2 = view(at, 2, SEQ); at += 2 * SEQ
    vs = view(at, 2, SEQ); at += 2 * SEQ
    vtok = view(at, 2, 256); at += 512
    gz = view(at, 2, SEQ); at += 2 * SEQ
    zc = view(at, 2, SEQ); at += 2 * SEQ
    sm = view(at, 2, 384); at += 768
    pt = sm[:, 1]
    yo = view(at, 512); at += 512
    proj = view(0, 8, SEQ)
    zg = view(8 * SEQ, 2, SEQ)
    sg = view(10 * SEQ, 2, SEQ)
    p_raw = view(13 * SEQ, 2, SEQ)

    bq = view(0, 3, SEQ)
    bk = view(3 * SEQ, 2, SEQ)
    bv = view(5 * SEQ, 2, SEQ)
    bsk = view(7 * SEQ, 2, SEQ)
    b_pe = view(9 * SEQ, SEQ)
    b_t2 = view(10 * SEQ, SEQ)
    b_kpe = view(11 * SEQ, SEQ)
    bsq = view(12 * SEQ, 3, SEQ)
    b_yo = view(12 * SEQ, 512)
    b_sm = view(15 * SEQ, 2, 384)
    b_vtok = view(15 * SEQ + 768, 2, 2, P)
    b_gz = view(15 * SEQ + 1280, 2, SEQ)
    b_zc = view(15 * SEQ + 1792, 2, SEQ)
    b_rq, b_rkv = view(24 * SEQ, SEQ), view(25 * SEQ, SEQ)
    b_cs = view(0, 2, SEQ)
    b_csq = view(15 * SEQ, 8, SEQ)

    xc = view(0, DT, SEQ)
    xbp = rsn.rearrange("p a b -> p (a b)")[:, 0:528].rearrange("p (a b) -> p a b", a=2)
    rg = view(DT * SEQ, 4, SEQ)
    ig = view(20 * SEQ, 4, SEQ)
    c_gz, c_zc = view(24 * SEQ, 2, SEQ), rsn
    soft = view(25 * SEQ, 3, DT)

    s_dx = view(0, 4, SEQ)
    s_z = view(4 * SEQ, 4, SEQ)
    s_y = view(8 * SEQ, 4, SEQ)
    s_xdt = view(12 * SEQ, 2, 4, P)
    s_cb = view(16 * SEQ, 384)
    s_tok = view(16 * SEQ + 384, 4, P)
    s_xbp = view(18 * SEQ + 384, 2, 264)
    s_e = view(20 * SEQ + 400, 2, 384)
    s_zc = [view(23 * SEQ + 400, SEQ), sin_b[:]]
    s_ac, s_dt = cos_a, sin_a
    s_acm = [cos_b[0:64], cos_b[64:P]]
    s_bc = [sq[:, 0], sq[:, 1]]
    s_xv = [rstd[:], vec[:, 0:SEQ]]
    ln_c = view(0, DT, SEQ)
    d_q, d_k, d_v = view(0, 3, SEQ), view(3 * SEQ, 3, SEQ), view(6 * SEQ, 3, SEQ)
    d_vtok = view(9 * SEQ, 3, 2, P)
    d_s = view(12 * SEQ, 3, 384)
    d_mat = view(12 * SEQ + 1152, 3, 384)
    d_gz, d_zc = cos_a, sin_a

    block = ctx.enter_context(nc.Block())

    @block.sync
    def _(sp):
        c = Steps(counts, "sp")
        sp.dma_start(vec[:], t["vecs"]).then_inc(small_in, 16)
        sp.dma_start(con[:], t["consts"]).then_inc(small_in, 16)
        sp.dma_start(scratch[:, 0:SEQ].bitcast(I32), t["positions"].to_broadcast([P, SEQ])).then_inc(small_in, 16)
        sp.dma_start(h[:], t["x"]).then_inc(h_in, 16)
        n_slots = t["slots"].shape[0]
        for s in range(RAW):
            sp.dma_start(raw[s][:], t["slots"][s]).then_inc(landed[s], 16)
        c.k["slot"] = RAW
        with c.loop(sp, "slots", 1, n_slots // RAW) as i:
            for s in range(RAW):
                sp.wait_ge(lo_ready, c.at("slot", -RAW + 1) * 2)
                sp.dma_start(raw[s][:], t["slots"][i * RAW + s]).then_inc(landed[s], 16)
                c.next("slot")
        sp.wait_ge(out_ready, 1)
        sp.dma_start(t["out"], h[:]).then_inc(stored, 16)
        sp.wait_ge(stored, 16)

    @block.tensor
    def _(pe):
        c = Steps(counts, "pe")

        def slot():
            c.next("slot")
            pe.wait_ge(lo_ready, c.at("slot") * 2 + -1)
            return (c.k["slot"] - 1) % SPLIT

        def second_half():
            pe.wait_ge(lo_ready, c.at("slot") * 2)

        def tile(w, blocks, hi, lo, ks, fresh=False, arriving=0):
            pe.wait_ge(tile_taken, c.at("tile", 0 if fresh else -1))
            g = G[c.bank][:, 0:SEQ]
            c.bank ^= 1
            for n, (b, k) in enumerate(zip(blocks, ks)):
                if b == SLOT // 2:
                    second_half()
                if arriving == DT or arriving == 1 and n in (0, len(ks) - 2):
                    pe.wait_ge(x_lo, c.next("x") if arriving == DT else c.at("x", -1 if n == 0 else 0))
                wh, wl = w_hi[w][:, b * P:(b + 1) * P], w_lo[w][:, b * P:(b + 1) * P]
                pe.matmul(g, wh, hi[:, k], start=n == 0, stop=False)
                pe.matmul(g, wh, lo[:, k], start=False, stop=False)
                last = pe.matmul(g, wl, hi[:, k], start=False, stop=n == len(ks) - 1)
                if b == SLOT // 2 - 1 and len(ks) == SLOT:
                    last.then_inc(half_used, 1)
            last.then_inc(tile_done, 1)
            c.next("tile")

        def norm(mats, srcs, need, value):
            pe.wait_ge(factor_ready, c.at("norm"))
            pe.wait_ge(need, value)
            for n, s in enumerate(srcs):
                last = pe.matmul(bN[:, 0:SEQ], mats, s, start=n == 0, stop=n == len(srcs) - 1)
            last.then_inc(norm_summed, 1)
            c.next("norm")

        def norm_pair(mats, srcs):
            pe.wait_ge(factor_ready, c.at("norm"))
            pe.wait_ge(sq_head, c.next("sq_head", 2))
            for n, s in enumerate(srcs):
                last = pe.matmul(bN[:, n * SEQ:(n + 1) * SEQ], mats, s, start=True, stop=True)
            last.then_inc(norm_summed, 1)
            c.next("norm")

        def model_norm():
            norm(K("avg_model"), [acc[:]], summed, c.next("sum", DT))

        def rotate(buf, swap, n=1):
            pe.wait_ge(rot_read, c.at("rot"))
            pe.wait_ge(scaled, c.next("scaled", n))
            pe.matmul(bR[:, 0:SEQ], swap, buf, start=True, stop=True).then_inc(rot_done, 1)
            c.next("rot")

        def turn(srcs, need, value):
            pe.wait_ge(turn_read, c.at("turn"))
            pe.wait_ge(need, value)
            for n, s in enumerate(srcs):
                last = pe.transpose(bT[:, n * P:(n + 1) * P], s, K("ident"))
            last.then_inc(turn_done, 1)
            c.next("turn")

        def square_tiles(hi, lo, arriving=0):
            w = slot()
            tile(w, range(SLOT), hi, lo, range(SLOT), arriving=arriving)

        def mod_slot(m, fresh=False):
            w = slot()
            pe.wait_ge(tile_taken, c.at("tile", 0 if fresh else -1))
            g = G[c.bank][0:2, 0:SEQ]
            c.bank ^= 1
            for b in range(8):
                if b == 4:
                    second_half()
                k = 8 * (m % 2) + b
                cols = slice(b * SEQ, (b + 1) * SEQ)
                pe.matmul(g, ada_hl[:, k], w_hi[w][:, cols], start=b == 0, stop=False)
                last = pe.matmul(g, ada_hz[:, k], w_lo[w][:, cols], start=False, stop=b == 7)
                if b == 3:
                    last.then_inc(half_used, 1)
            last.then_inc(tile_done, 1)
            c.next("tile")

        def mod_columns():
            pe.wait_ge(tile_taken, c.at("tile"))
            g = G[c.bank]
            c.bank ^= 1
            for e in range(2):
                last = pe.matmul(g[:, e:e + 1], acc[0:2, e * P:(e + 1) * P], K("ones", 1, rows=2), start=True, stop=True)
            last.then_inc(tile_done, 1)
            c.next("tile")

        def proj_slot(fresh=False):
            w = slot()
            pe.wait_ge(p_ready, c.at("p"))
            for n in range(8):
                tile(w, [2 * n, 2 * n + 1], c_hi, c_lo, [0, 1], fresh=fresh and n == 0)

        def gates(hi, lo):
            for n in range(8):
                square_tiles(hi, lo, arriving=DT if n == 0 else 0)
                if n == 0:
                    model_norm()
            proj_slot()
            with c.loop(pe, "gates", 0, 2):
                for _ in range(4):
                    square_tiles(hi, lo)

        def out_and_gates(y, x):
            for n in range(4):
                square_tiles(*y, arriving=1 if n == 0 else 0)
            with c.loop(pe, "outs", 1, 4):
                for _ in range(4):
                    square_tiles(*y)
            gates(*x)

        def a_turn_weights():
            turn([sm[:, 0, 0:P], sm[:, 0, P:2 * P], sm[:, 0, 2 * P:3 * P]], weighted, c.next("weighted"))

        def a_mix():
            pe.wait_ge(turn_read, c.at("turn"))
            pe.wait_ge(y_ready, c.at("mixed"))
            for e in range(2):
                o = bO[:, e * SEQ:(e + 1) * SEQ]
                pe.matmul(o, vtok[:, 0, e * P:(e + 1) * P], pt[:, 0:SEQ], start=True, stop=False)
                last = pe.matmul(o[:, P:SEQ], vtok[:, 1, e * P:(e + 1) * P], pt[:, SEQ:SEQ + P],
                                 start=False, stop=True)
            last.then_inc(mixed, 1)
            c.next("mixed")

        def a_norm_out():
            norm(K("avg_256"), [yo[:, 0:SEQ], yo[:, SEQ:512]], mixed_read, c.next("mixed_read"))

        def a_head(hi, lo, prev, first):
            for j in range(8):
                square_tiles(hi, lo, arriving=DT if first and j == 0 else 0)
                if first and j == 0:
                    model_norm()
                if j in (1, 2, 3, 4):
                    norm(K("avg_128"), [sqh[:, (j - 1) % 2]], sq_head, c.next("sq_head"))
                if j == 1 and prev:
                    a_turn_weights()
                if j == 2 and prev:
                    a_mix()
                if j == 3 and prev:
                    a_norm_out()
                if j in (3, 4, 5, 6):
                    rotate(qn[:, (j - 3) % 2], K("swap_128"))
                if j in (5, 6):
                    turn([vs[:, j - 5, 0:P], vs[:, j - 5, P:SEQ]], tile_taken, c.at("tile", -1))
                if j == 7:
                    pe.wait_ge(roped, c.next("roped", 4))
                    pe.wait_ge(score_read, c.at("score_read"))
                    for s in range(2):
                        q, k = qr[:, s], qr[:, 2 + s]
                        pe.matmul(bS[s][:, 0:P], q[:, 0:P], k[:, 0:P], start=True, stop=True)
                        pe.matmul(bS[s][:, P:3 * P], q[:, P:SEQ], k, start=True, stop=True).then_inc(scored, 1)
                    c.next("score_read", 2)
                if j % 2 == 0:
                    mod_slot(j // 2)
                if j in (3, 7):
                    mod_columns()

        def layer_a(x, y):
            hi, lo = x
            a_head(hi, lo, False, True)
            with c.loop(pe, "a_heads", 1, A_HEADS):
                a_head(hi, lo, True, False)
            c.next("p")
            proj_slot()
            a_turn_weights()
            a_mix()
            a_norm_out()
            c.next("x", A_HEADS)
            out_and_gates(y, x)

        def b_pair(hi, lo, prev):
            c.bank = 0
            mod_slot(0, fresh=True)
            w = slot()
            for n in range(3):
                tile(w, range(4 * n, 4 * n + 4), c_hi, c_lo, range(4))
            mod_slot(1)
            if prev:
                b_turn_weights()
            norm_pair(K("avg_128"), [bsq[:, 0], bsq[:, 1]])
            w = slot()
            for n in range(4):
                tile(w, range(4 * n, 4 * n + 4), c_hi, c_lo, range(4, 8))
            norm(K("avg_64"), [bsq[:, 2]], sq_head, c.next("sq_head"))
            if prev:
                b_mix()
            mod_columns()
            mod_slot(2)
            rotate(bq[:, 2], K("swap_64"), 3)
            norm_pair(K("avg_128"), [bsk[:, 0], bsk[:, 1]])
            square_tiles(hi, lo)
            turn([bv[:, s, n * P:(n + 1) * P] for s in range(2) for n in range(2)], tile_taken, c.at("tile", -1))
            mod_slot(3)
            square_tiles(hi, lo)
            mod_columns()
            pe.wait_ge(roped, c.next("roped"))
            pe.wait_ge(scaled, c.next("scaled", 2))
            pe.wait_ge(score_read, c.at("score_read"))
            for s in range(2):
                r = slice(64 * s, 64 * s + 64)
                for u, v, w_ in ((0, P, P), (P, 3 * P, SEQ)):
                    q = slice(u, u + P)
                    pe.matmul(bS[s][:, u:v], bq[:, s, q], bk[:, s, 0:w_], start=True, stop=False)
                    last = pe.matmul(bS[s][:, u:v], b_pe[r, q], b_kpe[r, 0:w_], start=False, stop=True)
                last.then_inc(scored, 1)
            c.next("score_read", 2)

        def b_turn_weights():
            turn([b_sm[:, 0, n * P:(n + 1) * P] for n in range(3)], weighted, c.next("weighted"))
            pe.wait_ge(rot_read, c.at("rot"))
            for n in range(3):
                last = pe.transpose(bR[:, n * P:(n + 1) * P], b_sm[:, 1, n * P:(n + 1) * P], K("ident"))
            last.then_inc(turn_done, 1)
            c.next("turn")

        def b_mix():
            pe.wait_ge(turn_read, c.at("turn"))
            pe.wait_ge(y_ready, c.at("mixed"))
            for s in range(2):
                o = bO[:, s * SEQ:(s + 1) * SEQ]
                pe.matmul(o, b_vtok[:, s, 0], b_sm[:, s, 0:SEQ], start=True, stop=False)
                last = pe.matmul(o[:, P:SEQ], b_vtok[:, s, 1], b_sm[:, s, SEQ:SEQ + P], start=False, stop=True)
            last.then_inc(mixed, 1)
            c.next("mixed")

        def layer_b(x, y):
            hi, lo = x
            for n in range(9):
                square_tiles(hi, lo, arriving=DT if n == 0 else 0)
                if n == 0:
                    model_norm()
                if n in (4, 8):
                    c.next("sq_head", 4)
                    norm(K("avg_512"), [b_csq[:, n - 4 + m] for m in range(4)], sq_head, c.k["sq_head"])
            norm(K("avg_64"), [bsq[:, 0]], sq_head, c.next("sq_head"))
            rotate(b_cs[:, 0], K("swap_64"))
            c.next("roped")
            pe.wait_ge(x_lo, c.next("x", 8))
            b_pair(hi, lo, False)
            with c.loop(pe, "b_pairs", 1, B_PAIRS):
                b_pair(hi, lo, True)
            c.bank = 0
            c.next("p")
            proj_slot(fresh=True)
            b_turn_weights()
            b_mix()
            c.next("x", B_PAIRS)
            out_and_gates(y, x)

        def layer_c(x, y):
            for n in range(4):
                square_tiles(*x, arriving=DT if n == 0 else 0)
                if n == 0:
                    model_norm()
            with c.loop(pe, "c_in", 1, 3):
                for _ in range(4):
                    square_tiles(*x)
            for g in range(5):
                if g < 4:
                    w = slot()
                    pe.wait_ge(x_lo, c.next("x", 5 if g == 3 else 1))
                    for n in range(8):
                        k = 4 * (g % 2) + 2 * (n // 4)
                        tile(w, [2 * n, 2 * n + 1], c_hi, c_lo, [k, k + 1])
                for _ in range(4):
                    square_tiles(*x)
            c.next("p")
            proj_slot()
            c.next("x", DT - 4)
            out_and_gates(y, x)

        def s_rows(m):
            pe.wait_ge(masked, c.next("rows"))
            pe.wait_ge(rows_read, c.at("rows", -1))
            ones = K("ones")
            pe.matmul(bR[:, 0:SEQ], ones[0:64], s_acm[0], start=True, stop=True)
            pe.matmul(bS[1][:, 0:SEQ], ones[64:P], s_acm[1], start=True, stop=True).then_inc(rows_done, 1)

        def s_out(m):
            pe.wait_ge(m_ready, c.next("yd"))
            pe.wait_ge(turn_read, c.at("turn"))
            pe.wait_ge(s_y_ready, c.at("yd", -1))
            for hh in range(2):
                r = slice(64 * hh, 64 * hh + 64)
                o = bO[r, 0:SEQ]
                pe.matmul(o, s_xdt[:, 0, m, r], s_e[:, hh, 0:SEQ], start=True, stop=False)
                last = pe.matmul(o[:, P:SEQ], s_xdt[:, 1, m, r], s_e[:, hh, SEQ:384], start=False, stop=True)
            last.then_inc(yd_done, 1)

        def s_norm():
            norm(K("avg_512"), [acc[:]], s_sum, c.next("s_sum", 4))

        def s_group(prev):
            for n in range(10):
                j = n - 2
                square_tiles(p_hi, p_lo)
                if prev and 1 <= j <= 4:
                    s_out(j - 1)
                if prev and 0 <= j <= 3:
                    s_rows(j)
                if 2 <= j <= 5:
                    x = s_xv[j % 2]
                    turn([x[:, 0:P], x[:, P:SEQ]], gluon, c.next("gluon", 3 if j == 2 else 1))
                if j == 5:
                    pe.wait_ge(cb_read, c.at("cb"))
                    b, q = s_bc
                    pe.matmul(bS[0][:, 0:SEQ], b[:, 0:P], q, start=True, stop=True)
                    pe.matmul(bS[0][:, SEQ:384], b[:, P:SEQ], q[:, P:SEQ], start=True, stop=True).then_inc(cb_done, 1)
                    c.next("cb")
                    if prev:
                        s_norm()
            c.next("gluon", 4)

        def s_project():
            pe.wait_ge(x_lo, c.next("x", 2))
            for _ in range(8):
                w = slot()
                for e in range(2):
                    tile(w, range(8 * e, 8 * e + 8), q_hi, q_lo, range(8))

        def layer_norm():
            pe.wait_ge(tile_taken, c.at("tile"))
            for n in range(DT):
                last = pe.matmul(bR[:, 0:SEQ], K("avg_model"), h[:, n], start=n == 0, stop=n == DT - 1)
            last.then_inc(ln_done, 1)
            pe.wait_ge(factor_ready, c.at("norm"))
            for n in range(DT):
                pe.wait_ge(ln_sq, c.next("ln"))
                last = pe.matmul(bN[:, 0:SEQ], K("avg_model"), ln_c[:, n], start=n == 0, stop=n == DT - 1)
            last.then_inc(norm_summed, 1)
            c.next("norm")

        def layer_s():
            square_tiles(p_hi, p_lo, arriving=DT)
            turn([s_dt[:, 0:P], s_dt[:, P:SEQ], s_ac[:, 0:P], s_ac[:, P:SEQ]], dt_ready, 1)
            s_group(False)
            s_group(True)
            with c.loop(pe, "s_pairs", 1, S_PAIRS):
                s_group(True)
                s_project()
                s_group(True)
            s_rows(0)
            for m in range(4):
                if m < 3:
                    s_rows(m + 1)
                s_out(m)
            s_norm()
            s_project()
            layer_norm()

        def d_scores(g):
            pe.wait_ge(tile_taken, c.at("tile", -1))
            pe.wait_ge(score_read, c.at("score_read"))
            b = (bS[0], bS[1], bR)[g]
            q, k = d_q[:, g], d_k[:, g]
            pe.matmul(b[:, 0:P], q[:, 0:P], k[:, 0:P], start=True, stop=True)
            pe.matmul(b[:, P:3 * P], q[:, P:SEQ], k, start=True, stop=True).then_inc(scored, 1)
            if g == 2:
                c.next("score_read", 3)

        def d_turn_weights(g):
            turn([d_s[:, g, n * P:(n + 1) * P] for n in range(3)], weighted,
                 c.next("weighted") if g == 0 else c.at("weighted"))

        def d_turn_values(g):
            turn([d_v[:, g, 0:P], d_v[:, g, P:SEQ]], tile_taken, c.at("tile", -1))

        def d_mix():
            pe.wait_ge(turn_read, c.at("turn"))
            pe.wait_ge(y_ready, c.at("mixed", S_GROUPS))
            for g in range(3):
                pe.matmul(bO[:, 0:SEQ], d_vtok[:, g, 0], d_s[:, g, 0:SEQ], start=g == 0, stop=False)
                last = pe.matmul(bO[:, P:SEQ], d_vtok[:, g, 1], d_s[:, g, SEQ:384], start=False, stop=g == 2)
            last.then_inc(mixed, 1)
            c.next("mixed")

        def d_head(prev, first=False):
            for n in range(10):
                if first and n == 3:
                    pe.wait_ge(x_lo, c.next("x", DT))
                square_tiles(*((p_hi, p_lo) if 3 <= n <= 8 else (q_hi, q_lo)), arriving=DT if first and n == 0 else 0)
                if prev and n == 0:
                    d_turn_weights(2)
                if prev and n in (1, 2):
                    d_turn_values(n)
                if prev and n == 3:
                    d_mix()
                if n in (4, 5, 6):
                    d_scores(n - 4)
                if n == 7:
                    d_turn_values(0)
                if n in (8, 9):
                    d_turn_weights(n - 8)

        def layer_d():
            d_head(False, first=True)
            d_head(True)
            with c.loop(pe, "d_pairs", 1, DIL_HEADS // 2):
                d_head(True)
                d_head(True)
            d_turn_weights(2)
            d_turn_values(1)
            d_turn_values(2)
            d_mix()
            pe.wait_ge(x_lo, c.next("x", DIL_HEADS))
            with c.loop(pe, "d_out", 0, 2):
                for _ in range(4):
                    w = slot()
                    for e in range(2):
                        tile(w, range(8 * e, 8 * e + 8), c_hi, c_lo, range(8))
            layer_norm()

        pe.wait_ge(lam_in, 1)
        pe.matmul(bS[0][:, 0:4], K("ones"), tiny[:, 0:4], start=True, stop=True).then_inc(lam_sum, 1)
        PQ = [(p_hi, p_lo), (q_hi, q_lo)]
        for layer in range(DEPTH):
            x, y = PQ[layer % 2], PQ[(layer + 1) % 2]
            if layer in (0, 3):
                layer_a(x, y)
            elif layer == 1:
                layer_b(x, y)
            else:
                layer_c(x, y)
        layer_s()
        layer_d()

    @block.scalar
    def _(act):
        c = Steps(counts, "act")

        def link(ins):
            ins.then_inc(act_step, 1)
            act.wait_ge(act_step, c.next("act"))

        def hold(sem_, value):
            act.wait_ge(sem_, value)
            act.sem_inc(act_passed, 1)

        def hi_ahead(half, ahead=2):
            k = c.k["slot"] + ahead - 1
            cols = slice(half * HALF, (half + 1) * HALF)
            if half == 0:
                act.wait_ge(landed[k % RAW], c.fours("slot", ahead - 1) * 16)
            act.activation(w_hi[k % SPLIT][:, cols], raw[k % RAW][:, cols], ACT.Copy).then_inc(hi_ready, 1)

        def factor_pair():
            act.wait_ge(factor_ready, c.at("norm"))
            act.wait_ge(norm_summed, c.next("norm"))
            link(act.activation(bN[:], bN[:], ACT.Ln, bias=K("eps_6")))
            act.activation(rsn.rearrange("p a b -> p (a b)")[:, 0:512], bN[:], ACT.Exp, scale=-0.5).then_inc(factor_ready, 1)

        def tick(tiles=1, read=False):
            c.next("slot")
            if tiles == 1:
                act.wait_ge(half_used, c.next("half"))
            else:
                act.wait_ge(tile_done, c.at("tile", (tiles + 1) // 2))
            hi_ahead(0)
            act.wait_ge(tile_done, c.next("tile", tiles))
            hi_ahead(1)
            if read:
                act.wait_ge(tile_taken, c.at("tile"))

        def tail(n, hi, gain, sem_, value, par):
            hold(sem_, value)
            act.activation(hi[:, n], h[:, n], ACT.Copy, scale=gain).then_inc(x_hi, 1)
            hold(summed, c.at("sum", -1))
            act.activation(sq[:, par], h[:, n], ACT.Square).then_inc(squared, 1)
            c.next("sum")

        def factor(dst, eps="eps_6"):
            act.wait_ge(factor_ready, c.at("norm"))
            act.wait_ge(norm_summed, c.next("norm"))
            link(act.activation(bN[:, SEQ:], bN[:, 0:SEQ], ACT.Ln, bias=K(eps)))
            act.activation(dst, bN[:, SEQ:], ACT.Exp, scale=-0.5).then_inc(factor_ready, 1)

        def sigmoid(buf, sem_, value):
            act.wait_ge(sem_, value)
            link(act.activation(buf, buf, ACT.Exp, scale=-1.0))
            link(act.activation(buf, buf, ACT.Ln, bias=1.0))
            act.activation(buf, buf, ACT.Exp, scale=-1.0).then_inc(sig_ready, 1)
            c.next("sig")

        def p_slot(layer):
            tick(8)

        def gates(hi, gain_at, last):
            for half in range(2):
                if half:
                    tick(8)
                with c.loop(act, "gates_last" if last else "gates", 0, 2) as i:
                    def finish(j):
                        if last:
                            act.wait_ge(res_ready, c.next("res"))
                        else:
                            tail(i * 4 + (8 * half + j), hi, vec[:, bass.ds(i * 4 + (gain_at + 8 * half + j), 1)],
                                 res_ready, c.next("res"), j % 2)
                    for j in range(4):
                        tick()
                        sigmoid(zg[:, j % 2], clamped, c.next("clamped"))
                        if j:
                            finish(j - 1)
                    finish(3)

        def out_and_gates(layer, x, y):
            a = VEC["ple_norm"] + layer * DT
            with c.loop(act, "outs", 0, 4) as i:
                for j in range(4):
                    tick()
                    tail(i * 4 + j, x[0], vec[:, bass.ds(i * 4 + (a + j), 1)], tile_taken, c.at("tile"), j % 2)
            factor(rstd[:])
            gates(y[0], VEC["norm_gain"] + (layer + 1) * DT, layer == DEPTH - 1)

        def turned(dst, src):
            act.wait_ge(turn_done, c.next("turn"))
            act.activation(dst, src, ACT.Copy).then_inc(turn_read, 1)

        def a_square_out():
            act.wait_ge(mixed, c.next("mixed"))
            act.activation(yo, bO[:], ACT.Square).then_inc(mixed_read, 1)

        def a_y_hi(y, i):
            hold(y_ready, c.next("y"))
            act.activation(y[0][:, bass.ds(i * 2, 2), :], yo.rearrange("p (a b) -> p a b", a=2), ACT.Copy).then_inc(x_hi, 1)

        def a_softmax():
            act.wait_ge(maxed, c.next("maxed"))
            for s in range(2):
                act.activation(sm[:, s, 0:P], sm[:, s, 0:P], ACT.Exp, bias=tiny[:, 4 + 2 * s:5 + 2 * s],
                               accum_out=tiny[:, 8 + 2 * s:9 + 2 * s])
                last = act.activation(sm[:, s, P:384], sm[:, s, P:384], ACT.Exp, bias=tiny[:, 5 + 2 * s:6 + 2 * s],
                                      accum_out=tiny[:, 9 + 2 * s:10 + 2 * s])
            last.then_inc(exped, 1)

        def a_head(y, i, prev, first):
            for j in range(8):
                tick(read=True)
                if j < 4:
                    act.activation(sqh[:, j % 2], qs[:, j % 3], ACT.Square).then_inc(sq_head, 1)
                if j in (1, 2, 3, 4):
                    factor(rsn[:, (j - 1) % 2])
                if j == 1 and prev:
                    turned(pt, bT[:, 0:384])
                if j == 2 and prev:
                    a_square_out()
                if j == 3 and prev:
                    factor(rsn[:, 2])
                if j == 4 and prev:
                    a_y_hi(y, i - 1)
                if j in (5, 6):
                    turned(vtok[:, :, (j - 5) * P:(j - 4) * P], bT[:, 0:SEQ].rearrange("p (a b) -> p a b", a=2))
                if j in (6, 7):
                    sigmoid(zc[:, j - 6], clamped, c.next("clamped"))
                if j == 7:
                    a_softmax()
                if j % 2 == 0:
                    tick()
                if j in (3, 7):
                    c.next("tile")

        def layer_a(layer, x, y):
            factor(rstd[:])
            a_head(y, 0, False, True)
            with c.loop(act, "a_heads", 1, A_HEADS) as i:
                a_head(y, i, True, False)
            split_p(layer)
            tick(8)
            turned(pt, bT[:, 0:384])
            a_square_out()
            factor(rsn[:, 2])
            a_y_hi(y, A_HEADS - 1)
            out_and_gates(layer, x, y)

        def squares(dst, src):
            act.activation(dst, src, ACT.Square).then_inc(sq_head, 1)

        def b_y_hi(y, i):
            hold(y_ready, c.next("y"))
            act.activation(y[0][:, bass.ds(i * 2, 2), :], b_yo.rearrange("p (a b) -> p a b", a=2), ACT.Copy).then_inc(x_hi, 1)

        def b_turned():
            turned(b_sm[:, 0], bT[:, 0:384])
            turned(b_sm[:, 1], bR[:, 0:384])

        def b_pair(y, i, prev):
            tick()
            tick(3, read=True)
            for n in range(3):
                squares(bsq[:, n], bq[:, n])
            tick()
            if prev:
                b_turned()
            factor_pair()
            tick(4, read=True)
            for n in range(2):
                squares(bsk[:, n], bk[:, n])
            factor(rsn[:, 2])
            c.next("tile")
            tick()
            factor_pair()
            tick()
            turned(b_vtok.rearrange("p a b c -> p (a b c)"), bT[:])
            sigmoid(b_zc[:, 0], clamped, c.next("clamped"))
            if prev:
                b_y_hi(y, i - 1)
            tick()
            tick()
            sigmoid(b_zc[:, 1], clamped, c.next("clamped"))
            act.wait_ge(maxed, c.next("maxed"))
            for s in range(2):
                act.activation(b_sm[:, s, 0:P], b_sm[:, s, 0:P], ACT.Exp, bias=tiny[:, 4 + 2 * s:5 + 2 * s],
                               accum_out=tiny[:, 8 + 2 * s:9 + 2 * s])
                last = act.activation(b_sm[:, s, P:384], b_sm[:, s, P:384], ACT.Exp, bias=tiny[:, 5 + 2 * s:6 + 2 * s],
                                      accum_out=tiny[:, 9 + 2 * s:10 + 2 * s])
            last.then_inc(exped, 1)
            c.next("tile")

        def layer_b(layer, x, y):
            for n in range(9):
                tick_first = n == 0
                if tick_first:
                    factor(rstd[:])
                tick(read=True)
                if n < 8:
                    name = "b_cq_norm" if n < 4 else "b_ckv_norm"
                    act.activation(c_hi[:, n], b_cs[:, n % 2], ACT.Copy, scale=V(name, n % 4)).then_inc(x_hi, 1)
                    squares(b_csq[:, n], b_cs[:, n % 2])
                else:
                    squares(bsq[:, 0], b_cs[:, 0])
                if n == 4:
                    factor(b_rq)
            factor(b_rkv)
            factor(rsn[:, 0])
            b_pair(y, 0, False)
            with c.loop(act, "b_pairs", 1, B_PAIRS) as i:
                b_pair(y, i, True)
            split_p(layer)
            tick(8)
            b_turned()
            b_y_hi(y, B_PAIRS - 1)
            c.next("mixed", B_PAIRS)
            out_and_gates(layer, x, y)

        def softplus(e, u, w, l):
            act.wait_ge(soft_in, c.next("soft"))
            act.activation(e, u, ACT.Exp, scale=-1.0).then_inc(soft_out, 1)
            act.wait_ge(soft_in, c.next("soft"))
            link(act.activation(l, u, ACT.Ln))
            act.activation(w, l, ACT.Exp, scale=-1.0).then_inc(soft_out, 1)

        def c_split(g):
            act.wait_ge(conv_done, 4 * (g + 1))
            act.activation(c_hi[:, 4 * (g % 2):4 * (g % 2) + 4], xc[:, 4 * g:4 * g + 4], ACT.Copy).then_inc(x_hi, 1)

        def c_decay():
            act.wait_ge(chain_in, c.next("chain"))
            u = rg.rearrange("p a b -> p (a b)")
            act.preload_act_table(ACT.Tanh)
            act.activation(bS[0][:], u[:, 0:512], ACT.Tanh)
            link(act.activation(bS[1][:], u[:, 512:1024], ACT.Tanh))
            link(act.activation(u, u, ACT.Exp, scale=-1.0))
            act.preload_act_table_set("natural_log_exp_and_others")

        def c_scale():
            act.activation(bR[:], bS[0][:], ACT.Ln, scale=2.0)
            link(act.activation(bT[:], bS[1][:], ACT.Ln, scale=2.0))
            act.activation(bS[0][:], bS[0][:], ACT.Ln, bias=1.0)
            link(act.activation(bS[1][:], bS[1][:], ACT.Ln, bias=1.0))
            for bank, power in ((bR, 0.5), (bT, 0.5), (bS[0], -0.5), (bS[1], -0.5)):
                last = act.activation(bank[:], bank[:], ACT.Exp, scale=power)
            last.then_inc(chain_out, 1)

        def layer_c(layer, x, y):
            softplus(soft[:, 0], soft[:, 1], soft[:, 2], sp8)
            factor(rstd[:])
            with c.loop(act, "c_in", 0, 3):
                for _ in range(4):
                    tick()
            c_split(0)

            def y_high(n):
                act.wait_ge(gated, c.next("gated"))
                act.activation(y[0][:, n], c_gz[:, n % 2], ACT.Copy).then_inc(x_hi, 1)
            for g in range(5):
                if g < 4:
                    tick(8, read=True)
                    for buf in (rg, ig):
                        b = buf.rearrange("p a b -> p (a b)")
                        link(act.activation(b, b, ACT.Exp, scale=-1.0))
                        link(act.activation(b, b, ACT.Ln, bias=1.0))
                        act.activation(b, b, ACT.Exp, scale=-1.0).then_inc(gates_out, 1)
                for j in range(4):
                    tick()
                    if g:
                        sigmoid(c_zc[:, j % 2], clamped, c.next("clamped"))
                        if j:
                            y_high(4 * g - 5 + j)
                    if g < 3 and j == 0:
                        c_split(g + 1)
                    if g < 4 and j == 0:
                        c_decay()
                    if g < 4 and j == 1:
                        c_scale()
                if g:
                    y_high(4 * g - 1)
            split_p(layer)
            tick(8)
            out_and_gates(layer, x, y)

        def split_p(layer):
            act.wait_ge(p_in, 16 * (c.next("p")))
            act.activation(c_hi[:, 0:2], p_raw, ACT.Copy).then_inc(p_hi_ready, 1)

        def modulated(hi, at, norm=False):
            for i in range(4):
                for j in range(4):
                    n = i * 4 + j
                    if norm:
                        act.wait_ge(ln_go, c.next("ln_go"))
                    act.activation(hi[:, n], h[:, n], ACT.Identity, bias=mod[:, bass.ds(i * 4 + (at + j), 1)],
                                   scale=mod[:, bass.ds(i * 4 + (at + DT + j), 1)]).then_inc(x_hi, 1)

        def s_decay():
            act.wait_ge(rows_read, c.next("rows"))
            act.activation(s_e, s_e, ACT.Exp).then_inc(decayed, 1)

        def s_y_hi(par):
            act.wait_ge(y_ready, c.next("y"))
            act.activation(q_hi[:, 4 * par:4 * par + 4], s_y, ACT.Copy).then_inc(x_hi, 1)

        def s_sigmoid(n):
            sigmoid(s_zc[n % 2], clamped, c.next("clamped"))

        def s_square(m):
            act.wait_ge(s_y_ready, c.next("s_y"))
            act.wait_ge(s_sum, c.at("s_y", -2))
            act.activation(rsn[:, m % 2], s_y[:, m], ACT.Square).then_inc(s_sq, 1)

        def s_group(par, prev):
            for n in range(10):
                tick()
                if prev and 2 <= n <= 5:
                    s_decay()
                if n:
                    s_sigmoid(n - 1)
                if prev and 3 <= n <= 6:
                    s_square(n - 3)
                if prev and n == 7:
                    factor(rsn[:, 2], "eps_5")
                if prev and n == 8:
                    s_y_hi(1 - par)
            s_sigmoid(9)

        def s_project():
            for _ in range(8):
                tick(2)

        def layer_norm(w):
            for n in range(DT):
                act.wait_ge(ln_go, c.next("ln_go"))
                act.activation(ln_c[:, n], h[:, n], ACT.Square).then_inc(ln_sq, 1)
            factor(rstd[:], "eps_5")

        def layer_s():
            act.wait_ge(mod_ready, 1)
            modulated(p_hi, 0)
            tick()
            act.activation(tiny[:, 0:1], V("s_A_log"), ACT.Exp).then_inc(soft_out, 1)
            s_softplus()
            s_group(0, False)
            s_group(1, True)
            with c.loop(act, "s_pairs", 1, S_PAIRS):
                s_group(0, True)
                s_project()
                s_group(1, True)
            for m in range(4):
                s_decay()
                s_square(m)
            factor(rsn[:, 2], "eps_5")
            s_y_hi(1)
            s_project()
            layer_norm(0)

        def s_softplus():
            softplus(s_y[:, 0], s_y[:, 1], s_y[:, 2], s_y[:, 3])

        def d_softmax():
            act.wait_ge(maxed, c.next("maxed"))
            act.activation(d_s[:, :, 0:P], d_s[:, :, 0:P], ACT.Exp, bias=tiny[:, 4:5], scale=P ** -0.5,
                           accum_out=tiny[:, 8:9])
            act.activation(d_s[:, :, P:384], d_s[:, :, P:384], ACT.Exp, bias=tiny[:, 5:6], scale=P ** -0.5,
                           accum_out=tiny[:, 9:10]).then_inc(exped, 1)

        def d_weights(g):
            turned(d_s[:, g], bT[:, 0:384])

        def d_values(g):
            turned(d_vtok[:, g], bT[:, 0:SEQ].rearrange("p (a b) -> p a b", a=2))

        def d_y_hi(n):
            hold(y_ready, c.next("y"))
            act.activation(c_hi[:, n], rsn[:, 0], ACT.Copy).then_inc(x_hi, 1)

        def d_head(i, par, prev):
            for n in range(10):
                tick()
                if prev and n == 0:
                    d_weights(2)
                if prev and n in (1, 2):
                    d_values(n)
                if prev and n == 3:
                    d_y_hi(i * 2 + (par - 1))
                if n == 6:
                    d_softmax()
                if n == 7:
                    d_values(0)
                if n in (8, 9):
                    d_weights(n - 8)
                if n == 9:
                    sigmoid(d_zc[:], clamped, c.next("clamped"))

        def layer_d():
            c.next("turn", 1 + 4 * S_GROUPS)
            modulated(q_hi, 48, norm=True)
            for i in range(4):
                for j in range(4):
                    n = i * 4 + j
                    act.activation(p_hi[:, n], h[:, n], ACT.Copy).then_inc(x_hi, 1)
            d_head(0, 0, False)
            d_head(0, 1, True)
            with c.loop(act, "d_pairs", 1, DIL_HEADS // 2) as i:
                d_head(i, 0, True)
                d_head(i, 1, True)
            d_weights(2)
            d_values(1)
            d_values(2)
            d_y_hi(DIL_HEADS - 1)
            with c.loop(act, "d_out", 0, 2):
                for _ in range(4):
                    tick(2)
            layer_norm(1)

        act.preload_act_table(ACT.Sin)
        act.wait_ge(trig_in, 1)
        for n, (sin, half) in enumerate(((sin_a, cos_a), (sin_b, cos_b))):
            act.activation(half[:], sin[:], ACT.Sin, scale=0.5).then_inc(act_step, 1)
            act.wait_ge(act_step, c.next("act"))
            act.activation(sin[:], sin[:], ACT.Sin).then_inc(trig_out, 1)
        act.preload_act_table_set("natural_log_exp_and_others")
        b = tiny[:, 48:64]
        act.wait_ge(ada_in, 1)
        link(act.activation(b, b, ACT.Exp, scale=-1.0))
        link(act.activation(b, b, ACT.Ln, bias=1.0))
        act.activation(b, b, ACT.Exp, scale=-1.0).then_inc(ada_z, 1)
        act.wait_ge(ada_in, 2)
        link(act.activation(ada_hl[:, :, 0], b, ACT.Copy))
        act.activation(ada_hz[:, :, 0], b, ACT.Copy).then_inc(ada_out, 1)
        act.wait_ge(lam_sum, 1)
        act.activation(tiny[:, 4:8], bS[0][:, 0:4], ACT.Exp).then_inc(lam_exp, 1)
        c.k["slot"] = 0
        for ahead in (1, 2):
            hi_ahead(0, ahead)
            hi_ahead(1, ahead)
        act.wait_ge(h_in, 16)

        def start(i):
            for j in range(4):
                tail(i * 4 + j, p_hi, vec[:, bass.ds(i * 4 + (VEC["norm_gain"] + j), 1)], h_in, 16, j % 2)
        start(0)
        with c.loop(act, "start", 1, 4) as i:
            start(i)
        PQ = [(p_hi, p_lo), (q_hi, q_lo)]
        for layer in range(DEPTH):
            x, y = PQ[layer % 2], PQ[(layer + 1) % 2]
            if layer in (0, 3):
                layer_a(layer, x, y)
            elif layer == 1:
                layer_b(layer, x, y)
            else:
                layer_c(layer, x, y)
        layer_s()
        layer_d()

    @block.vector
    def _(dve):
        c = Steps(counts, "dve")

        def link(ins):
            ins.then_inc(dve_step, 1)
            dve.wait_ge(dve_step, c.next("dve"))

        def lo_half(half, ahead=2):
            k = c.k["slot"] + ahead - 1
            cols = slice(half * HALF, (half + 1) * HALF)
            dve.wait_ge(hi_ready, c.at("slot", ahead) * 2 + (half - 1) if half == 0 else c.at("slot", ahead) * 2)
            dve.tensor_tensor(w_lo[k % SPLIT][:, cols], raw[k % RAW][:, cols], w_hi[k % SPLIT][:, cols], SUB).then_inc(lo_ready, 1)

        def begin():
            c.next("slot")
            lo_half(0)

        def take():
            dve.wait_ge(tile_done, c.next("tile"))
            g = G[c.bank][:, 0:SEQ]
            c.bank ^= 1
            return g

        def mod_tick(m):
            begin()
            g = take()[0:2]
            if m % 2 == 0:
                dve.tensor_copy(acc[0:2], g).then_inc(tile_taken, 1)
            else:
                dve.wait_ge(tile_taken, c.at("tile", -1))
                dve.tensor_tensor(acc[0:2], acc[0:2], g, ADD).then_inc(tile_taken, 1)
            lo_half(1)

        def mod_columns(i, at):
            two = lambda base: bass.ds(i * 4 + (base + at), 2)
            dve.tensor_tensor(mod[:, two(0)], take()[:, 0:2], vec[:, two(VEC["ada_b"])], ADD).then_inc(tile_taken, 1)

        def tail(n, x, gain):
            dve.wait_ge(x_hi, c.next("x"))
            dve.scalar_tensor_tensor(x[1][:, n], h[:, n], gain, x[0][:, n], MUL, SUB).then_inc(x_lo, 1)

        def factor():
            dve.wait_ge(factor_ready, c.next("norm"))

        def p_slot():
            c.next("slot")
            for n in range(8):
                g = take()
                dve.tensor_copy(proj[:, n], g).then_inc(tile_taken, 1)
            lo_half(0)
            lo_half(1)

        def gates(x, gain_at, last):
            for half in range(2):
                if half:
                    p_slot()
                with c.loop(dve, "gates_last" if last else "gates", 0, 2) as i:
                    def finish(j):
                        n = i * 4 + (8 * half + j)
                        dve.wait_ge(sig_ready, c.next("sig"))
                        link(dve.tensor_tensor(sg[:, j % 2], zg[:, j % 2], proj[:, i * 4 + j], MUL))
                        dve.tensor_tensor(h[:, n], h[:, n], sg[:, j % 2], ADD).then_inc(res_ready, 1)
                        dve.wait_ge(res_ready, c.next("res"))

                    def low(j):
                        if not last:
                            tail(i * 4 + (8 * half + j), x, vec[:, bass.ds(i * 4 + (gain_at + 8 * half + j), 1)])
                    for j in range(4):
                        begin()
                        g = take()
                        dve.tensor_tensor(zg[:, j % 2], g, rstd[:], MUL).then_inc(tile_taken, 1)
                        lo_half(1)
                        if j > 0:
                            finish(j - 1)
                        if j > 1:
                            low(j - 2)
                    finish(3)
                    low(2)
                    low(3)

        def out_and_gates(layer, x, y):
            a = VEC["ple_norm"] + layer * DT
            with c.loop(dve, "outs", 0, 4) as i:
                for j in range(4):
                    n = i * 4 + j
                    begin()
                    g = take()
                    dve.tensor_tensor(h[:, n], g, h[:, n], ADD).then_inc(tile_taken, 1)
                    lo_half(1)
                    dve.wait_ge(tile_taken, c.at("tile"))
                    tail(n, x, vec[:, bass.ds(i * 4 + (a + j), 1)])
            factor()
            gates(y, VEC["norm_gain"] + (layer + 1) * DT, layer == DEPTH - 1)

        def a_weigh(j):
            dve.wait_ge(exped, c.next("exped"))
            link(dve.reciprocal(tiny[:, 12:16], tiny[:, 8:12]))
            link(dve.tensor_scalar(tiny[:, 14:16], tiny[:, 14:16], lam[:, j:j + 1], None, MUL))
            spans = ((0, P), (P, 384))
            for b, (u, v) in enumerate(spans):
                last = dve.tensor_scalar(sm[:, 0, u:v], sm[:, 0, u:v], tiny[:, 12 + b:13 + b], None, MUL)
            link(last)
            for b, (u, v) in enumerate(spans):
                last = dve.scalar_tensor_tensor(sm[:, 0, u:v], sm[:, 1, u:v], tiny[:, 14 + b:15 + b],
                                                sm[:, 0, u:v], MUL, ADD)
            last.then_inc(weighted, 1)

        def a_silu(e):
            dve.wait_ge(sig_ready, c.next("sig"))
            link(dve.tensor_tensor(gz[:, e], gz[:, e], zc[:, e], MUL))

        def a_finish(j):
            factor()
            for e in range(2):
                last = dve.tensor_tensor(gz[:, e], gz[:, e], rsn[:, 2], MUL)
            link(last)
            for e in range(2):
                last = dve.scalar_tensor_tensor(yo[:, e * SEQ:(e + 1) * SEQ], bO[:, e * SEQ:(e + 1) * SEQ],
                                                tiny[:, 16 + 2 * j + e:17 + 2 * j + e], gz[:, e], MUL, MUL)
            last.then_inc(y_ready, 1)
            dve.wait_ge(y_ready, c.next("y"))

        def a_y_lo(y, i):
            dve.wait_ge(x_hi, c.next("x"))
            y2 = bass.ds(i * 2, 2)
            dve.tensor_tensor(y[1][:, y2, :], yo.rearrange("p (a b) -> p a b", a=2), y[0][:, y2, :], SUB).then_inc(x_lo, 1)

        def a_head(y, i, prev, first, jl):
            for j in range(8):
                begin()
                g = take()
                if first and j == 0:
                    factor()
                dve.wait_ge(scaled, c.at("scaled"))
                dve.wait_ge(roped, c.at("rot"))
                if j < 4:
                    dst = qs[:, j % 3]
                elif j < 6:
                    dst = vs[:, j - 4]
                else:
                    dst = gz[:, j - 6]
                dve.tensor_tensor(dst, g, rstd[:], MUL).then_inc(tile_taken, 1)
                lo_half(1)
                if j in (2, 3, 4, 5):
                    n = j - 2
                    factor()
                    gain = V("a_q_norm" if n < 2 else "a_k_norm", jl)
                    dve.scalar_tensor_tensor(qn[:, n % 2], qs[:, n % 3], gain, rsn[:, n % 2], MUL, MUL).then_inc(scaled, 1)
                    c.next("scaled")
                if j in (3, 4, 5, 6):
                    n = j - 3
                    dve.wait_ge(rot_done, c.next("rot"))
                    dve.tensor_tensor(qr[:, n], bR[:, 0:SEQ], sin_a[:], MUL).then_inc(rot_read, 1)
                    dve.wait_ge(rot_read, c.at("rot"))
                    dve.wait_ge(cos_done, c.at("rot"))
                    dve.tensor_tensor(qr[:, n], qr[:, n], t2[:, n % 2], ADD).then_inc(roped, 1)
                if j == 0 and prev:
                    a_silu(1)
                    a_weigh(jl)
                if j == 4 and prev:
                    a_finish(jl)
                if j == 5 and prev:
                    a_y_lo(y, i - 1)
                if j == 7:
                    a_silu(0)
                    for s in range(2):
                        dve.wait_ge(scored, c.next("scored"))
                        dve.scalar_tensor_tensor(sm[:, s], bS[s][:, 0:384], P ** -0.5, K("mask"), MUL, ADD).then_inc(score_read, 1)
                    dve.wait_ge(score_read, c.at("scored"))
                    for s in range(2):
                        dve.tensor_reduce(tiny[:, 4 + 2 * s:5 + 2 * s], sm[:, s, 0:P], AX.X, MAX, negate=True)
                        last = dve.tensor_reduce(tiny[:, 5 + 2 * s:6 + 2 * s], sm[:, s, P:384], AX.X, MAX, negate=True)
                    last.then_inc(maxed, 1)
                if j % 2 == 0:
                    mod_tick(j // 2)
                if j in (3, 7):
                    mod_columns(i, 64 * jl + j // 2 - 1)

        def layer_a(layer, x, y):
            jl = 0 if layer == 0 else 1
            a_head(y, 0, False, True, jl)
            with c.loop(dve, "a_heads", 1, A_HEADS) as i:
                a_head(y, i, True, False, jl)
            split_p(layer)
            a_silu(1)
            a_weigh(jl)
            p_slot()
            a_finish(jl)
            a_y_lo(y, A_HEADS - 1)
            c.next("mixed", A_HEADS)
            out_and_gates(layer, x, y)

        def b_scale(buf, gain, fac):
            dve.scalar_tensor_tensor(buf, buf, gain, fac, MUL, MUL).then_inc(scaled, 1)
            c.next("scaled")

        def rope(dst, sin, other):
            dve.wait_ge(rot_done, c.next("rot"))
            dve.tensor_tensor(dst, bR[:, 0:SEQ], sin, MUL).then_inc(rot_read, 1)
            dve.wait_ge(rot_read, c.at("rot"))
            dve.wait_ge(cos_done, c.at("rot"))
            dve.tensor_tensor(dst, dst, other, ADD).then_inc(roped, 1)

        def b_finish():
            dve.wait_ge(sig_ready, c.next("sig", 2))
            for s in range(2):
                last = dve.tensor_tensor(b_gz[:, s], b_gz[:, s], b_zc[:, s], MUL)
            link(last)
            dve.wait_ge(mixed, c.next("mixed"))
            dve.tensor_tensor(b_yo, bO[:], b_gz.rearrange("p a b -> p (a b)"), MUL).then_inc(y_ready, 1)
            dve.wait_ge(y_ready, c.next("y"))

        def b_y_lo(y, i):
            dve.wait_ge(x_hi, c.next("x"))
            y2 = bass.ds(i * 2, 2)
            dve.tensor_tensor(y[1][:, y2, :], b_yo.rearrange("p (a b) -> p a b", a=2), y[0][:, y2, :], SUB).then_inc(x_lo, 1)

        def b_pair(y, i, prev):
            c.bank = 0
            mod_tick(0)
            c.next("slot")
            for n in range(3):
                g = take()
                dve.wait_ge(weighted, c.at("exped"))
                dve.tensor_tensor(bq[:, n], g, b_rq, MUL).then_inc(tile_taken, 1)
            lo_half(0)
            lo_half(1)
            if prev:
                b_weigh()
            mod_tick(1)
            c.next("slot")
            for n in range(4):
                g = take()
                dst = bv[:, n // 2] if n % 2 else bk[:, n // 2]
                dve.tensor_tensor(dst, g, b_rkv, MUL).then_inc(tile_taken, 1)
            lo_half(0)
            lo_half(1)
            dve.wait_ge(tile_taken, c.at("tile"))
            factor()
            for n in range(2):
                b_scale(bq[:, n], V("b_qn"), rsn[:, n])
            if prev:
                b_finish()
            factor()
            b_scale(bq[:, 2], V("b_qr"), rsn[:, 2])
            mod_columns(i, 32)
            mod_tick(2)
            rope(b_pe, sin_b[:], b_t2)
            begin()
            g = take()
            dve.tensor_tensor(b_gz[:, 0], g, rstd[:], MUL).then_inc(tile_taken, 1)
            lo_half(1)
            factor()
            for n in range(2):
                b_scale(bk[:, n], V("b_kn"), rsn[:, n])
            if prev:
                b_y_lo(y, i - 1)
            mod_tick(3)
            begin()
            g = take()
            dve.tensor_tensor(b_gz[:, 1], g, rstd[:], MUL).then_inc(tile_taken, 1)
            mod_columns(i, 34)
            lo_half(1)
            for s in range(2):
                dve.wait_ge(scored, c.next("scored"))
                dve.scalar_tensor_tensor(b_sm[:, s], bS[s][:, 0:384], 192 ** -0.5, K("mask"), MUL, ADD).then_inc(score_read, 1)
            dve.wait_ge(score_read, c.at("scored"))
            for s in range(2):
                dve.tensor_reduce(tiny[:, 4 + 2 * s:5 + 2 * s], b_sm[:, s, 0:P], AX.X, MAX, negate=True)
                last = dve.tensor_reduce(tiny[:, 5 + 2 * s:6 + 2 * s], b_sm[:, s, P:384], AX.X, MAX, negate=True)
            last.then_inc(maxed, 1)

        def b_weigh():
            dve.wait_ge(exped, c.next("exped"))
            link(dve.reciprocal(tiny[:, 12:16], tiny[:, 8:12]))
            for s in range(2):
                for b, (u, v) in enumerate(((0, P), (P, 384))):
                    last = dve.tensor_scalar(b_sm[:, s, u:v], b_sm[:, s, u:v],
                                             tiny[:, 12 + 2 * s + b:13 + 2 * s + b], None, MUL)
            last.then_inc(weighted, 1)

        def layer_b(layer, x, y):
            for n in range(9):
                begin()
                g = take()
                if n == 0:
                    factor()
                dve.tensor_tensor(b_cs[:, n % 2], g, rstd[:], MUL).then_inc(tile_taken, 1)
                lo_half(1)
                if n < 8:
                    name = "b_cq_norm" if n < 4 else "b_ckv_norm"
                    dve.wait_ge(x_hi, c.next("x"))
                    dve.scalar_tensor_tensor(c_lo[:, n], b_cs[:, n % 2], V(name, n % 4), c_hi[:, n], MUL, SUB).then_inc(x_lo, 1)
                    dve.wait_ge(x_lo, c.at("x"))
            c.next("norm", 2)
            factor()
            b_scale(b_cs[:, 0], V("b_kr"), rsn[:, 0])
            rope(b_kpe, sin_b[:], b_t2)
            dve.wait_ge(roped, c.at("rot"))
            b_pair(y, 0, False)
            with c.loop(dve, "b_pairs", 1, B_PAIRS) as i:
                b_pair(y, i, True)
            b_weigh()
            c.bank = 0
            split_p(layer)
            p_slot()
            b_finish()
            b_y_lo(y, B_PAIRS - 1)
            out_and_gates(layer, x, y)

        def softplus(z, e, u, w, l, out):
            dve.scalar_tensor_tensor(u, z, -1.0, z, MUL, MAX).then_inc(soft_in, 1)
            dve.wait_ge(soft_out, c.next("soft"))
            dve.tensor_scalar(u, e, 1.0, None, ADD).then_inc(soft_in, 1)
            dve.wait_ge(soft_out, c.next("soft"))
            link(dve.tensor_scalar(u, u, 1.0, None, SUB))
            link(dve.tensor_tensor(e, e, u, SUB))
            link(dve.tensor_tensor(e, e, w, MUL))
            link(dve.tensor_tensor(l, l, e, ADD))
            link(dve.scalar_tensor_tensor(out, z, 0.0, l, MAX, ADD))

        def c_split(g):
            dve.wait_ge(x_hi, c.next("x"))
            k = slice(4 * (g % 2), 4 * (g % 2) + 4)
            dve.tensor_tensor(c_lo[:, k], xc[:, 4 * g:4 * g + 4], c_hi[:, k], SUB).then_inc(x_lo, 1)

        def c_exponent(g):
            dve.wait_ge(gates_out, 2 * g + 2)
            for n in range(4):
                last = dve.tensor_scalar(rg[:, n], rg[:, n], sp8[:, 4 * g + n:4 * g + n + 1], 1e-19, MUL, MAX)
            last.then_inc(chain_in, 1)
            link(dve.tensor_tensor(ig, ig, xc[:, 4 * g:4 * g + 4], MUL))

        def c_scale():
            b = ig.rearrange("p a b -> p (a b)")
            dve.wait_ge(chain_out, c.next("chain"))
            for one, two in ((bR, bT), (bS[0], bS[1])):
                dve.tensor_tensor(b[:, 0:512], b[:, 0:512], one[:], MUL)
                link(dve.tensor_tensor(b[:, 512:1024], b[:, 512:1024], two[:], MUL))

        def c_scan(g):
            for n in range(4):
                last = dve.tensor_tensor_scan(xc[:, 4 * g + n], rg[:, n], ig[:, n], 0.0, MUL, ADD)
            link(last)

        def layer_c(layer, x, y):
            lam_ = vec[:, VEC["c_lambda"]:VEC["c_lambda"] + DT]
            z = c_gz[:, 0, 0:DT]
            link(dve.tensor_scalar(z, lam_, -1.0, None, MUL))
            softplus(z, soft[:, 0], soft[:, 1], soft[:, 2], sp8, sp8)
            link(dve.tensor_scalar(sp8, sp8, 8.0, None, MUL))
            link(dve.memset(xbp[:, :, 0:3], 0.0))
            factor()
            def c_input(i, j):
                n = i * 4 + j
                begin()
                g = take()
                xb = xbp[:, j % 2]
                dve.tensor_tensor(xb[:, 3:259], g, rstd[:], MUL).then_inc(tile_taken, 1)
                lo_half(1)
                dve.wait_ge(tile_taken, c.at("tile"))
                w = lambda k: vec[:, bass.ds(i * 4 + (VEC["c_conv_w"] + DT * k + j), 1)]
                link(dve.tensor_scalar(xc[:, n], xb[:, 0:SEQ], w(0),
                                       vec[:, bass.ds(i * 4 + (VEC["c_conv_b"] + j), 1)], MUL, ADD))
                for k in (1, 2):
                    link(dve.scalar_tensor_tensor(xc[:, n], xb[:, k:k + SEQ], w(k), xc[:, n], MUL, ADD))
                dve.scalar_tensor_tensor(xc[:, n], xb[:, 3:3 + SEQ], w(3), xc[:, n], MUL, ADD).then_inc(conv_done, 1)

            def finish(n):
                dve.wait_ge(sig_ready, c.next("sig"))
                link(dve.tensor_tensor(c_gz[:, n % 2], c_gz[:, n % 2], c_zc[:, n % 2], MUL))
                dve.tensor_tensor(c_gz[:, n % 2], c_gz[:, n % 2], xc[:, n], MUL).then_inc(gated, 1)

            def low(n):
                dve.wait_ge(x_hi, c.next("x"))
                dve.tensor_tensor(y[1][:, n], c_gz[:, n % 2], y[0][:, n], SUB).then_inc(x_lo, 1)
                dve.wait_ge(x_lo, c.at("x"))
            with c.loop(dve, "c_in", 0, 3) as i:
                for j in range(4):
                    c_input(i, j)
            dve.wait_ge(conv_done, 12)
            c_split(0)
            for g in range(5):
                if g < 4:
                    c.next("slot")
                    for n in range(8):
                        t_ = take()
                        m = 2 * (n // 4) + n % 2
                        bias = V("c_b_x" if n % 4 > 1 else "c_b_a", 4 * g + m)
                        dst = (ig if n % 4 > 1 else rg)[:, m]
                        dve.tensor_scalar(dst, t_, bias, SIG_MIN, ADD, MAX).then_inc(tile_taken, 1)
                    lo_half(0)
                    lo_half(1)
                for j in range(4):
                    if g == 0:
                        c_input(3, j)
                        if j == 3:
                            dve.wait_ge(conv_done, DT)
                    else:
                        n = 4 * (g - 1) + j
                        if j > 1:
                            low(n - 2)
                        begin()
                        t_ = take()
                        dve.tensor_tensor(c_gz[:, j % 2], t_, rstd[:], MUL).then_inc(tile_taken, 1)
                        lo_half(1)
                        if j:
                            finish(n - 1)
                    if g < 4 and j == 0:
                        c_exponent(g)
                    if g < 3 and j == 0:
                        c_split(g + 1)
                    if g < 4 and j == 2:
                        c_scale()
                    if g < 4 and j == 3:
                        c_scan(g)
                if g:
                    finish(4 * g - 1)
                    low(4 * g - 2)
                    low(4 * g - 1)
            split_p(layer)
            dve.wait_ge(x_lo, c.at("x"))
            p_slot()
            out_and_gates(layer, x, y)

        def split_p(layer):
            dve.wait_ge(p_hi_ready, c.next("p"))
            dve.tensor_tensor(c_lo[:, 0:2], p_raw, c_hi[:, 0:2], SUB).then_inc(p_ready, 1)

        def modulated(x, at):
            for i in range(4):
                for j in range(4):
                    n = i * 4 + j
                    x1 = ln_c[:, j]
                    link(dve.tensor_scalar(x1, h[:, n], mod[:, bass.ds(i * 4 + (at + DT + j), 1)],
                                           mod[:, bass.ds(i * 4 + (at + j), 1)], MUL, ADD))
                    dve.wait_ge(x_hi, c.next("x"))
                    dve.tensor_tensor(x[1][:, n], x1, x[0][:, n], SUB).then_inc(x_lo, 1)
                    dve.wait_ge(x_lo, c.at("x"))
            dve.sem_inc(mod_x, 1)

        def s_conv(i, par, n):
            xb = s_xbp[:, n % 2]
            if n < 2:
                dst = s_bc[n]
                dve.wait_ge(cb_done, c.at("cb"))
                a, b = 2, 32 + 8 * n + par
            else:
                dst = s_xv[n % 2]
                a, b = 8, 4 * par + n - 2
            dve.wait_ge(tile_taken, c.at("tile"))
            w = lambda k: vec[:, bass.ds(i * a + (VEC["s_conv_w"] + 48 * k + b), 1)]
            link(dve.tensor_scalar(dst, xb[:, 0:SEQ], w(0), vec[:, bass.ds(i * a + (VEC["s_conv_b"] + b), 1)], MUL, ADD))
            for k in (1, 2):
                link(dve.scalar_tensor_tensor(dst, xb[:, k:k + SEQ], w(k), dst, MUL, ADD))
            link(dve.scalar_tensor_tensor(dst, xb[:, 3:3 + SEQ], w(3), dst, MUL, ADD))
            s_clamp(n, dst)

        def s_clamp(n, src):
            dve.wait_ge(gluon, c.at("glued", -1))
            c.next("glued")
            dve.tensor_scalar(s_zc[n % 2], src, SIG_MIN, None, MAX).then_inc(clamped, 1)

        def s_y_out(m):
            dve.wait_ge(yd_done, c.next("yd"))
            link(dve.tensor_tensor(s_y[:, m], bO[:, 0:SEQ], s_dx[:, m], ADD))
            dve.tensor_tensor(s_y[:, m], s_y[:, m], s_z[:, m], MUL).then_inc(s_y_ready, 1)

        def s_inputs(i, par, m):
            dve.wait_ge(gluon, c.next("gluon", 3 if m == 0 else 1))
            dve.wait_ge(s_y_ready, c.at("yd"))
            link(dve.tensor_scalar(s_dx[:, m], s_xv[m % 2], vec[:, bass.ds(i * 8 + (VEC["s_D"] + 4 * par + m), 1)], None, MUL))
            dve.wait_ge(turn_done, c.next("turn"))
            for b in range(2):
                for hh in range(2):
                    head = bass.ds(i * 16 + (8 * par + 2 * m + hh), 1)
                    last = dve.tensor_scalar(s_xdt[:, b, m, 64 * hh:64 * hh + 64], bT[:, b * P + 64 * hh:b * P + 64 * hh + 64],
                                             s_tok[:, b, head], None, MUL)
            last.then_inc(turn_read, 1)

        def s_segments(i, par, m):
            dve.wait_ge(rows_done, c.next("rows"))
            for hh in range(2):
                bank = (bR, bS[1])[hh]
                for b in range(2):
                    head = bass.ds(i * 16 + (8 * par + 2 * m + hh), 1)
                    last = dve.tensor_scalar(s_e[:, hh, SEQ * b:SEQ + P * b], bank[:, P * b:SEQ], s_tok[:, 2 + b, head],
                                             0.0, SUB, MIN)
            last.then_inc(rows_read, 1)

        def s_scale_y(i, par):
            factor()
            for m in range(4):
                last = dve.scalar_tensor_tensor(s_y[:, m], s_y[:, m], vec[:, bass.ds(i * 8 + (VEC["s_norm_g"] + 4 * par + m), 1)],
                                                rsn[:, 2], MUL, MUL)
            last.then_inc(y_ready, 1)
            dve.wait_ge(y_ready, c.next("y"))

        def s_y_lo(par):
            dve.wait_ge(x_hi, c.next("x"))
            four = slice(4 * par, 4 * par + 4)
            dve.tensor_tensor(q_lo[:, four], s_y, q_hi[:, four], SUB).then_inc(x_lo, 1)

        def s_group(i, par, prev):
            for n in range(10):
                j = n - 2
                if prev and n == 9:
                    s_y_lo(1 - par)
                begin()
                g = take()
                dve.tensor_copy(s_xbp[:, n % 2, 3:3 + SEQ] if n < 6 else s_z[:, n - 6], g).then_inc(tile_taken, 1)
                lo_half(1)
                if prev and 0 <= j <= 3:
                    s_segments(i, par - 1, j)
                if prev and 1 <= j <= 4:
                    s_y_out(j - 1)
                if 2 <= j <= 5:
                    s_inputs(i, par, j - 2)
                if n < 6:
                    s_conv(i, par, n)
                else:
                    dve.wait_ge(tile_taken, c.at("tile"))
                    s_clamp(n, s_z[:, n - 6])
                if n == 7:
                    dve.wait_ge(cb_done, c.next("cb"))
                    dve.tensor_tensor(s_cb[:, 0:P], bS[0][:, 0:P], K("causal"), MUL)
                    dve.tensor_copy(s_cb[:, P:SEQ], bS[0][:, P:SEQ])
                    dve.tensor_tensor(s_cb[:, SEQ:384], bS[0][:, SEQ:384], K("causal"), MUL).then_inc(cb_read, 1)
                if prev and n == 8:
                    s_scale_y(i, par - 1)
            c.next("gluon", 4)
            dve.wait_ge(gluon, c.at("gluon"))

        def project_tile(n, gate):
            g = take()
            dve.scalar_tensor_tensor(h[:, n], g, gate, h[:, n], MUL, ADD).then_inc(tile_taken, 1)

        def s_project():
            dve.wait_ge(scaled_h, 1)
            for s in range(8):
                c.next("slot")
                for e in range(2):
                    n = 2 * s + e
                    project_tile(n, mod[:, 32 + n:33 + n])
                    lo_half(e)

        def layer_norm(w):
            dve.wait_ge(ln_done, c.next("mean"))
            for n in range(DT):
                dve.tensor_tensor(h[:, n], h[:, n], bR[:, 0:SEQ], SUB).then_inc(ln_go, 1)
            c.next("ln_go", DT)
            factor()
            for i in range(4):
                def low(j):
                    n = i * 4 + j
                    x1 = ln_c[:, j]
                    link(dve.tensor_scalar(x1, h[:, n], mod[:, bass.ds(i * 4 + (64 + j), 1)],
                                           mod[:, bass.ds(i * 4 + (48 + j), 1)], MUL, ADD))
                    dve.wait_ge(x_hi, c.next("x"))
                    dve.tensor_tensor(q_lo[:, n], x1, q_hi[:, n], SUB).then_inc(x_lo, 1)
                    if j == 3:
                        dve.wait_ge(x_lo, c.at("x"))
                for j in range(4):
                    n = i * 4 + j
                    link(dve.scalar_tensor_tensor(h[:, n], h[:, n], vec[:, bass.ds(i * 4 + (VEC["ln_g"] + w * DT + j), 1)],
                                                  rstd[:], MUL, MUL))
                    dve.tensor_scalar(h[:, n], h[:, n], vec[:, bass.ds(i * 4 + (VEC["ln_b"] + w * DT + j), 1)],
                                      None, ADD).then_inc(ln_go, 1)
                    dve.wait_ge(ln_go, c.next("ln_go"))
                    if w == 0 and j:
                        low(j - 1)
                if w == 0:
                    low(3)

        def layer_s():
            c.k["turn"] = 2 * 3 * A_HEADS + 3 * B_PAIRS
            link(dve.tensor_scalar(mod[:, DT:3 * DT], mod[:, DT:3 * DT], 1.0, None, ADD))
            dve.tensor_scalar(mod[:, 4 * DT:6 * DT], mod[:, 4 * DT:6 * DT], 1.0, None, ADD).then_inc(mod_ready, 1)
            dve.wait_ge(mod_ready, 1)
            modulated((p_hi, p_lo), 0)
            link(dve.memset(s_xbp[:, :, 0:3], 0.0))
            begin()
            g = take()
            dve.tensor_scalar(s_dt[:], g, V("s_dt_bias"), None, ADD).then_inc(tile_taken, 1)
            lo_half(1)
            dve.wait_ge(tile_taken, c.at("tile"))
            c.next("soft")
            softplus(s_dt[:], s_y[:, 0], s_y[:, 1], s_y[:, 2], s_y[:, 3], s_dt[:])
            link(dve.tensor_scalar(s_y[:, 0], s_dt[:], tiny[:, 0:1], -1.0, MUL, MUL))
            link(dve.memset(s_y[:, 1], 1.0))
            dve.tensor_tensor_scan(s_ac[:], s_y[:, 1], s_y[:, 0], 0.0, MUL, ADD).then_inc(dt_ready, 1)
            dve.wait_ge(turn_done, c.next("turn"))
            dve.tensor_copy(s_tok.rearrange("p a b -> p (a b)"), bT[:]).then_inc(turn_read, 1)
            dve.wait_ge(turn_read, c.at("turn"))
            s_group(0, 0, False)
            s_group(0, 1, True)
            with c.loop(dve, "s_pairs", 1, S_PAIRS) as i:
                s_group(i, 0, True)
                s_project()
                s_group(i, 1, True)
            last = S_PAIRS
            s_segments(last, -1, 0)
            for m in range(4):
                s_y_out(m)
                if m < 3:
                    s_segments(last, -1, m + 1)
            s_scale_y(last, -1)
            s_y_lo(1)
            s_project()
            dve.wait_ge(tile_taken, c.at("tile"))
            layer_norm(0)

        def d_finish_scores(g, i, par):
            b = (bS[0], bS[1], bR)[g]
            dve.wait_ge(scored, c.next("scored"))
            dve.scalar_tensor_tensor(d_s[:, g], d_mat[:, g], con[:, bass.ds(i * 2 + (CON["slopes"] + 8 * g + par), 1)],
                                     b[:, 0:384], MUL, ADD).then_inc(score_read, 1)
            if g == 2:
                dve.wait_ge(score_read, c.at("scored"))
                dve.tensor_reduce(tiny[:, 4:5], d_s[:, :, 0:P], AX.XY, MAX, negate=True)
                link(dve.tensor_reduce(tiny[:, 5:6], d_s[:, :, P:384], AX.XY, MAX, negate=True))
                dve.tensor_scalar(tiny[:, 4:6], tiny[:, 4:6], P ** -0.5, None, MUL).then_inc(maxed, 1)

        def d_weigh():
            dve.wait_ge(exped, c.next("exped"))
            link(dve.reciprocal(tiny[:, 12:14], tiny[:, 8:10]))
            dve.tensor_scalar(d_s[:, :, 0:P], d_s[:, :, 0:P], tiny[:, 12:13], None, MUL)
            dve.tensor_scalar(d_s[:, :, P:384], d_s[:, :, P:384], tiny[:, 13:14], None, MUL).then_inc(weighted, 1)

        def d_finish():
            dve.wait_ge(gluon, c.next("gluon"))
            dve.wait_ge(mixed, c.next("mixed"))
            dve.tensor_tensor(rsn[:, 0], bO[:, 0:SEQ], d_gz[:], MUL).then_inc(y_ready, 1)
            dve.wait_ge(y_ready, c.next("y"))

        def d_y_lo(n):
            dve.wait_ge(x_hi, c.next("x"))
            dve.tensor_tensor(c_lo[:, n], rsn[:, 0], c_hi[:, n], SUB).then_inc(x_lo, 1)
            dve.wait_ge(x_lo, c.at("x"))

        def d_head(i, par, prev):
            dsts = [d_q[:, 0], d_q[:, 1], d_q[:, 2], d_k[:, 0], d_k[:, 1], d_k[:, 2],
                    d_v[:, 0], d_v[:, 1], d_v[:, 2], d_gz[:]]
            for n in range(10):
                begin()
                g = take()
                dve.tensor_copy(dsts[n], g).then_inc(tile_taken, 1)
                lo_half(1)
                if prev and n == 3:
                    d_finish()
                if prev and n == 4:
                    d_y_lo(i * 2 + (par - 1))
                if n in (4, 5, 6):
                    d_finish_scores(n - 4, i, par)
                if n == 7:
                    d_weigh()

        def layer_d():
            for i in range(4):
                for j in range(4):
                    n = i * 4 + j
                    dve.wait_ge(x_hi, c.next("x"))
                    dve.tensor_tensor(p_lo[:, n], h[:, n], p_hi[:, n], SUB).then_inc(x_lo, 1)
            dve.wait_ge(x_lo, c.at("x"))
            dve.sem_inc(mod_x, 1)
            dve.wait_ge(d_in, 16)
            d_head(0, 0, False)
            d_head(0, 1, True)
            with c.loop(dve, "d_pairs", 1, DIL_HEADS // 2) as i:
                d_head(i, 0, True)
                d_head(i, 1, True)
            d_finish()
            d_y_lo(DIL_HEADS - 1)
            dve.wait_ge(scaled_h, 2)
            with c.loop(dve, "d_out", 0, 2) as i:
                for s in range(4):
                    c.next("slot")
                    for e in range(2):
                        project_tile(i * 8 + (2 * s + e), mod[:, bass.ds(i * 8 + (80 + 2 * s + e), 1)])
                        lo_half(e)
            dve.wait_ge(tile_taken, c.at("tile"))
            layer_norm(1)

        dve.wait_ge(small_in, 48)
        ang, n_ = view(SEQ, SEQ), view(2 * SEQ, SEQ)
        link(dve.tensor_copy(ang, scratch[:, 0:SEQ].bitcast(I32)))
        c1 = 6.28125
        c2 = round((2 * math.pi - c1) * 2 ** 20) / 2 ** 20
        c3 = 2 * math.pi - c1 - c2
        big = 1.5 * 2 ** 23
        for dst, inv in ((sin_a, "inv_128"), (sin_b, "inv_64")):
            link(dve.tensor_scalar(dst[:], ang, K(inv), None, MUL))
            link(dve.tensor_scalar(n_, dst[:], 1 / (2 * math.pi), None, MUL))
            link(dve.tensor_scalar(n_, n_, big, None, ADD))
            link(dve.tensor_scalar(n_, n_, big, None, SUB))
            for cc in (c1, c2, c3):
                link(dve.scalar_tensor_tensor(dst[:], n_, -cc, dst[:], MUL, ADD))
            link(dve.tensor_scalar(dst[:], dst[:], -3.1415925, 3.1415925, MAX, MIN))
        for n, (a, b) in enumerate((("a_lq1", "a_lk1"), ("a_lq2", "a_lk2"))):
            last = dve.tensor_tensor(tiny[:, 2 * n:2 * n + 2], vec[:, VEC[a]:VEC[a] + 2], vec[:, VEC[b]:VEC[b] + 2], MUL)
        link(last)
        dve.sem_inc(trig_in, 1)
        dve.sem_inc(lam_in, 1)
        dve.wait_ge(trig_out, 2)
        for cos in (cos_a, cos_b):
            link(dve.tensor_tensor(cos[:], cos[:], cos[:], MUL))
            link(dve.tensor_scalar(cos[:], cos[:], -2.0, 1.0, MUL, ADD))
        b, cv = tiny[:, 48:64], vec[:, VEC["c_vec"]:VEC["c_vec"] + DT]
        dve.tensor_scalar(b, cv, SIG_MIN, None, MAX).then_inc(ada_in, 1)
        link(dve.memset(ada_hz[:, :, 1].bitcast(F32), 0.0))
        dve.wait_ge(ada_z, 1)
        dve.tensor_tensor(b, b, cv, MUL).then_inc(ada_in, 1)
        dve.wait_ge(ada_out, 1)
        link(dve.tensor_tensor(ada_hl[:, :, 1], b, ada_hl[:, :, 0], SUB))
        dve.wait_ge(lam_exp, 1)
        for n, layer in enumerate((0, 3)):
            init = 0.8 - 0.6 * math.exp(-0.3 * layer)
            link(dve.tensor_tensor(lam[:, n:n + 1], tiny[:, 6 + n:7 + n], tiny[:, 4 + n:5 + n], SUB))
            link(dve.tensor_scalar(lam[:, n:n + 1], lam[:, n:n + 1], init, None, SUB))
            link(dve.tensor_scalar(tiny[:, 16 + 2 * n:18 + 2 * n],
                                   vec[:, VEC["a_sub_norm"] + 2 * n:VEC["a_sub_norm"] + 2 * n + 2],
                                   1.0 - init, None, MUL))
        c.k["slot"] = 0
        for ahead in (1, 2):
            lo_half(0, ahead)
            lo_half(1, ahead)
        with c.loop(dve, "start", 0, 4) as i:
            for j in range(4):
                tail(i * 4 + j, (p_hi, p_lo), vec[:, bass.ds(i * 4 + (VEC["norm_gain"] + j), 1)])
        PQ = [(p_hi, p_lo), (q_hi, q_lo)]
        for layer in range(DEPTH):
            x, y = PQ[layer % 2], PQ[(layer + 1) % 2]
            if layer in (0, 3):
                layer_a(layer, x, y)
            elif layer == 1:
                layer_b(layer, x, y)
            else:
                layer_c(layer, x, y)
        layer_s()
        layer_d()
        dve.wait_ge(dve_step, c.at("dve"))
        dve.sem_inc(out_ready, 1)

    @block.gpsimd
    def _(pool):
        c = Steps(counts, "pool")

        def add_squares(j, n_first):
            pool.wait_ge(squared, c.next("sq"))
            if n_first:
                pool.wait_ge(norm_summed, c.at("model_norm"))
                pool.tensor_copy(acc[:], sq[:, j % 2]).then_inc(summed, 1)
            else:
                pool.wait_ge(summed, c.at("sq", -1))
                pool.tensor_tensor(acc[:], acc[:], sq[:, j % 2], ADD).then_inc(summed, 1)

        def sixteen_squares(norms_before):
            c.k["model_norm"] = norms_before
            add_squares(0, True)
            for j in range(1, 4):
                add_squares(j, False)
            with c.loop(pool, "squares", 1, 4):
                for j in range(4):
                    add_squares(j, False)

        def clamp(dst, src):
            pool.wait_ge(tile_taken, c.at("tile"))
            pool.sem_inc(pool_passed, 1)
            pool.tensor_scalar(dst, src, SIG_MIN, None, MAX).then_inc(clamped, 1)
            c.next("sig")

        def gates(last):
            for half in range(2):
                if half:
                    c.next("tile", 8)
                if last:
                    with c.loop(pool, "gates_last", 0, 2):
                        for j in range(4):
                            c.next("tile")
                            clamp(zg[:, j % 2], zg[:, j % 2])
                    continue
                for q in range(2):
                    for j in range(4):
                        c.next("tile")
                        clamp(zg[:, j % 2], zg[:, j % 2])
                        if j:
                            add_squares(j - 1, half == 0 and q == 0 and j == 1)
                    add_squares(3, False)

        def out_and_gates(layer):
            sixteen_squares(c.k["norm"])
            c.next("tile", DT)
            c.next("norm")
            c.k["model_norm"] = c.k["norm"]
            gates(layer == DEPTH - 1)

        def a_head(prev):
            for j in range(8):
                c.next("tile")
                if j in (2, 3, 4, 5):
                    n = j - 2
                    pool.wait_ge(scaled, c.next("scaled"))
                    pool.tensor_tensor(t2[:, n % 2], qn[:, n % 2], cos_a[:], MUL).then_inc(cos_done, 1)
                if j in (6, 7):
                    clamp(zc[:, j - 6], gz[:, j - 6])
                if j % 2 == 0 or j in (3, 7):
                    c.next("tile")
            c.next("turn", 3 if prev else 2)

        def layer_a(layer):
            c.next("norm")
            a_head(False)
            with c.loop(pool, "a_heads", 1, A_HEADS):
                a_head(True)
            c.next("norm", 5 * A_HEADS)
            pool.wait_ge(turn_read, c.at("turn"))
            c.next("turn")
            pool.dma_start(p_raw, t["p"][layer]).then_inc(p_in, 16)
            c.next("tile", 8)
            out_and_gates(layer)

        def cosine(src):
            pool.tensor_tensor(b_t2, src, cos_b[:], MUL).then_inc(cos_done, 1)

        def b_pair(prev):
            pool.wait_ge(scaled, c.next("scaled", 3))
            cosine(bq[:, 2])
            c.next("scaled", 2)
            for s in range(2):
                c.next("tile", 12 if s == 0 else 2)
                clamp(b_zc[:, s], b_gz[:, s])
            c.next("tile")
            c.next("turn", 3 if prev else 1)

        def layer_b(layer):
            c.next("norm")
            c.next("tile", 9)
            pool.wait_ge(scaled, c.next("scaled"))
            cosine(b_cs[:, 0])
            b_pair(False)
            with c.loop(pool, "b_pairs", 1, B_PAIRS):
                b_pair(True)
            c.next("norm", 3 + 3 * B_PAIRS)
            pool.wait_ge(turn_read, c.at("turn"))
            c.next("turn", 2)
            pool.dma_start(p_raw, t["p"][layer]).then_inc(p_in, 16)
            c.next("tile", 8)
            out_and_gates(layer)

        def layer_c(layer):
            c.next("norm")
            c.next("tile", DT - 4)
            for g in range(5):
                c.next("tile", 8 if 0 < g < 4 else 12 if g == 0 else 0)
                for j in range(4 if g else 0):
                    c.next("tile")
                    clamp(c_zc[:, j % 2], c_gz[:, j % 2])
            pool.wait_ge(gated, DT)
            pool.dma_start(p_raw, t["p"][layer]).then_inc(p_in, 16)
            c.next("tile", 8)
            out_and_gates(layer)

        def s_silu(n):
            buf = s_bc[n] if n < 2 else s_xv[n % 2] if n < 6 else s_z[:, n - 6]
            pool.wait_ge(sig_ready, c.next("sig"))
            pool.tensor_tensor(buf, buf, s_zc[n % 2], MUL).then_inc(gluon, 1)
            c.next("gluon")

        def s_mask_rows(i, par, m):
            pool.wait_ge(rows_done, c.at("rows"))
            pool.sem_inc(pool_passed, 1)
            pick = con[:, bass.ds(i * 16 + (CON["pick"] + 8 * par + 2 * m), 1)]
            pool.tensor_tensor(cos_b[:], s_ac[:], pick.to_broadcast([P, SEQ]), MUL).then_inc(masked, 1)
            c.next("rows")

        def s_weights():
            pool.wait_ge(decayed, c.next("decayed"))
            pool.wait_ge(cb_read, c.at("cb"))
            pool.tensor_tensor(s_e[:, 0], s_e[:, 0], s_cb, MUL)
            pool.tensor_tensor(s_e[:, 1], s_e[:, 1], s_cb, MUL).then_inc(m_ready, 1)

        def s_add_square(m):
            pool.wait_ge(s_sq, c.next("s_sq"))
            pool.wait_ge(s_sum, c.at("s_sq", -1))
            if m == 0:
                pool.wait_ge(norm_summed, c.at("norm"))
                pool.sem_inc(pool_passed, 1)
                pool.tensor_copy(acc[:], rsn[:, 0]).then_inc(s_sum, 1)
                c.next("norm")
            else:
                pool.tensor_tensor(acc[:], acc[:], rsn[:, m % 2], ADD).then_inc(s_sum, 1)

        def s_group(i, par, prev):
            if prev:
                s_mask_rows(i, par - 1, 0)
            for n in range(10):
                j = n - 2
                if prev and 0 <= j <= 3:
                    if j < 3:
                        s_mask_rows(i, par - 1, j + 1)
                    s_weights()
                if n:
                    s_silu(n - 1)
                if prev and 3 <= n <= 6:
                    s_add_square(n - 3)
            s_silu(9)
            c.next("cb")

        def layer_s():
            pool.wait_ge(mod_x, 1)
            pool.tensor_scalar(h[:], h[:], DEEPNORM_ALPHA, None, MUL).then_inc(scaled_h, 1)
            pool.wait_ge(dt_ready, 1)
            s_group(0, 0, False)
            s_group(0, 1, True)
            with c.loop(pool, "s_pairs", 1, S_PAIRS) as i:
                s_group(i, 0, True)
                s_group(i, 1, True)
            for m in range(4):
                if m == 0:
                    s_mask_rows(S_PAIRS, -1, 0)
                if m < 3:
                    s_mask_rows(S_PAIRS, -1, m + 1)
                s_weights()
                s_add_square(m)
            c.next("tile", 1 + 10 * S_GROUPS + DT * S_PAIRS)
            c.next("norm")

        def layer_d():
            pool.wait_ge(norm_summed, c.at("norm"))
            pool.dma_start(d_mat.rearrange("p a b -> p (a b)"), t["distance"]).then_inc(d_in, 16)
            pool.wait_ge(mod_x, 2)
            pool.tensor_scalar(h[:], h[:], DEEPNORM_ALPHA, None, MUL).then_inc(scaled_h, 1)

            def head():
                c.next("tile", 10)
                s_gate()

            def s_gate():
                pool.wait_ge(tile_taken, c.at("tile"))
                pool.wait_ge(gluon, c.at("gluon"))
                pool.sem_inc(pool_passed, 1)
                pool.tensor_scalar(d_zc[:], d_gz[:], SIG_MIN, None, MAX).then_inc(clamped, 1)
                c.next("gluon")
                pool.wait_ge(sig_ready, c.next("sig"))
                pool.tensor_tensor(d_gz[:], d_gz[:], d_zc[:], MUL).then_inc(gluon, 1)
            head()
            with c.loop(pool, "d_heads", 1, DIL_HEADS):
                head()

        sixteen_squares(0)
        for layer in range(DEPTH):
            if layer in (0, 3):
                layer_a(layer)
            elif layer == 1:
                layer_b(layer)
            else:
                layer_c(layer)
        layer_s()
        layer_d()


def _blocks(w):
    k, n = w.shape
    return w.reshape(k // P, P, n // P, P).transpose(2, 0, 1, 3)


def _slots(blocks):
    n = blocks.shape[0]
    return blocks.reshape(n // SLOT, SLOT, P, P).transpose(0, 2, 1, 3).reshape(n // SLOT, P, SLOT * P)


def _square_slots(w):
    b = _blocks(w)
    return _slots(b.reshape(-1, P, P))


def _ple_slots(w_out, w_gate, w_proj):
    proj = _slots(_blocks(w_proj).reshape(-1, P, P))
    gate = _square_slots(w_gate)
    return [proj[0:1], _square_slots(w_out), gate[0:8], proj[1:2], gate[8:16]]


def _layout(i):
    slots = []
    ada = i["ada_w_2"].reshape(2, 2, 8, P, 24, SEQ).transpose(0, 4, 1, 3, 2, 5).reshape(96, P, SLOT * P)
    for layer in range(DEPTH):
        j = layer // 3
        if layer in (0, 3):
            b = _blocks(i["a_w_in"][j]).reshape(4, A_HEADS, 2, DT, P, P).transpose(1, 0, 2, 3, 4, 5)
            main = _slots(b.reshape(-1, P, P))
            mods = ada[64 * j:64 * j + 32]
            slots.append(np.stack([main[0::2], mods, main[1::2]], 1).reshape(-1, P, SLOT * P))
            slots += _ple_slots(i["a_w_out"][j], i["ple_w_gate"][layer], i["ple_w_proj"][layer])
        if layer == 1:
            w = i["b_w_in"][0]
            slots.append(_square_slots(w[:, 0:1024]))
            slots.append(_square_slots(np.concatenate([w[:, 1024:1088], w[:, 1024:1088]], 1)))
            gate = _square_slots(w[:, 1088:])
            uq = i["b_w_uq"][0].reshape(512, 2 * B_PAIRS, 192)
            uq = [_blocks(np.concatenate([uq[:, 2 * n, :P], uq[:, 2 * n + 1, :P], uq[:, 2 * n, P:], uq[:, 2 * n + 1, P:]], 1))
                  for n in range(B_PAIRS)]
            ukv = _blocks(i["b_w_ukv"][0]).reshape(B_PAIRS, SLOT, P, P)
            for n in range(B_PAIRS):
                pad = np.zeros((4, P, P), np.float32)
                four = [_slots(np.concatenate([uq[n].reshape(12, P, P), pad])), _slots(ukv[n]),
                        gate[2 * n:2 * n + 1], gate[2 * n + 1:2 * n + 2]]
                for m in range(4):
                    slots += [ada[32 + 4 * n + m:33 + 4 * n + m], four[m]]
            slots += _ple_slots(i["b_w_out"][0], i["ple_w_gate"][layer], i["ple_w_proj"][layer])
        if layer == 2:
            w = i["c_w_in"][0]
            into = _square_slots(w[:, :D])
            gate = _square_slots(w[:, D:])
            slots.append(into[:12])
            groups = [_blocks(i[n][0, g]).reshape(4, P, P) for g in range(C_GROUPS) for n in ("c_w_a", "c_w_x")]
            groups = _slots(np.concatenate(groups))
            for g in range(5):
                slots += [groups[g:g + 1]] * (g < 4) + [gate[4 * g - 4:4 * g] if g else into[12:]]
            slots += _ple_slots(i["c_w_out"][0], i["ple_w_gate"][layer], i["ple_w_proj"][layer])
    w = _square_slots(i["a_in_w_2"][0][:, :10240])
    z, xs, b, cc = w[0:32], w[32:64], w[64:72], w[72:80]
    dt = i["a_in_w_2"][0][:, 10240:]
    slots.append(_square_slots(np.concatenate([dt, dt], 1)))
    out = _blocks(i["a_out_w_2"][0]).reshape(8, 2, S_PAIRS, 8, P, P).transpose(2, 0, 1, 3, 4, 5)
    out = _slots(out.reshape(-1, P, P)).reshape(S_PAIRS, 8, P, SLOT * P)
    for g in range(8):
        slots += [b[g:g + 1], cc[g:g + 1], xs[4 * g:4 * g + 4], z[4 * g:4 * g + 4]]
        if g and g % 2 == 0:
            slots.append(out[g // 2 - 1])
    slots.append(out[S_PAIRS - 1])
    w, kv = _square_slots(i["b_in_w_2"][0]), _square_slots(i["kv_w_2"])
    for n in range(DIL_HEADS):
        slots += [w[n:24:8], kv[n:24:8], kv[24 + n:48:8], w[24 + n:25 + n]]
    slots.append(_slots(_blocks(i["b_out_w_2"][0]).reshape(-1, P, P)))
    n = sum(len(s) for s in slots)
    slots.append(np.zeros((-(n + 2) % RAW + 2, P, SLOT * P), np.float32))
    return np.concatenate(slots)


def _cols(v, n):
    return np.ascontiguousarray(v.reshape(n, P).T)


def _vectors(i):
    two = lambda v: np.concatenate([v, v])
    f = {
        "norm_gain": _cols(i["norm_gain"], DEPTH * DT), "ple_norm": _cols(i["ple_norm"], DEPTH * DT),
        "a_q_norm": _cols(i["a_q_norm"], 2), "a_k_norm": _cols(i["a_k_norm"], 2),
        "a_lq1": _cols(i["a_lambda_q1"], 2), "a_lq2": _cols(i["a_lambda_q2"], 2),
        "a_lk1": _cols(i["a_lambda_k1"], 2), "a_lk2": _cols(i["a_lambda_k2"], 2),
        "a_sub_norm": _cols(i["a_sub_norm"], 4), "b_cq_norm": _cols(i["b_cq_norm"], 4),
        "b_ckv_norm": _cols(i["b_ckv_norm"], 4), "b_qn": _cols(i["b_q_nope_norm"], 1),
        "b_qr": _cols(two(i["b_q_rope_norm"][0]), 1), "b_kn": _cols(i["b_k_nope_norm"], 1),
        "b_kr": _cols(two(i["b_k_rope_norm"][0]), 1), "c_conv_w": _cols(i["c_conv_w"], 4 * DT),
        "c_conv_b": _cols(i["c_conv_b"], DT), "c_b_a": _cols(i["c_b_a"], DT), "c_b_x": _cols(i["c_b_x"], DT),
        "c_lambda": _cols(i["c_lambda"], DT), "c_vec": _cols(i["c_2"], DT), "ada_b": _cols(i["ada_b_2"], 96),
        "ln_g": _cols(i["ln_g_2"], 2 * DT), "ln_b": _cols(i["ln_b_2"], 2 * DT),
        "s_conv_w": _cols(i["a_conv_w_2"], 4 * 48), "s_conv_b": _cols(i["a_conv_b_2"], 48),
        "s_dt_bias": _cols(two(i["a_dt_bias_2"][0]), 1), "s_A_log": _cols(two(i["a_A_log_2"][0]), 1),
        "s_D": _cols(np.repeat(i["a_D_2"][0], 64), 32), "s_norm_g": _cols(i["a_norm_g_2"], 32),
    }
    return np.ascontiguousarray(np.concatenate([f[n] for n, _ in VEC_PARTS], 1))


def _constants():
    f = {"avg_model": np.full((P, P), 1 / D), "avg_512": np.full((P, P), 1 / 512),
         "avg_256": np.full((P, P), 1 / 256), "avg_128": np.full((P, P), 1 / 128),
         "avg_64": np.kron(np.eye(2), np.full((64, 64), 1 / 64)), "ones": np.ones((P, P)), "ident": np.eye(P)}

    def swap(half):
        m = np.zeros((P, P))
        for o in range(P):
            base, r = o // (2 * half) * 2 * half, o % (2 * half)
            m[base + (r + half) % (2 * half), o] = -1.0 if r < half else 1.0
        return m
    f["swap_128"], f["swap_64"] = swap(64), swap(32)
    q, k = np.arange(P)[:, None] // 64, np.arange(P)[None] // 64
    diag = np.where(k <= q, 0.0, NEG)
    f["mask"] = np.concatenate([diag, np.zeros((P, P)), diag], 1)
    inv = lambda half: (10000.0 ** (-(np.arange(P) % half) / half))[:, None]
    f["inv_128"], f["inv_64"] = inv(64), inv(32)
    f["eps_6"], f["eps_5"] = np.full((P, 1), 1e-6), np.full((P, 1), 1e-5)
    f["slopes"] = np.tile((2.0 ** (-8.0 * np.arange(1, 25) / 24))[None], (P, 1))
    f["pick"] = np.concatenate([np.eye(64), np.eye(64, k=-1)])
    f["causal"] = np.triu(np.ones((P, P)))
    return np.ascontiguousarray(np.concatenate([f[n] for n, _ in CONST_PARTS], 1).astype(np.float32))


def _distance():
    d = np.arange(SEQ)[:, None] - np.arange(SEQ)[None]
    out = []
    for window, dilation in ((128, 1), (512, 4), (2048, 16)):
        ok = (d >= 0) & (d <= window) & (d % dilation == 0)
        m = np.where(ok, -d * P ** 0.5, NEG)
        out.append(np.concatenate([m[:P, :P], m[P:]], 1))
    return np.ascontiguousarray(np.concatenate(out, 1).astype(np.float32))


def _features_first(a):
    s, d = a.shape
    return np.ascontiguousarray(a.T.reshape(d // P, P, s).transpose(1, 0, 2))


COUNTS = {
    ('sp', 'slots'): {'slot': 4},
    ('pe', 'a_heads'): {'slot': 12, 'tile': 14, 'norm': 5, 'sq_head': 4, 'scaled': 4, 'rot': 4, 'turn': 3, 'roped': 4, 'score_read': 2, 'weighted': 1, 'mixed': 1, 'mixed_read': 1},
    ('pe', 'outs'): {'slot': 4, 'tile': 4},
    ('pe', 'gates'): {'tile': 4, 'slot': 4},
    ('pe', 'b_pairs'): {'norm': 3, 'tile': 15, 'turn': 3, 'score_read': 2, 'slot': 8, 'roped': 1, 'mixed': 1, 'sq_head': 5, 'weighted': 1, 'rot': 1, 'scaled': 5},
    ('pe', 'c_in'): {'tile': 4, 'slot': 4},
    ('pe', 's_pairs'): {'norm': 2, 'tile': 36, 'turn': 8, 'slot': 28, 'x': 2, 'gluon': 20, 'cb': 2, 'rows': 8, 'yd': 8, 's_sum': 8},
    ('pe', 'd_pairs'): {'slot': 20, 'mixed': 2, 'turn': 12, 'tile': 20, 'score_read': 6, 'weighted': 2},
    ('pe', 'd_out'): {'slot': 4, 'tile': 8},
    ('act', 'start'): {'sum': 4},
    ('act', 'a_heads'): {'slot': 12, 'act': 9, 'norm': 5, 'half': 12, 'tile': 14, 'turn': 3, 'clamped': 2, 'sig': 2, 'maxed': 1, 'mixed': 1, 'y': 1},
    ('act', 'outs'): {'slot': 4, 'sum': 4, 'tile': 4, 'half': 4},
    ('act', 'gates'): {'tile': 4, 'clamped': 4, 'slot': 4, 'sum': 4, 'half': 4, 'act': 8, 'sig': 4, 'res': 4},
    ('act', 'b_pairs'): {'maxed': 1, 'slot': 8, 'act': 7, 'sig': 2, 'norm': 3, 'turn': 3, 'tile': 15, 'clamped': 2, 'half': 6, 'y': 1},
    ('act', 'c_in'): {'slot': 4, 'tile': 4, 'half': 4},
    ('act', 'gates_last'): {'slot': 4, 'act': 8, 'sig': 4, 'tile': 4, 'clamped': 4, 'half': 4, 'res': 4},
    ('act', 's_pairs'): {'slot': 28, 'act': 42, 'sig': 20, 'norm': 2, 'tile': 36, 'clamped': 20, 'half': 20, 'y': 2, 'rows': 8, 's_y': 8},
    ('act', 'd_pairs'): {'maxed': 2, 'slot': 20, 'act': 4, 'sig': 2, 'turn': 12, 'tile': 20, 'clamped': 2, 'half': 20, 'y': 2},
    ('act', 'd_out'): {'slot': 4, 'tile': 8},
    ('dve', 'start'): {'x': 4},
    ('dve', 'a_heads'): {'dve': 6, 'slot': 12, 'x': 1, 'tile': 14, 'norm': 5, 'scaled': 4, 'rot': 4, 'sig': 2, 'scored': 2, 'exped': 1, 'y': 1},
    ('dve', 'outs'): {'slot': 4, 'x': 4, 'tile': 4},
    ('dve', 'gates'): {'tile': 4, 'slot': 4, 'dve': 4, 'x': 4, 'sig': 4, 'res': 4},
    ('dve', 'b_pairs'): {'slot': 8, 'mixed': 1, 'x': 1, 'sig': 2, 'norm': 3, 'tile': 15, 'rot': 1, 'dve': 2, 'exped': 1, 'scored': 2, 'y': 1, 'scaled': 5},
    ('dve', 'c_in'): {'slot': 4, 'tile': 4, 'dve': 12},
    ('dve', 'gates_last'): {'slot': 4, 'sig': 4, 'tile': 4, 'dve': 4, 'res': 4},
    ('dve', 's_pairs'): {'slot': 28, 'x': 2, 'norm': 2, 'tile': 36, 'dve': 64, 'y': 2, 'turn': 8, 'glued': 20, 'gluon': 20, 'cb': 2, 'rows': 8, 'yd': 8},
    ('dve', 'd_pairs'): {'slot': 20, 'mixed': 2, 'x': 2, 'gluon': 2, 'y': 2, 'tile': 20, 'dve': 4, 'exped': 2, 'scored': 6},
    ('dve', 'd_out'): {'slot': 4, 'tile': 8},
    ('pool', 'squares'): {'sq': 4},
    ('pool', 'a_heads'): {'tile': 14, 'scaled': 4, 'sig': 2, 'turn': 3},
    ('pool', 'b_pairs'): {'tile': 15, 'turn': 3, 'sig': 2, 'scaled': 5},
    ('pool', 'gates_last'): {'tile': 4, 'sig': 4},
    ('pool', 's_pairs'): {'sig': 20, 'norm': 2, 'gluon': 20, 'cb': 2, 'rows': 8, 'decayed': 8, 's_sq': 8},
    ('pool', 'd_heads'): {'gluon': 1, 'sig': 1, 'tile': 10},
}


def kernel(**inputs):
    import concourse.bacc as _bacc
    from concourse.bass_utils import run_bass_kernel_spmd as _run
    i = {k: np.asarray(v) for k, v in inputs.items()}
    arrays = {
        "slots": _layout(i), "vecs": _vectors(i), "consts": _constants(),
        "positions": np.ascontiguousarray(i["positions"].reshape(1, SEQ).astype(np.int32)),
        "x": _features_first(i["x"][0]),
        "p": np.stack([_features_first(i["p"][n, 0]) for n in range(DEPTH)]),
        "distance": _distance(),
    }
    nc = _bacc.Bacc("TRN2", target_bir_lowering=False, num_devices=1)
    t = {n: nc.dram_tensor(f"in_{n}", a.shape, mybir.dt.from_np(a.dtype), kind="ExternalInput").ap()
         for n, a in arrays.items()}
    t["out"] = nc.dram_tensor("out_h", (P, DT, SEQ), F32, kind="ExternalOutput").ap()
    program(nc, t, COUNTS)
    r = _run(nc, [{f"in_{n}": a for n, a in arrays.items()}], core_ids=[0])
    o = r.results[0]["out_h"]
    return np.ascontiguousarray(o.transpose(2, 1, 0).reshape(1, SEQ, D))
```
